# Optimizing a Trainium2 kernel written in Bass

```python
import math
import jax, jax.numpy as jnp
from jax import lax
import numpy as np

D_MODEL = 1024
BATCH = 1
SEQ = 512
DEPTH = 1

ATT_PATTERNS = ((128, 1), (512, 4), (2048, 16))
ATT_GROUPS = len(ATT_PATTERNS)
ATT_HEADS = 8
ATT_HEAD_DIM = 64
ATT_WIDTH = ATT_HEADS * ATT_HEAD_DIM
ATT_BLOCK = 128
RWKV_WIDTH = D_MODEL
RWKV_HEAD_DIM = 64
RWKV_HEADS = RWKV_WIDTH // RWKV_HEAD_DIM
DECAY_LORA = 64
AAA_LORA = 64
GATE_LORA = 160
D_FF = 2816
CONV_WIDTH = 3
N_BRANCHES = 2
ATT_IN = ATT_GROUPS * 3 * ATT_WIDTH
RWKV_IN = 3 * RWKV_WIDTH + DECAY_LORA + AAA_LORA + GATE_LORA
GATE_IN = N_BRANCHES * D_MODEL
N_IN = ATT_IN + RWKV_IN + GATE_IN
RMS_EPS = 1e-6
GN_EPS = 64e-5


def rms_norm(x, w):
    xf = x.astype(jnp.float32)
    y = xf * lax.rsqrt(jnp.mean(xf * xf, axis=-1, keepdims=True) + RMS_EPS)
    return (y * w).astype(x.dtype)

def dilated_window_attention(q, k, v, window, dilation):
    b, s, h, e = q.shape
    back = window // dilation
    sub_len = -(-s // dilation)
    n_blk = -(-sub_len // ATT_BLOCK)
    s_pad = n_blk * ATT_BLOCK * dilation

    def to_blocks(t):
        t = jnp.pad(t, ((0, 0), (0, s_pad - s), (0, 0), (0, 0)))
        return t.reshape(b, n_blk, ATT_BLOCK, dilation, h, e)

    def with_prev(t):
        prev = jnp.concatenate([jnp.zeros_like(t[:, :1]), t[:, :-1]], axis=1)
        return jnp.concatenate([prev, t], axis=2)

    qb = to_blocks(q)
    kc = with_prev(to_blocks(k))
    vc = with_prev(to_blocks(v))
    scores = jnp.einsum('bnqrhe,bnkrhe->bnrhqk', qb, kc).astype(jnp.float32) * (e ** -0.5)
    qi = jnp.arange(ATT_BLOCK)[:, None]
    kj = jnp.arange(2 * ATT_BLOCK)[None, :]
    dist = qi + ATT_BLOCK - kj
    kpos = jnp.arange(n_blk)[:, None] * ATT_BLOCK + kj - ATT_BLOCK
    valid = ((dist >= 0) & (dist <= back))[None] & (kpos >= 0)[:, None, :]
    scores = jnp.where(valid[None, :, None, None], scores, -jnp.inf)
    m = jnp.max(scores, axis=-1, keepdims=True)
    p = jnp.exp(scores - m)
    den = jnp.sum(p, axis=-1)
    num = jnp.einsum('bnrhqk,bnkrhe->bnqrhe', p, vc.astype(jnp.float32))
    den_q = jnp.transpose(den, (0, 1, 4, 2, 3))
    out = (num / den_q[..., None]).reshape(b, s_pad, h, e)[:, :s]
    lse = (jnp.transpose(m[..., 0], (0, 1, 4, 2, 3)) + jnp.log(den_q)).reshape(b, s_pad, h)[:, :s]
    return out, lse

def attention_mixer(z):
    b, s, _ = z.shape
    qkv = z.reshape(b, s, ATT_GROUPS, 3, ATT_HEADS, ATT_HEAD_DIM)
    outs, lses = [], []
    for g, (window, dilation) in enumerate(ATT_PATTERNS):
        o, l = dilated_window_attention(qkv[:, :, g, 0], qkv[:, :, g, 1], qkv[:, :, g, 2], window, dilation)
        outs.append(o)
        lses.append(l)
    wts = jax.nn.softmax(jnp.stack(lses), axis=0)
    out = jnp.sum(wts[..., None] * jnp.stack(outs), axis=0)
    return out.reshape(b, s, ATT_WIDTH).astype(z.dtype)

def rwkv7_mixer(z, mu, w0, w2, a0, a2, g2, k_k, k_a, r_k, lnx_w, lnx_b):
    f32 = jnp.float32
    b, s, _ = z.shape
    z_prev = jnp.pad(z, ((0, 0), (1, 0), (0, 0)))[:, :s]
    z = z + (z_prev - z) * mu
    c = RWKV_WIDTH
    r, k, v, w_low, a_low, g_low = jnp.split(
        z, [c, 2 * c, 3 * c, 3 * c + DECAY_LORA, 3 * c + DECAY_LORA + AAA_LORA], axis=-1)
    w_log = -jax.nn.softplus(-(w0 + jnp.tanh(w_low) @ w2).astype(f32)) - 0.5
    decay = jnp.exp(-jnp.exp(w_log))
    a = jax.nn.sigmoid((a0 + a_low @ a2).astype(f32))
    g = jax.nn.sigmoid(g_low) @ g2
    k_mod = k.astype(f32) * (1.0 + (a - 1.0) * k_a)

    def heads(t):
        return t.astype(f32).reshape(b, s, RWKV_HEADS, RWKV_HEAD_DIM)

    kk = heads(k * k_k)
    kk = kk / jnp.maximum(jnp.sqrt(jnp.sum(kk * kk, axis=-1, keepdims=True)), 1e-12)
    r_h, k_h, v_h, w_h, a_h = heads(r), heads(k_mod), heads(v), heads(decay), heads(a)

    def step(state, inp):
        r_t, w_t, k_t, v_t, aa_t, bb_t = inp
        sa = jnp.einsum('bhvk,bhk->bhv', state, aa_t)
        state = state * w_t[:, :, None, :] + sa[..., None] * bb_t[:, :, None, :] + v_t[..., None] * k_t[:, :, None, :]
        return state, jnp.einsum('bhvk,bhk->bhv', state, r_t)

    tm = lambda t: jnp.swapaxes(t, 0, 1)
    state0 = jnp.zeros((b, RWKV_HEADS, RWKV_HEAD_DIM, RWKV_HEAD_DIM), f32)
    _, y = lax.scan(step, state0, (tm(r_h), tm(w_h), tm(k_h), tm(v_h), tm(-kk), tm(kk * a_h)))
    y = tm(y)
    mean = jnp.mean(y, axis=-1, keepdims=True)
    var = jnp.mean(jnp.square(y - mean), axis=-1, keepdims=True)
    y = ((y - mean) * lax.rsqrt(var + GN_EPS)).reshape(b, s, c) * lnx_w + lnx_b
    bonus = (jnp.sum(r_h * k_h * r_k, axis=-1, keepdims=True) * v_h).reshape(b, s, c)
    return ((y + bonus) * g).astype(z.dtype)

def conv_ffn(h, w_up, conv_w, conv_b, w_down):
    s = h.shape[1]
    u = h @ w_up
    up = jnp.pad(u, ((0, 0), (CONV_WIDTH - 1, 0), (0, 0)))
    u = conv_b + sum(conv_w[j] * up[:, j:j + s] for j in range(CONV_WIDTH))
    gate, val = jnp.split(u, 2, axis=-1)
    return (jax.nn.silu(gate) * val) @ w_down

def first_inputs(seed: int = 0) -> dict:
    key = jax.random.key(seed)
    ks = iter(jax.random.split(key, 32))
    f32 = jnp.float32
    L, D, C = DEPTH, D_MODEL, RWKV_WIDTH

    def nrm(shape, scale):
        return jax.random.normal(next(ks), shape, f32) * scale

    ramp = (jnp.arange(C, dtype=f32) / (C - 1)) ** 0.85
    inputs = {}
    inputs['x'] = nrm((BATCH, SEQ, D), 1.0)
    inputs['c'] = nrm((BATCH, D), 1.0)
    inputs['w_ada'] = nrm((L, D, 6 * D), 0.3 * D ** -0.5)
    inputs['b_ada'] = nrm((L, 6 * D), 0.02)
    inputs['norm1_w'] = 1.0 + nrm((L, D), 0.05)
    inputs['w_in'] = nrm((L, D, N_IN), D ** -0.5)
    inputs['b_gate'] = nrm((L, GATE_IN), 0.1)
    inputs['mu_shift'] = jax.random.uniform(next(ks), (L, RWKV_IN), f32)
    inputs['w0'] = -6.5 + 5.0 * ramp + nrm((L, C), 0.1)
    inputs['w2'] = nrm((L, DECAY_LORA, C), 0.1 * DECAY_LORA ** -0.5)
    inputs['a0'] = nrm((L, C), 0.1)
    inputs['a2'] = nrm((L, AAA_LORA, C), AAA_LORA ** -0.5)
    inputs['g2'] = nrm((L, GATE_LORA, C), GATE_LORA ** -0.5)
    inputs['k_k'] = 0.85 + nrm((L, C), 0.05)
    inputs['k_a'] = 1.0 + nrm((L, C), 0.05)
    inputs['r_k'] = nrm((L, RWKV_HEADS, RWKV_HEAD_DIM), 0.1)
    inputs['lnx_w'] = 1.0 + nrm((L, C), 0.05)
    inputs['lnx_b'] = nrm((L, C), 0.02)
    inputs['w_att_out'] = nrm((L, ATT_WIDTH, D), ATT_WIDTH ** -0.5)
    inputs['w_rwkv_out'] = nrm((L, C, D), C ** -0.5)
    inputs['w_o'] = nrm((L, D, D), D ** -0.5)
    inputs['norm2_w'] = 1.0 + nrm((L, D), 0.05)
    inputs['w_up'] = nrm((L, D, 2 * D_FF), D ** -0.5)
    inputs['conv_w'] = nrm((L, CONV_WIDTH, 2 * D_FF), CONV_WIDTH ** -0.5)
    inputs['conv_b'] = nrm((L, 2 * D_FF), 0.02)
    inputs['w_down'] = nrm((L, D_FF, D), D_FF ** -0.5)
    inputs['norm_f_w'] = 1.0 + nrm((D,), 0.05)
    return inputs

def first_block(x, c, w_ada, b_ada, norm1_w, w_in, b_gate, mu_shift, w0, w2, a0, a2, g2, k_k, k_a, r_k,
              lnx_w, lnx_b, w_att_out, w_rwkv_out, w_o, norm2_w, w_up, conv_w, conv_b, w_down, norm_f_w):
    for l in range(DEPTH):
        ada = (c @ w_ada[l] + b_ada[l])[:, None, :]
        sh1, sc1, gt1, sh2, sc2, gt2 = jnp.split(ada, 6, axis=-1)
        h = rms_norm(x, norm1_w[l]) * (1.0 + sc1) + sh1
        proj = h @ w_in[l]
        att_in, rwkv_in, gate_in = jnp.split(proj, [ATT_IN, ATT_IN + RWKV_IN], axis=-1)
        y_att = attention_mixer(att_in) @ w_att_out[l]
        y_rwkv = rwkv7_mixer(rwkv_in, mu_shift[l], w0[l], w2[l], a0[l], a2[l], g2[l], k_k[l], k_a[l],
                             r_k[l], lnx_w[l], lnx_b[l]) @ w_rwkv_out[l]
        g_att, g_rwkv = jnp.split(jax.nn.sigmoid(gate_in + b_gate[l]), N_BRANCHES, axis=-1)
        x = x + gt1 * ((g_att * y_att + g_rwkv * y_rwkv) @ w_o[l])
        h = rms_norm(x, norm2_w[l]) * (1.0 + sc2) + sh2
        x = x + gt2 * conv_ffn(h, w_up[l], conv_w[l], conv_b[l], w_down[l])
    return rms_norm(x, norm_f_w)


CHUNK = 64
Q_BLOCK = 128
MLA_HEADS = 8
MLA_NOPE = 64
MLA_ROPE = 32
MLA_QK = MLA_NOPE + MLA_ROPE
MLA_V = 64
Q_LORA = 256
KV_LORA = 128
ROPE_BASE = 10000.0
CA_HEADS = 8
CA_HEAD_DIM = 64
LEFT_CHUNKS = 8
BAND = (LEFT_CHUNKS + 1) * CHUNK
MAX_REL = 256
MLA_WIDTH = MLA_HEADS * MLA_V
CA_WIDTH = CA_HEADS * CA_HEAD_DIM
IN_WIDTHS = (Q_LORA, KV_LORA, MLA_ROPE, CA_WIDTH, CA_WIDTH, CA_WIDTH, D_MODEL, D_MODEL)
IN_WIDTH = Q_LORA + KV_LORA + MLA_ROPE + 3 * CA_WIDTH + 2 * D_MODEL
N_GROUPS = 4
EXPERTS_PER_GROUP = 8
N_EXPERTS = N_GROUPS * EXPERTS_PER_GROUP
TOP_K = 2
EXPERT_FF = 256
NORM_EPS = 1e-6
NEG_INF = -1e30
N_MOD = 6


def rms_norm_2(x, g):
    xf = x.astype(jnp.float32)
    y = xf * lax.rsqrt(jnp.mean(xf * xf, axis=-1, keepdims=True) + NORM_EPS)
    return (y * g.astype(jnp.float32)).astype(x.dtype)

def modulate(x, shift, scale):
    return x * (1 + scale[:, None, :]) + shift[:, None, :]

def rope(x, positions):
    half = x.shape[-1] // 2
    inv = ROPE_BASE ** (-jnp.arange(half, dtype=jnp.float32) / half)
    ang = positions.astype(jnp.float32)[..., None] * inv
    ang = ang.reshape(ang.shape[:2] + (1,) * (x.ndim - 3) + (half,))
    cos = jnp.cos(ang).astype(x.dtype)
    sin = jnp.sin(ang).astype(x.dtype)
    x1, x2 = x[..., :half], x[..., half:]
    return jnp.concatenate([x1 * cos - x2 * sin, x2 * cos + x1 * sin], axis=-1)

def mla_attend(q, k, v):
    b, s, h, _ = q.shape
    n_blocks = s // Q_BLOCK
    scale = MLA_QK ** -0.5
    key_chunk = jnp.arange(s) // CHUNK

    def one_block(i):
        qb = lax.dynamic_slice_in_dim(q, i * Q_BLOCK, Q_BLOCK, axis=1)
        sc = jnp.einsum('bqhd,bkhd->bhqk', qb, k).astype(jnp.float32) * scale
        q_chunk = (i * Q_BLOCK + jnp.arange(Q_BLOCK)) // CHUNK
        mask = key_chunk[None, :] <= q_chunk[:, None]
        sc = jnp.where(mask[None, None], sc, NEG_INF)
        p = jax.nn.softmax(sc, axis=-1).astype(v.dtype)
        return jnp.einsum('bhqk,bkhd->bqhd', p, v)

    out = lax.map(one_block, jnp.arange(n_blocks))
    return out.transpose(1, 0, 2, 3, 4).reshape(b, s, h * v.shape[-1])

def chunk_band_attend(q, k, v, rel_table):
    b, s, h, d = q.shape
    n_chunks = s // CHUNK
    scale = d ** -0.5
    pad = ((0, 0), (LEFT_CHUNKS * CHUNK, 0), (0, 0), (0, 0))
    kp = jnp.pad(k, pad)
    vp = jnp.pad(v, pad)
    rel = (jnp.arange(CHUNK)[:, None] + LEFT_CHUNKS * CHUNK) - jnp.arange(BAND)[None, :]
    idx = jnp.clip(rel, -MAX_REL, MAX_REL) + MAX_REL
    bias = rel_table.astype(jnp.float32)[:, idx]

    def one_chunk(n):
        qc = lax.dynamic_slice_in_dim(q, n * CHUNK, CHUNK, axis=1)
        kb = lax.dynamic_slice_in_dim(kp, n * CHUNK, BAND, axis=1)
        vb = lax.dynamic_slice_in_dim(vp, n * CHUNK, BAND, axis=1)
        sc = jnp.einsum('bqhd,bkhd->bhqk', qc, kb).astype(jnp.float32) * scale + bias[None]
        valid = (n * CHUNK - LEFT_CHUNKS * CHUNK + jnp.arange(BAND)) >= 0
        sc = jnp.where(valid[None, None, None, :], sc, NEG_INF)
        p = jax.nn.softmax(sc, axis=-1).astype(vb.dtype)
        return jnp.einsum('bhqk,bkhd->bqhd', p, vb)

    out = lax.map(one_chunk, jnp.arange(n_chunks))
    return out.transpose(1, 0, 2, 3, 4).reshape(b, s, h * d)

def hybrid_mixer(h, positions, w_in, g_q, w_uq, g_kv, w_uk, w_uv, rel_table, w_oa, w_ob, w_out):
    b, s, _ = h.shape
    proj = h @ w_in
    cuts = [int(v) for v in np.cumsum(IN_WIDTHS)[:-1]]
    q_lat, kv_lat, k_rope, q_b, k_b, v_b, gate_a, gate_b = jnp.split(proj, cuts, axis=-1)
    q_a = (rms_norm_2(q_lat, g_q) @ w_uq).reshape(b, s, MLA_HEADS, MLA_QK)
    q_a = jnp.concatenate([q_a[..., :MLA_NOPE], rope(q_a[..., MLA_NOPE:], positions)], axis=-1)
    kv_n = rms_norm_2(kv_lat, g_kv)
    k_nope = (kv_n @ w_uk).reshape(b, s, MLA_HEADS, MLA_NOPE)
    v_a = (kv_n @ w_uv).reshape(b, s, MLA_HEADS, MLA_V)
    k_r = rope(k_rope, positions)
    k_a = jnp.concatenate(
        [k_nope, jnp.broadcast_to(k_r[:, :, None, :], (b, s, MLA_HEADS, MLA_ROPE))], axis=-1)
    o_a = mla_attend(q_a, k_a, v_a)
    o_b = chunk_band_attend(
        q_b.reshape(b, s, CA_HEADS, CA_HEAD_DIM),
        k_b.reshape(b, s, CA_HEADS, CA_HEAD_DIM),
        v_b.reshape(b, s, CA_HEADS, CA_HEAD_DIM), rel_table)
    merged = jax.nn.sigmoid(gate_a) * (o_a @ w_oa) + jax.nn.sigmoid(gate_b) * (o_b @ w_ob)
    return merged @ w_out

def hierarchical_moe(h, w_rg, b_rg, w_re, b_re, w_gate, w_up, w_down):
    b, s, d = h.shape
    t = h.reshape(b * s, d)
    n_tok = t.shape[0]
    g_prob = jax.nn.softmax((t @ w_rg + b_rg).astype(jnp.float32), axis=-1)
    g_w, g_idx = lax.top_k(g_prob, 1)
    g_w, g_idx = g_w[:, 0], g_idx[:, 0]
    e_logits = (t @ w_re + b_re).astype(jnp.float32).reshape(n_tok, N_GROUPS, EXPERTS_PER_GROUP)
    e_sel = jnp.take_along_axis(e_logits, g_idx[:, None, None], axis=1)[:, 0]
    e_prob = jax.nn.softmax(e_sel, axis=-1)
    top_w, top_i = lax.top_k(e_prob, TOP_K)
    top_w = top_w / jnp.sum(top_w, axis=-1, keepdims=True)
    in_group = jnp.sum(jax.nn.one_hot(top_i, EXPERTS_PER_GROUP, dtype=jnp.float32) * top_w[..., None], axis=1)
    combine = (jax.nn.one_hot(g_idx, N_GROUPS, dtype=jnp.float32)[:, :, None]
               * in_group[:, None, :] * g_w[:, None, None]).astype(h.dtype)
    y = jnp.zeros_like(t)
    for g in range(N_GROUPS):
        sl = slice(g * EXPERTS_PER_GROUP, (g + 1) * EXPERTS_PER_GROUP)
        a = jnp.einsum('td,edf->tef', t, w_gate[sl])
        u = jnp.einsum('td,edf->tef', t, w_up[sl])
        hid = jax.nn.silu(a) * u * combine[:, g, :, None]
        y = y + jnp.einsum('tef,efd->td', hid, w_down[sl])
    return y.reshape(b, s, d)

def second_inputs(seed: int = 0) -> dict:
    key = jax.random.key(seed)
    ks = iter(jax.random.split(key, 32))
    L, D = DEPTH, D_MODEL

    def w(shape, fan_in):
        return jax.random.normal(next(ks), shape, jnp.float32) * (fan_in ** -0.5)

    def gain(shape):
        return 1.0 + 0.02 * jax.random.normal(next(ks), shape, jnp.float32)

    def small(shape, s=0.01):
        return s * jax.random.normal(next(ks), shape, jnp.float32)

    x = jax.random.normal(next(ks), (BATCH, SEQ, D), jnp.float32)
    c = jax.random.normal(next(ks), (BATCH, D), jnp.float32)
    offsets = jax.random.randint(next(ks), (BATCH, 1), 0, 10000, dtype=jnp.int32)
    positions = offsets + jnp.arange(SEQ, dtype=jnp.int32)[None, :]
    return {
        'x': x,
        'c': c,
        'positions': positions,
        'w_ada': w((L, D, N_MOD * D), D),
        'b_ada': small((L, N_MOD * D), 0.02),
        'g_mix': gain((L, D)),
        'w_in': w((L, D, IN_WIDTH), D),
        'g_q': gain((L, Q_LORA)),
        'w_uq': w((L, Q_LORA, MLA_HEADS * MLA_QK), Q_LORA),
        'g_kv': gain((L, KV_LORA)),
        'w_uk': w((L, KV_LORA, MLA_HEADS * MLA_NOPE), KV_LORA),
        'w_uv': w((L, KV_LORA, MLA_WIDTH), KV_LORA),
        'rel_bias': small((L, CA_HEADS, 2 * MAX_REL + 1), 0.5),
        'w_oa': w((L, MLA_WIDTH, D), MLA_WIDTH),
        'w_ob': w((L, CA_WIDTH, D), CA_WIDTH),
        'w_out': w((L, D, D), D),
        'g_ffn': gain((L, D)),
        'w_rg': w((L, D, N_GROUPS), D),
        'b_rg': small((L, N_GROUPS)),
        'w_re': w((L, D, N_EXPERTS), D),
        'b_re': small((L, N_EXPERTS)),
        'w_gate': w((L, N_EXPERTS, D, EXPERT_FF), D),
        'w_up': w((L, N_EXPERTS, D, EXPERT_FF), D),
        'w_down': w((L, N_EXPERTS, EXPERT_FF, D), EXPERT_FF),
        'g_final': gain((D,)),
    }

def second_block(x, c, positions, w_ada, b_ada, g_mix, w_in, g_q, w_uq, g_kv, w_uk, w_uv,
              rel_bias, w_oa, w_ob, w_out, g_ffn, w_rg, b_rg, w_re, b_re,
              w_gate, w_up, w_down, g_final):
    c_act = jax.nn.silu(c)
    for l in range(DEPTH):
        mod = c_act @ w_ada[l] + b_ada[l]
        sh1, sc1, gt1, sh2, sc2, gt2 = jnp.split(mod, N_MOD, axis=-1)
        h = modulate(rms_norm_2(x, g_mix[l]), sh1, sc1)
        mix = hybrid_mixer(h, positions, w_in[l], g_q[l], w_uq[l], g_kv[l], w_uk[l], w_uv[l],
                           rel_bias[l], w_oa[l], w_ob[l], w_out[l])
        x = x + gt1[:, None, :] * mix
        h = modulate(rms_norm_2(x, g_ffn[l]), sh2, sc2)
        ffn = hierarchical_moe(h, w_rg[l], b_rg[l], w_re[l], b_re[l], w_gate[l], w_up[l], w_down[l])
        x = x + gt2[:, None, :] * ffn
    return rms_norm_2(x, g_final)


def setup_inputs(seed=0):
    out = dict(first_inputs(seed))
    for name, value in second_inputs(seed + 1).items():
        if name != "x":
            out[name + "_2"] = value
    return out


def reference(
    x, c, w_ada, b_ada, norm1_w, w_in, b_gate, mu_shift, w0, w2, a0, a2, g2, k_k, k_a, r_k,
    lnx_w, lnx_b, w_att_out, w_rwkv_out, w_o, norm2_w, w_up, conv_w, conv_b, w_down, norm_f_w,
    c_2, positions_2, w_ada_2, b_ada_2, g_mix_2, w_in_2, g_q_2, w_uq_2, g_kv_2, w_uk_2, w_uv_2,
    rel_bias_2, w_oa_2, w_ob_2, w_out_2, g_ffn_2, w_rg_2, b_rg_2, w_re_2, b_re_2, w_gate_2,
    w_up_2, w_down_2, g_final_2,
):
    x = first_block(
        x, c, w_ada, b_ada, norm1_w, w_in, b_gate, mu_shift, w0, w2, a0, a2, g2, k_k, k_a, r_k,
        lnx_w, lnx_b, w_att_out, w_rwkv_out, w_o, norm2_w, w_up, conv_w, conv_b, w_down,
        norm_f_w,
    )
    return second_block(
        x, c_2, positions_2, w_ada_2, b_ada_2, g_mix_2, w_in_2, g_q_2, w_uq_2, g_kv_2, w_uk_2,
        w_uv_2, rel_bias_2, w_oa_2, w_ob_2, w_out_2, g_ffn_2, w_rg_2, b_rg_2, w_re_2, b_re_2,
        w_gate_2, w_up_2, w_down_2, g_final_2,
    )


_drawn_inputs = setup_inputs


def setup_inputs(seed=0):
    import zlib

    import numpy as np

    out = dict(_drawn_inputs(seed))
    spreads = {}
    factors = {'norm1_w': 2.967,
     'b_gate': 4.536,
     'w2': 7.34,
     'a0': 4.233,
     'k_k': 4.53,
     'k_a': 3.9,
     'lnx_w': 4.505,
     'lnx_b': 7.19,
     'conv_b': 3.769,
     'g_mix_2': 4.79,
     'g_q_2': 8.0,
     'g_kv_2': 8.0,
     'b_rg_2': 18.691,
     'b_re_2': 17.972,
     'g_final_2': 7.793,
     'g_ffn_2': 5.404}
    for name, (base, spread) in spreads.items():
        noise = np.random.default_rng([zlib.crc32(name.encode()), seed]).standard_normal(out[name].shape)
        drawn = base * np.exp(spread * noise) if base else spread * noise
        out[name] = __import__('jax').numpy.asarray(drawn.astype(out[name].dtype))
    for name, factor in factors.items():
        out[name] = (out[name] * factor).astype(out[name].dtype)
    return out
```

```python
from contextlib import ExitStack

import numpy as np
import concourse.bass as bass
from concourse import mybir

F32 = mybir.dt.float32
I32 = mybir.dt.int32
ACT = mybir.ActivationFunctionType
ALU = mybir.AluOpType
AX = mybir.AxisListType

P = 128
T = 512
D = 1024
KT = D // P
R = 4
SLOT = 2048
EPS = 1e-6
GN_EPS = 64e-5
KAPPA = float(np.exp(-0.5))
C = 64
NCH = T // C
LEVELS = (2, 4, 8, 16, 32)
NEG = -1e30
FF = 2816
FT = FF // P

COLS = [("b_ada", 48), ("norm1_w", 8), ("b_gate", 16), ("mu", 27), ("w0", 8), ("a0", 8), ("k_k", 8), ("k_a", 8),
        ("r_k", 8), ("lnx_w", 8), ("lnx_b", 8), ("norm2_w", 8), ("conv_w", 132), ("conv_b", 44), ("norm_f_w", 8),
        ("c", 8), ("c_2", 8), ("b_ada_2", 48), ("g_mix_2", 8), ("g_q_2", 2), ("g_kv_2", 1), ("g_ffn_2", 8),
        ("g_final_2", 8)]
COL_AT, NCOL = {}, 0
for _name, _n in COLS:
    COL_AT[_name] = NCOL
    NCOL += _n


def shape_constants():
    p = np.arange(P)[:, None]
    parts = []
    at = {}

    def add(name, a):
        at[name] = (sum(x.shape[1] for x in parts), a.shape[1])
        parts.append(np.ascontiguousarray(a, dtype=np.float32))

    add("ident", (p == np.arange(P)[None, :]))
    add("ones", np.ones((P, P)))
    add("headones", (p // 64 == np.arange(P)[None, :] // 64))
    q, s = p % 64, np.arange(64)[None, :]
    add("eye64", q == s)
    add("upper", q < s)
    add("upto", q <= s)
    add("pair1", (q // 2 == s // 2) & (s < q))
    add("pair1T", (q // 2 == s // 2) & (q < s))
    for b in LEVELS:
        add(f"level{b}", (q // (2 * b) == s // (2 * b)) & (q // b % 2 == 0) & (s // b % 2 == 1))
    add("restart", np.broadcast_to((np.arange(T) % C != 0)[None, :], (P, T)))
    inv = (10000.0 ** (-np.arange(16, dtype=np.float32) / np.float32(16))).astype(np.float32)
    add("freq", inv[np.arange(P) % 16][:, None])
    add("rotsign", np.where(p % 32 < 16, -1.0, 1.0))
    add("rank", np.broadcast_to(8.0 - np.arange(8)[None, :], (P, 8)))
    w = np.arange(256)[None, :]
    add("near", np.where((w >= p) & (w <= p + 128), 0.0, NEG))
    w = np.arange(T)[None, :]
    back = p - w + 384
    add("every4", np.where((back >= 0) & (back % 4 == 0), 0.0, NEG))
    add("every16", np.where((back >= 0) & (back % 16 == 0), 0.0, NEG))
    add("chunked", np.where(p // 64 >= w // 64 - 6, 0.0, NEG))
    add("pick", p == (np.arange(4 * P)[None, :] // P))
    return np.concatenate(parts, axis=1), at


CONSTS, CONST_AT = shape_constants()
NCONST = CONSTS.shape[1]


PHASES = [("ada1", 24), ("lora", 2), ("rkv", 12), ("rw_out", 8), ("qk", 12), ("v", 6), ("at_out", 8), ("w_o", 4),
          ("up", 22), ("down", 12), ("ada2", 24), ("in2", 9), ("lat2", 14), ("mla_out", 8), ("band_out", 8),
          ("w_out2", 4), ("moe", 96)]
FIRST, _n = {}, 0
for _name, _k in PHASES:
    FIRST[_name] = _n
    _n += _k

PRODUCTS = [("lora", "A"), ("ssq", "A"), ("bonus", "D"), ("tv", "AD"), ("tat", "AD"), ("tbh", "AD"), ("tkh", "AD"),
            ("ab", "D"), ("abT", "D"), ("akT", "D"), ("rbT", "D"), ("rkT", "D")]
for _b in LEVELS:
    PRODUCTS += [(f"y{_b}", "AD")] + ([(f"x{_b}", "D")] if _b != LEVELS[-1] else []) + [(f"xT{_b}", "D")]
PRODUCTS += [("w1", "AD"), ("sav", "AD"), ("z", "AD"), ("r", "D"), ("y0", "AD"), ("g", "D"), ("h", "AD")]
PNAMES = [n for n, _ in PRODUCTS]
PER_QUAD = {e: 2 * sum(e in who for _, who in PRODUCTS) for e in "AD"}


def emptied(quad, product, sub, engine):
    i = PNAMES.index(product)
    n = 2 * sum(engine in who for _, who in PRODUCTS[:i])
    if engine in PRODUCTS[i][1]:
        n += sub + 1
    else:
        n += 0
    return quad * PER_QUAD[engine] + n


class Link:

    def __init__(self, eng, sem):
        self.eng, self.sem, self.n, self.off = eng, sem, 0, 0

    def __call__(self, ins):
        ins.then_inc(self.sem, 1)
        self.n += 1
        return self.n + self.off

    def done(self, ins):
        self.eng.wait_ge(self.sem, self(ins))


def build(nc, a, stop=99):
    with ExitStack() as ctx:
        def sb(name, shape, dt=F32):
            return ctx.enter_context(nc.sbuf_tensor(name, shape, dt))

        def sem(name):
            return ctx.enter_context(nc.semaphore(name))

        ring = sb("ring", [P, R, SLOT])
        const = sb("const", [P, CONST_AT["near"][0]])
        cols = sb("cols", [P, NCOL])
        mod = sb("mod", [P, 48])[:, :]
        small = sb("small", [P, 160])
        hT = sb("hT", [P, KT, T])[:, :, :]
        arena = sb("arena", [P, 37888])
        ps = ctx.enter_context(nc.psum_tensor("ps", [P, 8, 512], F32))

        def area(at, *dims):
            n = int(np.prod(dims))
            v = arena[:, at:at + n]
            if len(dims) == 1:
                return v
            if len(dims) == 2:
                return v.rearrange("p (a b) -> p a b", b=dims[1])
            return v.rearrange("p (a b c) -> p a b c", b=dims[1], c=dims[2])

        def cst(name):
            o, n = CONST_AT[name]
            return const[:, o:o + n]

        def col(name, i=0, n=1):
            return cols[:, COL_AT[name] + i:COL_AT[name] + i + n]

        ident, ones, headones, eye64 = cst("ident"), cst("ones"), cst("headones"), cst("eye64")

        x_in = area(20480, KT, T)
        RT, Y0 = area(0, 8, T), area(4096, 8, T)
        GT = area(8192, 8, NCH, C)
        ST = area(12288, NCH, 8, C)
        BON = area(16384, 8, T)
        tmp = [[area(20480 + (s * 14 + i) * T, T) for i in range(14)] for s in range(2)]
        LOW = area(34816, T)
        GLO, GLO2 = area(35328, T), area(35840, T)
        W2A2 = area(36352, D)
        G2 = area(20480, 2, D)
        ytmp = [[area(22528 + (s * 3 + i) * T, T) for i in range(3)] for s in range(2)]
        merged = area(30720, KT, T)
        gate = area(28416, 2, T)
        QK = area(0, 24, T)
        VT = area(12288, 4, 1536)
        masks = area(18432, 1792)
        near, every4, every16 = masks[:, 0:256], masks[:, 256:768], masks[:, 768:1280]
        xT = area(0, KT, T)
        hid = area(4096, FT, T)
        cvt = [[area(16384 + (s * 2 + i) * T, T) for i in range(2)] for s in range(2)]
        sil = area(18432, 2, T)

        QL, KV = area(4096, 2, T), area(5120, T)
        KR, KRS = area(5632, T), area(6144, T)
        QA, KA = area(6656, 8, T), area(10752, 8, T)
        VA = area(14848, 4, T)
        QB, KB, VB = area(16896, 4, T), area(18944, 4, T), area(20992, 4, T)
        BT = area(23040, 8, T)
        CH = area(27136, T)
        COS, SIN = area(27648, T), area(28160, T)
        PROB2 = [area(28672 + i * T, T) for i in range(2)], area(29696, T), [area(30208 + i * T, T) for i in range(2)]
        OA, OB = area(31232, 4, T), area(33280, 4, T)
        LSQ, LRT = area(35328, 3, T), area(36864, 2, T)
        ROT = area(35328, 2, T)
        ANG = area(31232, 4, T)
        BROW = area(33280, 640)
        merged2, gate2 = area(6656, KT, T), area(4096, 2, T)
        CT = area(4096, 8, T)
        SG, MH, CB = area(8192, 2, T), area(9216, 4, T), area(11264, 2, T)
        WR, BRT = area(12288, KT, 36), area(12576, 36)
        RL = area(12672, 4, 36)
        rt_ = [area(12832 + 160 * i, 160) for i in range(12)]
        C2S = small[:, 88:96]
        rt_comb = area(14752, 4, 32)
        rt_e = area(14880, 20)
        PICK = area(14912, 4 * P)
        EPSC, GNC, ZERO, ONE, ZSINK = [small[:, i:i + 1] for i in range(5)]
        NM, DEN, RD = small[:, 6:8], small[:, 8:10], small[:, 10:12]
        PK = small[:, 12:20].rearrange("p (a b) -> p a b", b=4)
        OMU, OKA, GAIN = small[:, 20:47], small[:, 48:56], small[:, 56:64]
        PLS = [small[:, 64:72], small[:, 72:80]]
        ZERO8 = small[:, 80:88]
        RSTD = sb("rstd", [P, T])[:, :]

        full = [sem(f"full{i}") for i in range(R)]
        half_done = sem("half_done")
        freed = {"A": sem("freed_by_act"), "D": sem("freed_by_dve")}
        act_link, dve_link, pool_link = sem("act_link"), sem("dve_link"), sem("pool_link")
        got_const, got_x, got_lora, got_g2, got_masks, got_x1 = [sem(n) for n in (
            "got_const", "got_x", "got_lora", "got_g2", "got_masks", "got_x1")]
        squared, summed, rooted, normed = sem("squared"), sem("summed"), sem("rooted"), sem("normed")
        mod_ready = sem("mod_ready")
        scaled = sem("scaled")
        lora_ready = sem("lora_ready")
        made = sem("made")
        emptA, emptD = sem("emptied_by_act"), sem("emptied_by_dve")
        chan, cum, decay, maskp = sem("chan_ready"), sem("cum_ready"), sem("decay_ready"), sem("masked_by_pool")
        stepped, state_ready = sem("stepped"), sem("state_ready")
        y_made, mean_made, var_made, g_made = sem("y_made"), sem("mean_made"), sem("var_made"), sem("g_made")
        y_added, centred, y_sq, y_root, y_final = [sem(n) for n in (
            "y_added", "centred", "y_squared", "y_rooted", "y_final")]
        gate_ready = sem("gate_ready")
        scored, masked, peaked, probbed, turned, turnedS, weighed, outed, oturned, oready, recipd = [sem(n) for n in (
            "scored", "masked", "peaked", "probbed", "turned", "turned_copied", "weighed", "outed",
            "out_turned", "out_ready", "reciprocal_ready")]
        convd, silud, hidd = sem("conv_scaled"), sem("silu_ready"), sem("hidden_ready")
        silu_c, got_bias, got_pos, got_router = sem("silu_c"), sem("got_bias"), sem("got_positions"), sem("got_router")
        bias_row, bias_out = sem("bias_row"), sem("bias_out")
        lat_sq, lat_sum, lat_root, lat_ready = [sem("latent_" + n) for n in ("squared", "summed", "rooted", "ready")]
        angled, rotated, band_ready = sem("angled"), sem("sines"), sem("band_ready")
        routed, route_exp, combined, ct_made, ct_ready = [sem(n) for n in (
            "logits_made", "route_exp", "combined", "combine_turned", "combine_ready")]
        gu_done, cb_made, cb_read, silu_m, mhid, down_made, down_added = [sem(n) for n in (
            "gate_up_done", "weight_spread", "weight_copied", "moe_silu", "moe_hidden", "down_made", "down_added")]
        stored = sem("stored")

        HALVES = {"ada1": (0, 1), "lora": (0, 3), "rkv": (0, 24), "rw_out": (8, 8), "qk": (12, 12), "v": (6, 6),
                  "at_out": (8, 8), "w_o": (0, 8), "up": (0, 44), "down": (0, 8),
                  "ada2": (0, 1), "in2": (9, 8), "lat2": (14, 14), "mla_out": (8, 8), "band_out": (8, 8),
                  "w_out2": (0, 8), "moe": (64, 64)}
        BEFORE, na, nd = {}, 0, 0
        for ph, _k in PHASES:
            BEFORE[ph] = {"A": na, "D": nd}
            x_, y_ = HALVES.get(ph, (0, 0))
            na, nd = na + x_, nd + y_

        def drain_psum(pe, phase):
            for e in "AD":
                if BEFORE[phase][e]:
                    pe.wait_ge(freed[e], BEFORE[phase][e])

        def bc(v, n):
            return v.unsqueeze(2).broadcast_to([v.shape[0], v.shape[1], n])

        def rep(v, n):
            return v.unsqueeze(1).broadcast_to([v.shape[0], n, v.shape[1]])

        def chunks(v):
            return v.rearrange("p (c k) -> p c k", k=C)

        units = [(qt, h) for qt in range(4) for h in range(8)]
        PROB1 = [area(20224 + i * 1280, 1280) for i in range(2)], area(22784, 1280), [area(25344 + i * T, T) for i in range(2)]
        OT1 = area(26368, 4, T)

        def parts1(unit, i):
            qt, h = unit
            r = slice(h % 2 * 64, h % 2 * 64 + 64)
            k0 = max(0, qt - 1) * P
            scores, vals, maskl = [], [], []
            for g in range(3):
                lo, hi = (k0 if g == 0 else 0), (qt + 1) * P
                qT, kT = QK[r, g * 8 + h // 2, qt * P:qt * P + P], QK[r, g * 8 + 4 + h // 2, lo:hi]
                scores.append((g, [(qT, kT)], g, hi - lo))
                m = near[:, 256 - (hi - lo):256] if g == 0 else (every4, every16)[g - 1][:, 384 - qt * P:T]
                maskl.append(m)
                vals += [VT[:, kt, g * T + h * 64:g * T + h * 64 + 64] for kt in range(lo // P, hi // P)]
            return {"scores": scores, "tiles": len(vals), "values": vals, "masks": maskl,
                    "out": slice(h * 64, h * 64 + 64), "scale": 0.125}

        def parts_mla(unit, i):
            qt, h = unit
            n_ = (qt + 1) * P
            return {"scores": [(0, [(QA[0:96, h, qt * P:n_], KA[0:96, h, 0:n_])], i % 2, n_)], "tiles": qt + 1,
                    "values": [VA[:, kt, h * 64:h * 64 + 64] for kt in range(qt + 1)],
                    "masks": [CH[:, 384 - qt * P:T]], "out": slice(h * 64, h * 64 + 64), "scale": 96 ** -0.5}

        def parts_band(unit, i):
            qt, h = unit
            n_, r = (qt + 1) * P, slice(h % 2 * 64, h % 2 * 64 + 64)
            return {"scores": [(0, [(QB[r, h // 2, qt * P:n_], KB[r, h // 2, 0:n_])], i % 2, n_)], "tiles": qt + 1,
                    "values": [VB[:, kt, h * 64:h * 64 + 64] for kt in range(qt + 1)],
                    "masks": [BT[:, h, 384 - qt * P:T]], "out": slice(h * 64, h * 64 + 64), "scale": 0.125}

        TURNED = []
        for parts_, us_ in ((parts1, units), (parts_mla, units), (parts_band, units)):
            for i_, u_ in enumerate(us_):
                TURNED.append((TURNED[-1] if TURNED else 0) + -(-parts_(u_, i_)["tiles"] // 4))

        MOE_SLOTS = [("g", 0), ("u", 0)]
        for e_ in range(1, 32):
            MOE_SLOTS += [("g", e_), ("u", e_), ("d", e_ - 1)]
        MOE_SLOTS += [("d", 31)]
        MOE_HEAD, MOE_ROUNDS = 2 + 3 * 4, 6

        def moe_release(s, first):
            if s < R:
                return half_done, 2 * (first + s - R) + 2
            kind, e = MOE_SLOTS[s - R]
            return {"g": (gu_done, 4 * e + 2), "u": (gu_done, 4 * e + 4), "d": (down_made, 8 * e + 8)}[kind]

        block = ctx.enter_context(nc.Block())

        @block.sync
        def _(sp):
            for src, dst in ((a["consts"][:, 0:CONST_AT["near"][0]], const[:]), (a["cols"], cols[:])):
                sp.dma_start(dst, src).then_inc(got_const, 16)
            xv = a["x"].rearrange("(k p) t -> p k t", p=P)
            n = [0]

            def load(src, parts=P):
                m = n[0]
                n[0] += 1
                if m >= R:
                    sp.wait_ge(half_done, 2 * (m - R) + 2)
                size = src.shape[1] * src.shape[2]
                dst = ring[0:parts, m % R, 0:size].rearrange("p (k c) -> p k c", c=src.shape[2])
                sp.dma_start(dst, src).then_inc(full[m % R], 16)

            def wcols(w, c0, nc_=256):
                return w.rearrange("(k p) c -> p k c", p=P)[:, :, c0:c0 + nc_]

            def stream(w, count, at=0, step=256):
                first = n[0]
                wv = w.rearrange("(k p) c -> p k c", p=P)
                with sp.Fori(0, count // R) as i:
                    for j in range(R):
                        m = first + j
                        sp.wait_ge(half_done, i * (2 * R) + (2 * (m - R) + 2))
                        sp.dma_start(ring[:, m % R, :].rearrange("p (k c) -> p k c", c=256),
                                     wv[:, :, bass.ds(i * (R * 256) + (at + j * 256), 256)]).then_inc(full[m % R], 16)
                n[0] += count // R * R

            for j in range(R):
                load(wcols(a["w_ada"], j * 256))
            sp.dma_start(x_in, xv).then_inc(got_x, 16)
            sp.dma_start(W2A2[0:64, :], a["w2"]).then_inc(got_lora, 16)
            sp.dma_start(W2A2[64:128, :], a["a2"]).then_inc(got_lora, 16)
            stream(a["w_ada"], 20, at=4 * 256)
            RW = 4608
            if stop < 1:
                return
            load(wcols(a["w_in"], RW + 3072))
            load(wcols(a["w_in"], RW + 3328, 32))
            for q in range(4):
                for part in range(3):
                    load(wcols(a["w_in"], RW + part * D + q * 256))
            if stop < 2:
                return
            for g in range(4):
                load(wcols(a["w_in"], 7968 + D + g * 256))
                if g == 0:
                    sp.wait_ge(made, 8 * len(PRODUCTS))
                    sp.wait_ge(emptD, 4 * PER_QUAD["D"])
                    sp.wait_ge(emptA, 4 * PER_QUAD["A"])
                    sp.dma_start(G2[:, 0, :], a["g2"][0:128, :]).then_inc(got_g2, 16)
                    sp.dma_start(G2[0:32, 1, :], a["g2"][128:160, :]).then_inc(got_g2, 16)
                load(wcols(a["w_rwkv_out"], g * 256))
            if stop < 3:
                return
            for g in range(3):
                for part in range(2):
                    for c in range(2):
                        load(wcols(a["w_in"], g * 1536 + part * 512 + c * 256))
                if g == 0:
                    sp.wait_ge(half_done, 2 * FIRST["qk"])
                    sp.dma_start(masks, a["consts"][:, CONST_AT["near"][0]:CONST_AT["near"][0] + 1792]).then_inc(got_masks, 16)
            for g in range(3):
                for c in range(2):
                    load(wcols(a["w_in"], g * 1536 + 1024 + c * 256))
            for g in range(4):
                load(wcols(a["w_in"], 7968 + g * 256))
                load(wcols(a["w_att_out"], g * 256))
            if stop < 4:
                return
            for g in range(4):
                load(wcols(a["w_o"], g * 256))
                if g == 0:
                    sp.wait_ge(scored, len(units))
                    sp.dma_start(xT, xv).then_inc(got_x1, 16)
            upv = a["w_up"].rearrange("(k p) (g c) -> p g k c", p=P, g=2)
            first = n[0]
            def up_load(m, j):
                for g in range(2):
                    dst = ring[:, m % R, :].rearrange("p (g k c) -> p g k c", g=2, c=P)[:, g]
                    sp.dma_start(dst, upv[:, g, :, j]).then_inc(full[m % R], 8 * 2)
            with sp.Fori(0, 5) as i:
                for j in range(R):
                    m = first + j
                    sp.wait_ge(half_done, i * (2 * R) + (2 * (m - R) + 2))
                    up_load(m, bass.ds(i * (R * P) + j * P, P))
            for j in range(20, 22):
                m = first + j
                sp.wait_ge(half_done, 2 * (m - R) + 2)
                up_load(m, bass.ds(j * P, P))
            n[0] += 22
            dv = a["w_down"].rearrange("(k p) c -> p k c", p=P)
            for mm in range(4):
                for k0, k1 in ((0, 8), (8, 16), (16, 22)):
                    load(dv[:, k0:k1, mm * 256:mm * 256 + 256])

            if stop < 5:
                return
            stream(a["w_ada_2"], 24)
            load(wcols(a["w_in_2"], 0))
            load(wcols(a["w_kvr"], 0))
            load(wcols(a["w_kvr"], 256, 128))
            for c in range(6):
                load(wcols(a["w_in_2"], 416 + c * 256))
            for h in range(8):
                load(wcols(a["w_uq"], h * 256))
            for c in range(4):
                load(wcols(a["w_uk_2"], c * P, P))
            for c in range(2):
                load(wcols(a["w_uv_2"], c * 256))
            for w, at in ((a["w_oa_2"], 1952), (a["w_ob_2"], 1952 + D)):
                for g in range(4):
                    load(wcols(a["w_in_2"], at + g * 256))
                    load(wcols(w, g * 256))
            for g in range(4):
                load(wcols(a["w_out_2"], g * 256))
            if stop < 6:
                return
            first = n[0]
            gv = a["w_gate_2"].rearrange("e (k p) f -> p e k f", p=P)
            uv = a["w_up_2"].rearrange("e (k p) f -> p e k f", p=P)
            wd = a["w_down_2"].rearrange("e (k p) d -> p e k d", p=P)

            def moe_load(s, kind, e, free):
                m = first + s
                sem_, v = free
                sp.wait_ge(sem_, v)
                w = {"g": gv, "u": uv, "d": wd}[kind]
                c_ = 256 if kind != "d" else D
                src = w[:, e] if isinstance(e, int) else w[:, bass.ds(e, 1)].rearrange("p e k c -> p (e k) c")
                sp.dma_start(ring[:, m % R, :].rearrange("p (k c) -> p k c", c=c_), src).then_inc(full[m % R], 16)

            for s in range(MOE_HEAD):
                moe_load(s, *MOE_SLOTS[s], moe_release(s, first))
            with sp.Fori(0, MOE_ROUNDS) as i:
                for s in range(MOE_HEAD, MOE_HEAD + 12):
                    kind, e = MOE_SLOTS[s]
                    sem_, v = moe_release(s, first)
                    moe_load(s, kind, i * 4 + e, (sem_, i * (32 if sem_ is down_made else 16) + v))
            for s in range(MOE_HEAD + 12 * MOE_ROUNDS, 96):
                moe_load(s, *MOE_SLOTS[s], moe_release(s, first))
            sp.wait_ge(normed, 6)
            sp.dma_start(a["out"].rearrange("(k p) t -> p k t", p=P), hT).then_inc(stored, 16)
            sp.wait_ge(stored, 16)

        @block.tensor
        def _(pe):
            n = [0]

            def full_value(m):
                up0, up1 = FIRST["up"], FIRST["up"] + 22
                ups = sum(1 for x in range(up0, min(m, up1 - 1) + 1) if x % R == m % R)
                return 16 * (m // R + 1 + ups)

            def slot():
                m = n[0]
                n[0] += 1
                pe.wait_ge(full[m % R], full_value(m))
                return m

            def half(m, hf, bank, rhs, width=P, kts=KT, out=None, start=True, stop=True, inc=1, cols_=256, slot_=None):
                w = ring[:, m % R, 0:kts * cols_].rearrange("p (k c) -> p k c", c=cols_)
                dst = ps[0:width, bank, :] if out is None else out
                for k in range(kts):
                    mm = pe.matmul(dst, w[:, k, hf * P:hf * P + width], rhs(k),
                                   start=(start and k == 0), stop=(stop and k == kts - 1))
                mm.then_inc(half_done, inc)

            def wait_bank(phase, hh, who):
                cnt = who(hh)
                if cnt:
                    pe.wait_ge(freed[cnt[0]], cnt[1])

            pe.wait_ge(got_const, 32)

            def ada_halves(m, at, cvec):
                for hf in range(2):
                    w = ring[:, m % R, :].rearrange("p (k c) -> p k c", c=256)
                    o = ps[:, 7, bass.ds(at + hf, 1)] if not isinstance(at, int) else ps[:, 7, at + hf:at + hf + 1]
                    for k in range(KT):
                        mm = pe.matmul(o, w[:, k, hf * P:hf * P + P], cvec(k), start=(k == 0), stop=(k == KT - 1))
                    mm.then_inc(half_done, 1)

            def ada(cvec):
                first = n[0]
                with pe.Fori(0, 24 // R) as i:
                    for j in range(R):
                        m = first + j
                        pe.wait_ge(full[m % R], i * 16 + full_value(m))
                        ada_halves(m, i * (2 * R) + 2 * j, cvec)
                n[0] += 24

            ada(lambda k: col("c", k))

            def norm_sum(k_norm):
                pe.wait_ge(squared, k_norm + 1)
                for k in range(KT):
                    mm = pe.matmul(ps[:, 6, :], ones, hT[:, k, :], start=(k == 0), stop=(k == KT - 1))
                mm.then_inc(summed, 1)

            norm_sum(0)

            def h_(k):
                return hT[:, k, :]

            if stop < 1:
                return
            pe.wait_ge(normed, 1)
            drain_psum(pe, "lora")
            m = slot()
            half(m, 0, 0, h_)
            half(m, 1, 1, h_)
            m = slot()
            half(m, 0, 2, h_, width=32, cols_=32, inc=2)

            pe.wait_ge(lora_ready, 1)
            pe.wait_ge(got_lora, 32)
            made_n = [0]

            def product(q, name, s, body, dep=()):
                i = made_n[0]
                made_n[0] += 1
                assert PNAMES[(i // 2) % len(PRODUCTS)] == name and i % 2 == s
                idx = (i // 2) % len(PRODUCTS)
                if i >= 2:
                    pq, pn = (q, PNAMES[idx - 1]) if idx else (q - 1, PNAMES[-1])
                    for e, sm in (("A", emptA), ("D", emptD)):
                        if e in PRODUCTS[PNAMES.index(pn)][1]:
                            pe.wait_ge(sm, emptied(pq, pn, s, e))
                for d in dep:
                    for e, sm in (("A", emptA), ("D", emptD)):
                        if e in PRODUCTS[PNAMES.index(d)][1]:
                            pe.wait_ge(sm, emptied(q, d, s, e))
                last = body(4 + 2 * s, 5 + 2 * s)
                last.then_inc(made, 1)

            def per_chunk(banks, terms):
                for e in range(2):
                    r = slice(e * 64, e * 64 + 64)
                    for c in range(NCH):
                        cc = slice(c * C, c * C + C)
                        for i, (l, x) in enumerate(terms):
                            mm = pe.matmul(ps[r, banks[e], cc], l[r, cc], x[r, 0:64] if x is eye64 else x[r, cc],
                                           start=(i == 0), stop=(i == len(terms) - 1))
                return mm

            for q in range(4):
                drain_psum(pe, "rkv") if q == 0 else None
                for part in range(3):
                    m = slot()
                    for hf in range(2):
                        hh = q * 6 + part * 2 + hf
                        if hh >= 4:
                            pe.wait_ge(freed["D"], BEFORE["rkv"]["D"] + hh - 3)
                        half(m, hf, hh % 4, h_)
                for s in range(2):
                    j = 2 * q + s

                    def lora(A, B, j=j):
                        pe.matmul(ps[:, A, :], W2A2[0:64, j * P:j * P + P], LOW[0:64, :], start=True, stop=True)
                        return pe.matmul(ps[:, B, :], W2A2[64:128, j * P:j * P + P], LOW[64:128, :], start=True, stop=True)
                    product(q, "lora", s, lora)
                for s in range(2):
                    pe.wait_ge(chan, 6 * q + 1 + s)
                    product(q, "ssq", s, lambda A, B: pe.matmul(ps[:, A, :], headones, tmp[s][10], start=True, stop=True))
                for s in range(2):
                    pe.wait_ge(chan, 6 * q + 3 + s)
                    product(q, "bonus", s, lambda A, B: pe.matmul(ps[:, A, :], headones, tmp[s][10], start=True, stop=True))
                for s in range(2):
                    t_ = tmp[s]
                    product(q, "tv", s, lambda A, B: per_chunk((A, B), [(t_[2], eye64)]))
                for name, b in (("tat", 6), ("tbh", 5), ("tkh", 3)):
                    for s in range(2):
                        t_ = tmp[s]
                        pe.wait_ge(chan, 6 * q + 5 + s)
                        product(q, name, s, lambda A, B: per_chunk((A, B), [(t_[b], eye64)]))
                for name, l, x in (("ab", 6, 4), ("abT", 4, 6), ("akT", 8, 6), ("rbT", 4, 0), ("rkT", 8, 0)):
                    for s in range(2):
                        t_ = tmp[s]
                        product(q, name, s, lambda A, B: per_chunk((A, B), [(t_[l], t_[x])]))
                nlev = len(LEVELS)
                for li, b in enumerate(LEVELS):
                    prev = ("ab", "abT") if li == 0 else (f"x{LEVELS[li - 1]}", f"xT{LEVELS[li - 1]}")
                    mb = 6 if li % 2 == 0 else 8
                    for s in range(2):
                        t_ = tmp[s]
                        pe.wait_ge(maskp, q * 2 * nlev + 2 * li + s + 1)
                        product(q, f"y{b}", s, lambda A, B: per_chunk((A, B), [(t_[mb], t_[2])]), dep=prev)
                    if b != LEVELS[-1]:
                        for s in range(2):
                            t_ = tmp[s]
                            product(q, f"x{b}", s, lambda A, B: per_chunk((A, B), [(t_[3], t_[4])]), dep=(f"y{b}",))
                    for s in range(2):
                        t_ = tmp[s]
                        product(q, f"xT{b}", s, lambda A, B: per_chunk((A, B), [(t_[4], t_[3])]), dep=(f"y{b}",))
                fin = f"xT{LEVELS[-1]}"
                for s in range(2):
                    t_ = tmp[s]
                    product(q, "w1", s, lambda A, B: per_chunk((A, B), [(t_[11], t_[1])]), dep=(fin,))
                for s in range(2):
                    t_ = tmp[s]
                    product(q, "sav", s, lambda A, B: per_chunk((A, B), [(t_[3], t_[4])]), dep=("w1",))
                for s in range(2):
                    t_ = tmp[s]
                    product(q, "z", s, lambda A, B: per_chunk((A, B), [(t_[3], t_[7])]), dep=())
                for s in range(2):
                    t_ = tmp[s]
                    product(q, "r", s, lambda A, B: per_chunk((A, B), [(t_[5], t_[12])]), dep=("z",))
                for s in range(2):
                    t_ = tmp[s]
                    product(q, "y0", s, lambda A, B: per_chunk((A, B), [(t_[2], t_[12]), (t_[1], t_[13])]), dep=("sav",))
                for s in range(2):
                    t_ = tmp[s]
                    product(q, "g", s, lambda A, B: per_chunk((A, B), [(t_[5], t_[9])]))
                for s in range(2):
                    t_ = tmp[s]
                    product(q, "h", s, lambda A, B: per_chunk((A, B), [(t_[9], t_[2]), (t_[10], t_[1])]))

            if stop < 2:
                return
            for e, sm in (("A", emptA), ("D", emptD)):
                pe.wait_ge(sm, 4 * PER_QUAD[e])
            for c in range(1, NCH - 1):
                pe.wait_ge(state_ready, c - 1) if c > 1 else None
                A = 4 + 2 * (c % 2)
                for e in range(2):
                    r = slice(e * 64, e * 64 + 64)
                    for j in range(8):
                        mm = pe.matmul(ps[r, A + e, j * C:j * C + C], GT[r, j, c, :], ST[r, c - 1, j, :],
                                       start=True, stop=True)
                mm.then_inc(stepped, 1)
            pe.wait_ge(state_ready, NCH - 2)
            pe.wait_ge(got_g2, 32)

            def y_state(j):
                if j >= 2:
                    pe.wait_ge(y_final, j - 1)
                for e in range(2):
                    r = slice(e * 64, e * 64 + 64)
                    for c in range(1, NCH):
                        mm = pe.matmul(ps[r, 4 + 2 * (j % 2) + e, c * C:c * C + C], ST[r, c - 1, j, :],
                                       RT[r, j, c * C:c * C + C], start=True, stop=True)
                mm.then_inc(y_made, 1)

            def y_mean(j):
                pe.wait_ge(y_added, j + 1)
                if j >= 2:
                    pe.wait_ge(centred, j - 1)
                pe.matmul(ps[:, j % 2, :], headones, Y0[:, j, :], start=True, stop=True).then_inc(mean_made, 1)

            def y_var(j):
                pe.wait_ge(y_sq, j + 1)
                if j >= 2:
                    pe.wait_ge(y_root, j - 1)
                pe.matmul(ps[:, 2 + j % 2, :], headones, ytmp[j % 2][0], start=True, stop=True).then_inc(var_made, 1)

            def y_gate(j):
                b = 4 + 2 * (j % 2)
                pe.matmul(ps[:, b, :], G2[:, 0, j * P:j * P + P], GLO, start=True, stop=False)
                pe.matmul(ps[:, b, :], G2[0:32, 1, j * P:j * P + P], GLO2[0:32], start=False, stop=True).then_inc(g_made, 1)

            for t in range(8 + 2):
                if 0 <= t - 2 < 8:
                    y_var(t - 2)
                if 0 <= t - 1 < 8:
                    y_mean(t - 1)
                    y_gate(t - 1)
                if t < 8:
                    y_state(t)
            pe.wait_ge(y_final, 8)

            def gated_projection(phase, rhs, kts):
                drain_psum(pe, phase)
                for g in range(4):
                    m = slot()
                    for hf in range(2):
                        i = 2 * g + hf
                        if i >= 2:
                            pe.wait_ge(freed["A"], BEFORE[phase]["A"] + i - 1)
                        half(m, hf, i % 2, h_)
                    m = slot()
                    for hf in range(2):
                        i = 2 * g + hf
                        if i >= 2:
                            pe.wait_ge(freed["D"], BEFORE[phase]["D"] + i - 1)
                        half(m, hf, 2 + i % 2, rhs, kts=kts)

            gated_projection("rw_out", lambda k: Y0[:, k, :], KT)

            if stop < 3:
                return
            def alternate(phase, hh):
                if hh >= 4:
                    e = "AD"[hh % 2]
                    pe.wait_ge(freed[e], BEFORE[phase][e] + (hh - 4) // 2 + 1)

            drain_psum(pe, "qk")
            for t in range(12):
                m = slot()
                for hf in range(2):
                    alternate("qk", 2 * t + hf)
                    half(m, hf, (2 * t + hf) % 4, h_)

            def token_major(phase, count):
                drain_psum(pe, phase)
                for t in range(count):
                    m = slot()
                    w = ring[:, m % R, :].rearrange("p (k c) -> p k c", c=256)
                    for hf in range(2):
                        hh = 2 * t + hf
                        alternate(phase, hh)
                        for tt in range(2):
                            tok = (2 * hf + tt) * P
                            for k in range(KT):
                                mm = pe.matmul(ps[:, hh % 4, tt * 256:tt * 256 + 256], hT[:, k, tok:tok + P],
                                               w[:, k, :], start=(k == 0), stop=(k == KT - 1))
                        mm.then_inc(half_done, 1)

            token_major("v", 6)
            drain_psum(pe, "at_out")

            def attend(u0, us, parts_of, s_banks):
                def scores(i):
                    if i >= s_banks:
                        pe.wait_ge(masked, u0 + i - s_banks + 1)
                    bank = 0
                    for q_, ks, bk, n_ in parts_of(us[i], i)["scores"]:
                        for t_, (l, x) in enumerate(ks):
                            mm = pe.matmul(ps[:, bk, 0:n_], l, x, start=(t_ == 0), stop=(t_ == len(ks) - 1))
                    mm.then_inc(scored, 1)

                def turn(i):
                    n_ = parts_of(us[i], i)["tiles"]
                    pe.wait_ge(probbed, u0 + i + 1)
                    for t_ in range(n_):
                        if t_ % 4 == 0:
                            g = turn_n[0]
                            turn_n[0] += 1
                            if g >= 2:
                                pe.wait_ge(turnedS, g - 1)
                        mm = pe.transpose(ps[:, 4 + g % 2, t_ % 4 * P:t_ % 4 * P + P],
                                          prob[(u0 + i) % 2][:, t_ * P:t_ * P + P], ident)
                        if t_ % 4 == 3 or t_ == n_ - 1:
                            mm.then_inc(turned, 1)

                def weigh(i):
                    u = u0 + i
                    pe.wait_ge(turnedS, turn_n[0])
                    if u >= 2:
                        pe.wait_ge(outed, u - 1)
                    vs = parts_of(us[i], i)["values"]
                    for t_, v in enumerate(vs):
                        mm = pe.matmul(ps[:, 6 + u % 2, 0:64], probT[:, t_ * P:t_ * P + P], v,
                                       start=(t_ == 0), stop=(t_ == len(vs) - 1))
                    mm.then_inc(weighed, 1)

                def turn_out(i):
                    w = (u0 + i) // 8
                    pe.wait_ge(outed, u0 + i + 1)
                    if w >= 1:
                        pe.wait_ge(oready, w)
                    for t_ in range(4):
                        mm = pe.transpose(ps[:, 3, t_ * P:t_ * P + P], otok[w % 2][:, t_ * P:t_ * P + P], ident)
                    mm.then_inc(oturned, 1)

                scores(0)
                for i in range(len(us)):
                    if i + 1 < len(us):
                        scores(i + 1)
                    turn(i)
                    weigh(i)
                    if i % 8 == 7:
                        turn_out(i)

            turn_n = [0]
            prob, probT, otok = PROB1
            attend(0, units, parts1, 1)
            pe.wait_ge(oready, 4)
            gated_projection("at_out", lambda k: OT1[:, k, :], 4)

            if stop < 4:
                return
            drain_psum(pe, "w_o")
            for t in range(4):
                m = slot()
                for hf in range(2):
                    hh = 2 * t + hf
                    if hh >= 4:
                        pe.wait_ge(freed["D"], BEFORE["w_o"]["D"] + hh - 3)
                    half(m, hf, hh % 4, lambda k: merged[:, k, :])

            norm_sum(1)
            pe.wait_ge(normed, 2)
            drain_psum(pe, "up")
            first = n[0]

            def up_slot(m, fv, hbase):
                pe.wait_ge(full[m % R], fv)
                for g in range(2):
                    w = ring[:, m % R, :].rearrange("p (g k c) -> p g k c", g=2, c=P)[:, g]
                    if hbase is not None:
                        pe.wait_ge(freed["D"], hbase + g)
                    for k in range(KT):
                        mm = pe.matmul(ps[:, (2 * (m - first) + g) % 4, :], w[:, k, :], h_(k), start=(k == 0), stop=(k == KT - 1))
                    mm.then_inc(half_done, 1)

            D0 = BEFORE["up"]["D"]
            for j in range(2):
                up_slot(first + j, full_value(first + j), None)
            with pe.Fori(0, 5) as i:
                for j in range(2, 2 + R):
                    m = first + j
                    up_slot(m, i * 32 + full_value(m), i * (2 * R) + (D0 + 2 * j - 3))
            n[0] += 22
            pe.wait_ge(hidd, FT)
            drain_psum(pe, "down")
            for mm_ in range(4):
                for part, kts in enumerate((8, 8, 6)):
                    m = slot()
                    for hf in range(2):
                        hh = 2 * mm_ + hf
                        if hh >= 4 and part == 0:
                            pe.wait_ge(freed["D"], BEFORE["down"]["D"] + hh - 3)
                        half(m, hf, hh % 4, lambda k, part=part: hid[:, part * 8 + k, :], kts=kts,
                             start=(part == 0), stop=(part == 2))
            norm_sum(2)

            if stop < 5:
                return
            pe.wait_ge(silu_c, 1)
            drain_psum(pe, "ada2")
            ada(lambda k: C2S[:, k:k + 1])
            norm_sum(3)
            pe.wait_ge(normed, 4)
            drain_psum(pe, "in2")
            o = 0
            for t in range(7):
                m = slot()
                for hf in range(1 if t == 2 else 2):
                    alternate("in2", o)
                    half(m, hf, o % 4, h_, cols_=P if t == 2 else 256, inc=2 if t == 2 else 1)
                    o += 1

            def token_slots(phase, o, count, src, kts):
                for t in range(count):
                    m = slot()
                    w = ring[:, m % R, 0:kts * 256].rearrange("p (k c) -> p k c", c=256)
                    for hf in range(2):
                        alternate(phase, o)
                        for tt in range(2):
                            tok = (2 * hf + tt) * P
                            for k in range(kts):
                                mm = pe.matmul(ps[:, o % 4, tt * 256:tt * 256 + 256], src(k)[:, tok:tok + P],
                                               w[:, k, :], start=(k == 0), stop=(k == kts - 1))
                        mm.then_inc(half_done, 1)
                        o += 1

            token_slots("in2", o, 2, h_, KT)
            pe.wait_ge(lat_sq, 1)
            pe.matmul(ps[:, 6, :], ones, LSQ[:, 0, :], start=True, stop=False)
            pe.matmul(ps[:, 6, :], ones, LSQ[:, 1, :], start=False, stop=True)
            pe.matmul(ps[:, 7, :], ones, LSQ[:, 2, :], start=True, stop=True).then_inc(lat_sum, 1)
            pe.wait_ge(lat_ready, 1)
            drain_psum(pe, "lat2")
            o = 0
            for h in range(8):
                m = slot()
                for hf in range(2):
                    alternate("lat2", o)
                    half(m, hf, o % 4, lambda k: QL[:, k, :], width=96, kts=2)
                    o += 1
            for t in range(4):
                m = slot()
                for hf in range(2):
                    alternate("lat2", o)
                    w = ring[:, m % R, 0:P]
                    pe.matmul(ps[0:64, o % 4, :], w[:, hf * 64:hf * 64 + 64], KV, start=True, stop=True).then_inc(half_done, 1)
                    o += 1
            token_slots("lat2", o, 2, lambda k: KV, 1)
            drain_psum(pe, "mla_out")
            pe.wait_ge(band_ready, 1)
            prob, probT, otok = PROB2
            attend(32, units, parts_mla, 2)
            attend(64, units, parts_band, 2)
            pe.wait_ge(oready, 12)
            gated_projection("mla_out", lambda k: OA[:, k, :], 4)
            gated_projection("band_out", lambda k: OB[:, k, :], 4)
            drain_psum(pe, "w_out2")
            for t in range(4):
                m = slot()
                for hf in range(2):
                    hh = 2 * t + hf
                    if hh >= 4:
                        pe.wait_ge(freed["D"], BEFORE["w_out2"]["D"] + hh - 3)
                    half(m, hf, hh % 4, lambda k: merged2[:, k, :])
            norm_sum(4)
            pe.wait_ge(normed, 5)
            if stop < 6:
                return
            pe.wait_ge(got_router, 64)
            for tt in range(4):
                for k in range(KT):
                    mm = pe.matmul(ps[:, 7, tt * 36:tt * 36 + 36], hT[:, k, tt * P:tt * P + P], WR[:, k, :],
                                   start=(k == 0), stop=(k == KT - 1))
            mm.then_inc(routed, 1)
            pe.wait_ge(combined, 1)
            comb = rt_comb
            for g in range(8):
                if g >= 2:
                    pe.wait_ge(ct_ready, g - 1)
                for tt in range(4):
                    mm = pe.transpose(ps[0:4, 4 + g % 2, tt * P:tt * P + P], comb[:, tt, 4 * g:4 * g + 4], ident)
                mm.then_inc(ct_made, 1)
            pe.wait_ge(ct_ready, 8)
            drain_psum(pe, "moe")
            first = n[0]
            A0, D0 = BEFORE["moe"]["A"], BEFORE["moe"]["D"]

            def expert(s, e, e0, r, rnd):
                pe.wait_ge(cb_read, e + 1)
                w_row = CT[0:4, rnd, :] if isinstance(rnd, int) else CT[0:4, bass.ds(rnd, 1), :].rearrange("p a t -> p (a t)")
                for part, who, base in ((0, "A", A0), (1, "D", D0)):
                    m = first + s + part
                    pe.wait_ge(full[m % R], e0 + full_value(m))
                    pe.wait_ge(freed[who], e * 2 + base)
                    w = ring[:, m % R, :].rearrange("p (k c) -> p k c", c=256)
                    for f in range(2):
                        for k in range(KT):
                            mm = pe.matmul(ps[:, 2 * part + f, :], w[:, k, f * P:f * P + P], h_(k),
                                           start=(k == 0), stop=(k == KT - 1))
                        mm.then_inc(gu_done, 1)
                    if part == 0:
                        pe.matmul(ps[:, 7, :], PICK[0:4, r * P:r * P + P], w_row, start=True, stop=True).then_inc(cb_made, 1)

            def down(s, e, e0, par):
                m = first + s
                pe.wait_ge(full[m % R], e0 + full_value(m))
                pe.wait_ge(mhid, e * 2 + 2)
                w = ring[:, m % R, :].rearrange("p (k c) -> p k c", c=D)
                for mm_ in range(8):
                    pe.wait_ge(down_added, e * 8 + (1 if mm_ < 3 else mm_ - 1))
                    for k in range(2):
                        mm = pe.matmul(ps[:, 4 + mm_ % 3, :], w[:, k, mm_ * P:mm_ * P + P], MH[:, 2 * par + k, :],
                                       start=(k == 0), stop=(k == 1))
                    mm.then_inc(down_made, 1)

            def experts(lo, hi, e0=0, i=None):
                for e in range(lo, hi):
                    s = 3 * e - 1 if e else 0
                    ee = e if i is None else i * 4 + e
                    expert(s, ee, e0, e % 4, e // 4 if i is None else i + e // 4)
                    if e:
                        down(s + 2, ee + (-1) if i is not None else e - 1, e0, (e - 1) % 2)

            experts(0, 5)
            with pe.Fori(0, MOE_ROUNDS) as i:
                experts(5, 9, i * 48, i)
            experts(29, 32)
            down(95, 31, 0, 1)
            norm_sum(5)

        @block.scalar
        def _(act):
            lk = Link(act, act_link)
            act.wait_ge(got_const, 32)

            def norm_squares(k_norm, src):
                act.activation(hT, src, ACT.Square).then_inc(squared, 1)

            def norm_root(k_norm):
                act.wait_ge(summed, k_norm + 1)
                act.activation(RSTD, ps[:, 6, :], ACT.Sqrt, scale=1.0 / D, bias=EPSC).then_inc(rooted, 1)

            act.wait_ge(mod_ready, 1)
            act.wait_ge(got_x, 16)
            norm_squares(0, x_in)
            norm_root(0)
            if stop < 1:
                return

            act.wait_ge(got_lora, 32)
            for i, (dst, rows) in enumerate(((LOW, P), (GLO, P), (GLO2, 32))):
                act.wait_ge(half_done, 2 * FIRST["lora"] + (1, 2, 4)[i])
                act.activation(dst[0:rows], ps[0:rows, i, :], ACT.Copy if False else ACT.Identity,
                               scale=OMU[0:rows, 24 + i:25 + i], bias=ZERO[0:rows]).then_inc(scaled, 1)
            act.wait_ge(freed["D"], BEFORE["lora"]["D"] + 1)
            act.activation(LOW[0:64], LOW[0:64], ACT.Tanh).then_inc(act_link, 1)
            act.wait_ge(freed["D"], BEFORE["lora"]["D"] + 3)
            act.activation(GLO, GLO, ACT.Sigmoid).then_inc(act_link, 1)
            act.activation(GLO2[0:32], GLO2[0:32], ACT.Sigmoid).then_inc(act_link, 1)
            act.wait_ge(act_link, 3)
            act.activation(ZSINK, ZERO, ACT.Copy).then_inc(lora_ready, 1)

            np_ = len(PRODUCTS)

            def made_wait(q, name, s):
                act.wait_ge(made, 2 * np_ * q + 2 * PNAMES.index(name) + s + 1)

            def empty_half(q, name, s, dst):
                made_wait(q, name, s)
                act.activation(dst[0:64], ps[0:64, 4 + 2 * s, :], ACT.Copy).then_inc(emptA, 1)

            for q in range(4):
                for part in range(3):
                    for hf in range(2):
                        j = 2 * q + hf
                        hh = q * 6 + part * 2 + hf
                        act.wait_ge(half_done, 2 * FIRST["rkv"] + hh + 1)
                        if q and part == 0 and hf == 0:
                            act.wait_ge(made, 2 * np_ * q)
                            act.wait_ge(emptD, PER_QUAD["D"] * q)
                        act.activation(tmp[hf][part], ps[:, hh % 4, :], ACT.Identity,
                                       scale=OMU[:, part * 8 + j:part * 8 + j + 1], bias=ZERO).then_inc(scaled, 1)
                for s in range(2):
                    j = 2 * q + s
                    made_wait(q, "lora", s)
                    act.activation(tmp[s][3], ps[:, 4 + 2 * s, :], ACT.Sigmoid, bias=col("w0", j)).then_inc(act_link, 1)
                    act.wait_ge(act_link, 3 + 2 * q + s + 1)
                    act.activation(tmp[s][4], ps[:, 5 + 2 * s, :], ACT.Sigmoid, bias=col("a0", j)).then_inc(emptA, 1)
                for s in range(2):
                    made_wait(q, "ssq", s)
                    act.activation(tmp[s][10], ps[:, 4 + 2 * s, :], ACT.Sqrt, bias=ZERO).then_inc(emptA, 1)
                for s in range(2):
                    act.wait_ge(cum, 2 * q + s + 1)
                    t_ = tmp[s]
                    act.activation(t_[7], t_[5], ACT.Exp, scale=-KAPPA).then_inc(decay, 1)
                    act.activation(t_[8], t_[5], ACT.Exp, scale=KAPPA).then_inc(decay, 1)
                    act.activation(t_[6], t_[6], ACT.Exp, scale=-KAPPA).then_inc(decay, 1)
                for s in range(2):
                    act.wait_ge(chan, 6 * q + 5 + s) if s == 0 else act.wait_ge(chan, 6 * q + 6)
                    empty_half(q, "tv", s, tmp[s][1])
                for name, d in (("tat", 7), ("tbh", 9), ("tkh", 10)):
                    for s in range(2):
                        empty_half(q, name, s, tmp[s][d])
                for b in LEVELS:
                    for s in range(2):
                        empty_half(q, f"y{b}", s, tmp[s][4])
                for name, d in (("w1", 4), ("sav", 2), ("z", 5)):
                    for s in range(2):
                        empty_half(q, name, s, tmp[s][d])
                for s in range(2):
                    j = 2 * q + s
                    made_wait(q, "y0", s)
                    act.activation(Y0[0:64, j, :], ps[0:64, 4 + 2 * s, :], ACT.Copy).then_inc(emptA, 1)
                for s in range(2):
                    j = 2 * q + s
                    made_wait(q, "h", s)
                    act.activation(ST[0:64, :, j, :], chunks(ps[0:64, 4 + 2 * s, :]), ACT.Copy).then_inc(emptA, 1)
            if stop < 2:
                return

            def y_square(j):
                act.wait_ge(centred, j + 1)
                if j >= 2:
                    act.wait_ge(y_root, j - 1)
                act.activation(ytmp[j % 2][0], Y0[:, j, :], ACT.Square).then_inc(y_sq, 1)

            def y_roots(j):
                act.wait_ge(var_made, j + 1)
                if j >= 2:
                    act.wait_ge(y_final, j - 1)
                act.activation(ytmp[j % 2][1], ps[:, 2 + j % 2, :], ACT.Sqrt, scale=1.0 / 64, bias=GNC).then_inc(y_root, 1)

            for t in range(9):
                if t >= 1:
                    y_roots(t - 1)
                if t < 8:
                    y_square(t)

            def gates(phase, at):
                for g in range(4):
                    for hf in range(2):
                        i = 2 * g + hf
                        act.wait_ge(half_done, 2 * FIRST[phase] + 4 * g + hf + 1)
                        if i >= 2:
                            act.wait_ge(freed["D"], BEFORE[phase]["D"] + i - 1)
                        elif i == 0:
                            act.wait_ge(freed["D"], BEFORE[phase]["D"])
                        gb, bias = (gate, col("b_gate", at + i)) if at is not None else (gate2, ZERO)
                        act.activation(gb[:, i % 2, :], ps[:, i % 2, :], ACT.Sigmoid, bias=bias).then_inc(freed["A"], 1)

            if True:
                act.wait_ge(y_final, 8)
            gates("rw_out", 8)
            if stop < 3:
                return

            act.wait_ge(freed["D"], BEFORE["qk"]["D"])
            for i in range(12):
                act.wait_ge(half_done, 2 * FIRST["qk"] + 2 * i + 1)
                act.activation(QK[:, 2 * i, :], ps[:, 2 * i % 4, :], ACT.Copy).then_inc(freed["A"], 1)
            for i in range(6):
                act.wait_ge(half_done, 2 * FIRST["v"] + 2 * i + 1)
                act.activation(VT[:, 0:2, i * 256:i * 256 + 256], ps[:, 2 * i % 4, :].rearrange("p (a b) -> p a b", b=256),
                               ACT.Copy).then_inc(freed["A"], 1)

            turn_n = [0]

            def attend(u0, us, parts_of, prob, probT, OT):
                def exps(i):
                    u = u0 + i
                    act.wait_ge(peaked, u + 1)
                    n_ = parts_of(us[i], i)["tiles"] * P
                    act.activation(prob[u % 2][:, 0:n_], prob[u % 2][:, 0:n_], ACT.Exp, scale=parts_of(us[i], i)["scale"],
                                   bias=NM[:, u % 2:u % 2 + 1], accum_out=DEN[:, u % 2:u % 2 + 1]).then_inc(probbed, 1)

                def copies(i):
                    u = u0 + i
                    n_ = parts_of(us[i], i)["tiles"]
                    if u >= 1:
                        act.wait_ge(weighed, u)
                    for t_ in range(0, n_, 4):
                        g = turn_n[0]
                        turn_n[0] += 1
                        k = min(4, n_ - t_)
                        act.wait_ge(turned, g + 1)
                        act.activation(probT[:, t_ * P:(t_ + k) * P], ps[:, 4 + g % 2, 0:k * P], ACT.Copy).then_inc(turnedS, 1)

                def out_copy(i):
                    w = (u0 + i) // 8
                    act.wait_ge(oturned, w + 1)
                    qt = us[i][0]
                    act.activation(OT[:, :, qt * P:qt * P + P], ps[:, 3, :].rearrange("p (a b) -> p a b", b=P),
                                   ACT.Copy).then_inc(oready, 1)

                exps(0)
                for i in range(len(us)):
                    if i + 1 < len(us):
                        exps(i + 1)
                    copies(i)
                    if i % 8 == 0 and i:
                        out_copy(i - 1)
                out_copy(len(us) - 1)

            attend(0, units, parts1, PROB1[0], PROB1[1], OT1)
            gates("at_out", 0)
            if stop < 4:
                return

            act.wait_ge(freed["D"], BEFORE["up"]["D"])
            act.wait_ge(half_done, 2 * FIRST["up"])
            norm_squares(1, xT)
            norm_root(1)
            act.wait_ge(normed, 2)

            H0 = 2 * FIRST["up"]
            D0 = BEFORE["up"]["D"]

            def up_scale(jj, hb, cb):
                for g in range(2):
                    act.wait_ge(half_done, hb(2 * jj + g + 1))
                    if jj >= 2:
                        act.wait_ge(hidd, cb(jj - 1))
                    act.activation(cvt[jj % 2][g], ps[:, (2 * jj + g) % 4, :], ACT.Identity,
                                   scale=up_col(2, g, jj, cb), bias=up_col(3, g, jj, cb)).then_inc(convd, 1)

            def up_silu(jj, hb, cb, db):
                act.wait_ge(freed["D"], db(2 * jj + 1))
                act.activation(sil[:, jj % 2, :], cvt[jj % 2][0], ACT.Silu).then_inc(silud, 1)

            def up_col(tap, g, jj, cb):
                base = (COL_AT["conv_w"] + tap * 44 if tap < 3 else COL_AT["conv_b"]) + g * FT
                i = cb(jj)
                return cols[:, base + i:base + i + 1] if isinstance(i, int) else cols[:, bass.ds(i + base, 1)]

            ident_ = (lambda v: H0 + v), (lambda v: v), (lambda v: D0 + v)
            for jj in range(2):
                up_scale(jj, ident_[0], ident_[1])
                up_silu(jj, *ident_)
            with act.Fori(0, 5) as i:
                for jj in range(2, 2 + R):
                    f = (lambda v: i * 8 + (H0 + v)), (lambda v: i * 4 + v), (lambda v: i * 8 + (D0 + v))
                    up_scale(jj, f[0], f[1])
                    up_silu(jj, *f)
            act.wait_ge(freed["D"], BEFORE["ada2"]["D"])
            norm_squares(2, xT)
            norm_root(2)

            if stop < 5:
                return
            act.activation(C2S, col("c_2", 0, 8), ACT.Silu).then_inc(silu_c, 1)
            act.wait_ge(normed, 3)
            norm_squares(3, xT)
            norm_root(3)
            act.wait_ge(angled, 1)
            act.activation(ANG[:, 0:2, :], ANG[:, 0:2, :], ACT.Sin, bias=ZERO).then_inc(rotated, 1)

            def psum_out(phase, o, dst, src, v):
                act.wait_ge(half_done, 2 * FIRST[phase] + v)
                act.activation(dst, src, ACT.Copy).then_inc(freed["A"], 1)

            in2_value = lambda o: o + 1 if o < 4 else o + 2
            tok2 = lambda v: v.rearrange("p (a b) -> p a b", b=256)
            IN2 = [QL[:, 0, :], QL[:, 1, :], KV, KR, KRS] + [QB[:, j, :] for j in range(4)] + [KB[:, j, :] for j in range(4)]
            act.wait_ge(rotated, 1)
            for o in range(0, 13, 2):
                psum_out("in2", o, IN2[o], ps[:, o % 4, :], in2_value(o))
            for o in (14, 16):
                c, hf = divmod(o - 13, 2)
                psum_out("in2", o, VB[:, 2 * hf:2 * hf + 2, c * 256:c * 256 + 256], tok2(ps[:, o % 4, :]), in2_value(o))
            act.wait_ge(freed["D"], BEFORE["in2"]["D"] + 1)
            act.activation(LSQ[:, 0:2, :], QL, ACT.Square).then_inc(act_link, 1)
            act.activation(LSQ[:, 2, :], KV, ACT.Square).then_inc(lat_sq, 1)
            act.wait_ge(lat_sum, 1)
            act.activation(LRT[:, 0, :], ps[:, 6, :], ACT.Sqrt, scale=1.0 / 256, bias=EPSC).then_inc(lat_root, 1)
            act.activation(LRT[:, 1, :], ps[:, 7, :], ACT.Sqrt, scale=1.0 / 128, bias=EPSC).then_inc(lat_root, 1)
            for o in range(0, 16, 2):
                psum_out("lat2", o, QA[0:96, o // 2, :], ps[0:96, o % 4, :], o + 1)
            for o in range(16, 24, 2):
                psum_out("lat2", o, KA[0:64, o - 16, :], ps[0:64, o % 4, :], o + 1)
            for o in (24, 26):
                c, hf = divmod(o - 24, 2)
                psum_out("lat2", o, VA[:, 2 * hf:2 * hf + 2, c * 256:c * 256 + 256], tok2(ps[:, o % 4, :]), o + 1)
            attend(32, units, parts_mla, PROB2[0], PROB2[1], OA)
            attend(64, units, parts_band, PROB2[0], PROB2[1], OB)
            gates("mla_out", None)
            gates("band_out", None)
            act.wait_ge(freed["D"], BEFORE["moe"]["D"])
            act.wait_ge(half_done, 2 * FIRST["moe"])
            norm_squares(4, xT)
            norm_root(4)
            if stop < 6:
                return
            act.wait_ge(route_exp, 1)
            act.activation(rt_e, rt_e, ACT.Exp).then_inc(route_exp, 1)
            for g in range(8):
                act.wait_ge(ct_made, g + 1)
                act.activation(CT[0:4, g, :], ps[0:4, 4 + g % 2, :], ACT.Copy).then_inc(ct_ready, 1)
            act.activation(ZSINK, ZERO, ACT.Copy).then_inc(cb_read, 1)
            A0, D0 = BEFORE["moe"]["A"], BEFORE["moe"]["D"]

            def expert(e):
                if not (isinstance(e, int) and e == 0):
                    act.wait_ge(mhid, e * 2)
                for f in range(2):
                    act.wait_ge(gu_done, e * 4 + (f + 1))
                    act.activation(SG[:, f, :], ps[:, f, :], ACT.Silu).then_inc(freed["A"], 1)
                act.wait_ge(cb_made, e + 1)
                act.activation(CB[:, 0, :], ps[:, 7, :], ACT.Copy).then_inc(cb_read, 1)

            expert(0)
            with act.Fori(1, 32) as e:
                expert(e)
            act.wait_ge(down_added, 1 + 8 * 32)
            norm_squares(5, xT)
            norm_root(5)

        @block.gpsimd
        def _(pool):
            if stop < 1:
                return
            np_ = len(PRODUCTS)
            for q in range(4):
                for li, b in enumerate(LEVELS):
                    for s in range(2):
                        dst = tmp[s][6 if li % 2 == 0 else 8]
                        if li == 0 and s == 0:
                            pool.wait_ge(made, 2 * np_ * q + 2 * PNAMES.index("rkT") + 2)
                            pool.wait_ge(emptD, emptied(q, "rkT", 1, "D"))
                        if li >= 2:
                            pool.wait_ge(made, 2 * np_ * q + 2 * PNAMES.index(f"y{LEVELS[li - 2]}") + s + 1)
                        pool.tensor_tensor(chunks(dst), chunks(tmp[s][5]), rep(cst(f"level{b}"), NCH), ALU.mult).then_inc(maskp, 1)

            if stop < 5:
                return
            pool.wait_ge(half_done, 2 * FIRST["up"])
            pool.wait_ge(freed["D"], BEFORE["up"]["D"])
            pool.dma_start(BROW[0:8, 255:640], a["rel_reversed"][:, 0:385]).then_inc(bias_row, 16)
            pool.dma_start(CH, a["consts"][:, CONST_AT["chunked"][0]:CONST_AT["chunked"][0] + T]).then_inc(got_pos, 16)
            pool.dma_start(ANG[:, 3, :].bitcast(I32), a["positions"].partition_broadcast(P)).then_inc(got_pos, 16)
            pool.wait_ge(bias_row, 16)
            pool.tensor_copy(BROW[0:8, 0:255], BROW[0:8, 255:256].broadcast_to([8, 255])).then_inc(pool_link, 1)
            pool.wait_ge(pool_link, 1)
            pool.dma_start(a["bias_scratch"], BROW[0:8, :].unsqueeze(1).broadcast_to([8, P, 640])).then_inc(bias_out, 16)
            pool.wait_ge(bias_out, 16)
            pool.dma_start(BT, bass.AP(a["bias_scratch"].tensor, 127, [[639, P], [P * 640, 8], [1, T]])).then_inc(got_bias, 16)
            if stop < 6:
                return
            pool.wait_ge(half_done, 2 * FIRST["w_out2"])
            pool.wait_ge(freed["D"], BEFORE["w_out2"]["D"])
            pool.dma_start(WR[:, :, 0:4], a["w_rg_2"].rearrange("(k p) c -> p k c", p=P)).then_inc(got_router, 16)
            pool.dma_start(WR[:, :, 4:36], a["w_re_2"].rearrange("(k p) c -> p k c", p=P)).then_inc(got_router, 16)
            pool.dma_start(PICK[0:4], a["consts"][0:4, CONST_AT["pick"][0]:NCONST]).then_inc(got_router, 16)
            pool.dma_start(BRT, a["b_router"].partition_broadcast(P)).then_inc(got_router, 16)

        @block.vector
        def _(dve):
            lk = Link(dve, dve_link)
            tt, ts, stt = dve.tensor_tensor, dve.tensor_scalar, dve.scalar_tensor_tensor
            lk(dve.memset(EPSC, EPS))
            lk(dve.memset(GNC, GN_EPS))
            dve.memset(ZERO, 0.0).then_inc(dve_link, 1)
            lk.n += 1
            dve.wait_ge(dve_link, lk.n)
            dve.wait_ge(got_const, 32)
            lk.done(ts(OMU, col("mu", 0, 27), -1.0, 1.0, ALU.mult, ALU.add))
            ts(OKA, col("k_a", 0, 8), -1.0, 1.0, ALU.mult, ALU.add).then_inc(mod_ready, 1)

            def modulation(phase, bias):
                dve.wait_ge(half_done, 2 * FIRST[phase] + 48)
                lk.done(tt(mod[:], ps[:, 7, 0:48], bias, ALU.add))

            def gain(which, w):
                lk.done(ts(GAIN, mod[:, which * 24 + 8:which * 24 + 16], 1.0, None, ALU.add))
                lk.done(tt(GAIN, GAIN, w, ALU.mult))

            def norm_apply(k_norm, src, g, shift, dst):
                dve.wait_ge(rooted, k_norm + 1)
                lk.done(dve.reciprocal(RSTD, RSTD))
                lk.done(tt(dst, src, rep(RSTD, KT), ALU.mult))
                for k in range(KT):
                    if shift is None:
                        ins = ts(dst[:, k, :], dst[:, k, :], g[:, k:k + 1], None, ALU.mult)
                    else:
                        ins = ts(dst[:, k, :], dst[:, k, :], g[:, k:k + 1], shift[:, k:k + 1], ALU.mult, ALU.add)
                    if k == KT - 1:
                        ins.then_inc(normed, 1)

            modulation("ada1", col("b_ada", 0, 48))
            gain(0, col("norm1_w", 0, 8))
            ts(ONE, ZERO, 1.0, None, ALU.add).then_inc(freed["D"], 1)
            dve.wait_ge(got_x, 16)
            norm_apply(0, x_in, GAIN, mod[:, 0:8], hT)
            if stop < 1:
                return
            sc_n = 0

            def shift(dst, bank, mu, rows=P):
                nonlocal sc_n
                sc_n += 1
                dve.wait_ge(scaled, sc_n)
                stt(dst[0:rows, 1:T], ps[0:rows, bank, 0:T - 1], mu[0:rows], dst[0:rows, 1:T],
                    ALU.mult, ALU.add).then_inc(freed["D"], 1)

            for i, (dst, rows) in enumerate(((LOW, P), (GLO, P), (GLO2, 32))):
                shift(dst, i, col("mu", 24 + i), rows)

            np_ = len(PRODUCTS)

            def made_wait(q, name, s):
                dve.wait_ge(made, 2 * np_ * q + 2 * PNAMES.index(name) + s + 1)

            def bank_rows(s, e):
                return slice(e * 64, e * 64 + 64), 4 + 2 * s + e

            def empty_half(q, name, s, dst):
                made_wait(q, name, s)
                r, b = bank_rows(s, 1)
                dve.tensor_copy(dst[r], ps[r, b, :]).then_inc(emptD, 1)

            def empty_masked(q, name, s, dst, mask):
                made_wait(q, name, s)
                for e in range(2):
                    r, b = bank_rows(s, e)
                    ins = tt(chunks(dst[r]), chunks(ps[r, b, :]), rep(mask[r], NCH), ALU.mult)
                    if e == 0:
                        lk(ins)
                    else:
                        ins.then_inc(emptD, 1)

            def empty_added(q, name, s, dst, src, out3=None):
                made_wait(q, name, s)
                for e in range(2):
                    r, b = bank_rows(s, e)
                    ins = tt(dst[r], ps[r, b, :], src[r], ALU.add)
                    if e == 0:
                        lk(ins)
                    else:
                        ins.then_inc(emptD, 1)

            for q in range(4):
                for part in range(3):
                    for hf in range(2):
                        hh = q * 6 + part * 2 + hf
                        shift(tmp[hf][part], hh % 4, col("mu", part * 8 + 2 * q + hf))
                dve.wait_ge(freed["D"], BEFORE["rkv"]["D"] + 6 * q + 6)
                for s in range(2):
                    t_ = tmp[s]
                    lk.done(ts(t_[9], t_[1], col("k_k", 2 * q + s), None, ALU.mult))
                    tt(t_[10], t_[9], t_[9], ALU.mult).then_inc(chan, 1)
                for s in range(2):
                    t_ = tmp[s]
                    dve.wait_ge(emptA, emptied(q, "lora", s, "A"))
                    lk.done(dve.tensor_tensor_scan(t_[5], cst("restart"), t_[3], 0.0, ALU.mult, ALU.add))
                    tt(t_[6], t_[5], t_[3], ALU.subtract).then_inc(cum, 1)
                for s in range(2):
                    j = 2 * q + s
                    t_ = tmp[s]
                    dve.wait_ge(emptA, emptied(q, "ssq", s, "A"))
                    lk.done(ts(t_[10], t_[10], 1e-12, None, ALU.max))
                    lk.done(dve.reciprocal(t_[10], t_[10]))
                    lk.done(tt(t_[9], t_[9], t_[10], ALU.mult))
                    lk.done(ts(t_[10], t_[4], col("k_a", j), OKA[:, j:j + 1], ALU.mult, ALU.add))
                    lk.done(tt(t_[1], t_[1], t_[10], ALU.mult))
                    lk.done(stt(t_[10], t_[0], col("r_k", j), t_[1], ALU.mult, ALU.mult))
                    tt(t_[4], t_[4], t_[9], ALU.mult).then_inc(chan, 1)
                for s in range(2):
                    t_ = tmp[s]
                    dve.wait_ge(chan, 6 * q + 3 + s)
                    dve.wait_ge(decay, 6 * q + 3 * s + 3)
                    lk.done(stt(t_[6], t_[9], -1.0, t_[6], ALU.mult, ALU.mult))
                    lk.done(tt(t_[4], t_[4], t_[8], ALU.mult))
                    lk.done(tt(t_[8], t_[1], t_[8], ALU.mult))
                    lk.done(tt(t_[0], t_[0], t_[7], ALU.mult))
                    lk.done(dve.tensor_copy(PLS[s], chunks(t_[7])[:, :, C - 1]))
                    lk.done(tt(chunks(t_[5]), chunks(t_[4]), bc(PLS[s], C), ALU.mult))
                    tt(chunks(t_[3]), chunks(t_[8]), bc(PLS[s], C), ALU.mult).then_inc(chan, 1)
                for s in range(2):
                    made_wait(q, "bonus", s)
                    tt(BON[:, 2 * q + s, :], ps[:, 4 + 2 * s, :], tmp[s][2], ALU.mult).then_inc(emptD, 1)
                for name, d in (("tv", 1), ("tat", 7), ("tbh", 9), ("tkh", 10)):
                    for s in range(2):
                        empty_half(q, name, s, tmp[s][d])
                for name, d, mask in (("ab", 2, "pair1"), ("abT", 11, "upper"), ("akT", 11, "upper"),
                                      ("rbT", 12, "upto"), ("rkT", 13, "upto")):
                    for s in range(2):
                        t_ = tmp[s]
                        if name == "ab":
                            made_wait(q, name, s)
                            for e in range(2):
                                r, b = bank_rows(s, e)
                                lk.done(tt(chunks(t_[2][r]), chunks(ps[r, b, :]), rep(cst("pair1")[r], NCH), ALU.mult))
                            tt(chunks(t_[2]), chunks(t_[2]), rep(eye64, NCH), ALU.add).then_inc(emptD, 1)
                        elif name == "abT":
                            made_wait(q, name, s)
                            for e in range(2):
                                r, b = bank_rows(s, e)
                                lk.done(tt(chunks(t_[5][r]), chunks(ps[r, b, :]), rep(cst("upper")[r], NCH), ALU.mult))
                            lk.done(tt(chunks(t_[3]), chunks(t_[5]), rep(cst("pair1T"), NCH), ALU.mult))
                            tt(chunks(t_[3]), chunks(t_[3]), rep(eye64, NCH), ALU.add).then_inc(emptD, 1)
                        else:
                            empty_masked(q, name, s, t_[d], cst(mask))
                for b in LEVELS:
                    for s in range(2):
                        empty_half(q, f"y{b}", s, tmp[s][4])
                    if b != LEVELS[-1]:
                        for s in range(2):
                            empty_added(q, f"x{b}", s, tmp[s][2], tmp[s][2])
                    for s in range(2):
                        empty_added(q, f"xT{b}", s, tmp[s][3], tmp[s][3])
                for name, d in (("w1", 4), ("sav", 2), ("z", 5)):
                    for s in range(2):
                        empty_half(q, name, s, tmp[s][d])
                for s in range(2):
                    empty_added(q, "r", s, RT[:, 2 * q + s, :], tmp[s][0])
                for s in range(2):
                    empty_half(q, "y0", s, Y0[:, 2 * q + s, :])
                for s in range(2):
                    j = 2 * q + s
                    lk.done(tt(GT[:, j], rep(eye64, NCH), bc(PLS[s], C), ALU.mult))
                    gt = GT[:, j].rearrange("p c k -> p (c k)")
                    empty_added(q, "g", s, gt, gt)
                for s in range(2):
                    made_wait(q, "h", s)
                    r, b = bank_rows(s, 1)
                    dve.tensor_copy(ST[r, :, 2 * q + s, :], chunks(ps[r, b, :])).then_inc(emptD, 1)
            if stop < 2:
                return

            dve.wait_ge(emptA, 4 * PER_QUAD["A"])
            dve.wait_ge(emptD, 4 * PER_QUAD["D"])
            for c in range(1, NCH - 1):
                dve.wait_ge(stepped, c)
                for e in range(2):
                    r = slice(e * 64, e * 64 + 64)
                    v = ST[r, c].rearrange("p j k -> p (j k)")
                    ins = tt(v, ps[r, 4 + 2 * (c % 2) + e, :], v, ALU.add)
                    if e == 0:
                        lk(ins)
                    else:
                        ins.then_inc(state_ready, 1)

            def y_add(j):
                dve.wait_ge(y_made, j + 1)
                for e in range(2):
                    r = slice(e * 64, e * 64 + 64)
                    ins = tt(Y0[r, j, C:T], ps[r, 4 + 2 * (j % 2) + e, C:T], Y0[r, j, C:T], ALU.add)
                    if e == 0:
                        lk.done(ins)
                    else:
                        ins.then_inc(y_added, 1)

            def y_centre(j):
                dve.wait_ge(mean_made, j + 1)
                stt(Y0[:, j, :], ps[:, j % 2, :], -1.0 / 64, Y0[:, j, :], ALU.mult, ALU.add).then_inc(centred, 1)

            def y_finish(j):
                dve.wait_ge(y_root, j + 1)
                rs = ytmp[j % 2][1]
                lk.done(dve.reciprocal(rs, rs))
                y = Y0[:, j, :]
                lk.done(tt(y, y, rs, ALU.mult))
                lk.done(ts(y, y, col("lnx_w", j), col("lnx_b", j), ALU.mult, ALU.add))
                lk.done(tt(y, y, BON[:, j, :], ALU.add))
                dve.wait_ge(g_made, j + 1)
                tt(y, ps[:, 4 + 2 * (j % 2), :], y, ALU.mult).then_inc(y_final, 1)

            for t in range(10):
                if 0 <= t - 2 < 8:
                    y_finish(t - 2)
                if t < 8:
                    y_add(t)
                if 0 <= t - 1 < 8:
                    y_centre(t - 1)

            def gated(phase, first, gate, merged):
                for i in range(8):
                    g, hf = divmod(i, 2)
                    dve.wait_ge(half_done, 2 * FIRST[phase] + 4 * g + 2 + hf + 1)
                    dve.wait_ge(freed["A"], BEFORE[phase]["A"] + i + 1)
                    if first:
                        tt(merged[:, i, :], ps[:, 2 + i % 2, :], gate[:, i % 2, :], ALU.mult).then_inc(freed["D"], 1)
                    else:
                        lk.done(tt(gate[:, i % 2, :], ps[:, 2 + i % 2, :], gate[:, i % 2, :], ALU.mult))
                        tt(merged[:, i, :], merged[:, i, :], gate[:, i % 2, :], ALU.add).then_inc(freed["D"], 1)

            gated("rw_out", True, gate, merged)
            if stop < 3:
                return
            dve.wait_ge(freed["A"], BEFORE["qk"]["A"])
            for i in range(12):
                dve.wait_ge(half_done, 2 * FIRST["qk"] + 2 * i + 2)
                dve.tensor_copy(QK[:, 2 * i + 1, :], ps[:, (2 * i + 1) % 4, :]).then_inc(freed["D"], 1)
            for i in range(6):
                dve.wait_ge(half_done, 2 * FIRST["v"] + 2 * i + 2)
                dve.tensor_copy(VT[:, 2:4, i * 256:i * 256 + 256],
                                ps[:, (2 * i + 1) % 4, :].rearrange("p (a b) -> p a b", b=256)).then_inc(freed["D"], 1)

            def attend(u0, us, parts_of, prob, otok):
                def peaks(i):
                    u = u0 + i
                    pt = parts_of(us[i], i)
                    dve.wait_ge(scored, u + 1)
                    if u >= 2:
                        dve.wait_ge(turned, TURNED[u - 2])
                    o = 0
                    for g, (_, _, bk, n_) in enumerate(pt["scores"]):
                        ins = dve.tensor_tensor_reduce(out=prob[u % 2][:, o:o + n_], in0=ps[:, bk, 0:n_], in1=pt["masks"][g],
                                                       scale=1.0, scalar=NEG, op0=ALU.add, op1=ALU.max,
                                                       accum_out=PK[:, u % 2, g:g + 1])
                        o += n_
                        if g == len(pt["scores"]) - 1:
                            ins.then_inc(masked, 1)
                        else:
                            lk(ins)
                    dve.wait_ge(masked, u + 1)
                    if len(pt["scores"]) > 1:
                        dve.wait_ge(dve_link, lk.n)
                    lk.done(dve.tensor_reduce(PK[:, u % 2, 3:4], PK[:, u % 2, 0:len(pt["scores"])], AX.X, ALU.max))
                    ts(NM[:, u % 2:u % 2 + 1], PK[:, u % 2, 3:4], -pt["scale"], None, ALU.mult).then_inc(peaked, 1)

                def outs(i):
                    u = u0 + i
                    w = u // 8
                    pt = parts_of(us[i], i)
                    dve.wait_ge(probbed, u + 1)
                    lk.done(dve.reciprocal(RD[:, u % 2:u % 2 + 1], DEN[:, u % 2:u % 2 + 1]))
                    dve.wait_ge(weighed, u + 1)
                    if i % 8 == 0 and w >= 2:
                        dve.wait_ge(oturned, w - 1)
                    ts(otok[w % 2][:, pt["out"]], ps[:, 6 + u % 2, 0:64], RD[:, u % 2:u % 2 + 1], None, ALU.mult).then_inc(outed, 1)

                peaks(0)
                for i in range(len(us)):
                    if i + 1 < len(us):
                        peaks(i + 1)
                    outs(i)

            dve.wait_ge(got_masks, 16)
            attend(0, units, parts1, PROB1[0], PROB1[2])
            gated("at_out", False, gate, merged)
            if stop < 4:
                return

            dve.wait_ge(got_x1, 16)

            def residual(phase, gcol, wait_to=None):
                for i in range(8):
                    if phase == "down":
                        dve.wait_ge(half_done, 2 * FIRST[phase] + 6 * (i // 2) + 4 + i % 2 + 1)
                    else:
                        dve.wait_ge(half_done, 2 * FIRST[phase] + i + 1)
                    stt(xT[:, i, :], ps[:, i % 4, :], mod[:, gcol + i:gcol + i + 1], xT[:, i, :],
                        ALU.mult, ALU.add).then_inc(freed["D"], 1)

            residual("w_o", 16)
            gain(1, col("norm2_w", 0, 8))
            norm_apply(1, xT, GAIN, mod[:, 24:32], hT)

            D0, H0 = BEFORE["up"]["D"], 2 * FIRST["up"]

            def up_slot(jj, cb, lbase):
                for g in range(2):
                    dst, bank = cvt[jj % 2][g], (2 * jj + g) % 4
                    dve.wait_ge(convd, 2 * cb(jj) + (g + 1) if isinstance(cb(jj), int) else cb(jj) * 2 + (g + 1))
                    stt(dst[:, 1:T], ps[:, bank, 0:T - 1], up_col(1, g, jj, cb), dst[:, 1:T], ALU.mult, ALU.add).then_inc(dve_link, 1)
                    dve.wait_ge(dve_link, lbase(g + 1))
                    stt(dst[:, 2:T], ps[:, bank, 0:T - 2], up_col(0, g, jj, cb), dst[:, 2:T], ALU.mult, ALU.add).then_inc(freed["D"], 1)
                dve.wait_ge(silud, cb(jj) + 1)
                dve.wait_ge(freed["D"], (cb(jj) * 2) + (D0 + 2))
                i = cb(jj)
                h_out = hid[:, i, :] if isinstance(i, int) else hid[:, bass.ds(i, 1), :].rearrange("p a t -> p (a t)")
                tt(h_out, sil[:, jj % 2, :], cvt[jj % 2][1], ALU.mult).then_inc(hidd, 1)

            def up_col(tap, g, jj, cb):
                base = COL_AT["conv_w"] + tap * 44 + g * FT
                i = cb(jj)
                return cols[:, base + i:base + i + 1] if isinstance(i, int) else cols[:, bass.ds(i + base, 1)]

            l0 = lk.n
            for jj in range(2):
                up_slot(jj, lambda v: v, lambda v: l0 + 2 * jj + v)
            with dve.Fori(0, 5) as i:
                for jj in range(2, 2 + R):
                    up_slot(jj, lambda v: i * 4 + v, lambda v: i * 8 + (l0 + 2 * jj + v))
            lk.n = l0 + 44
            residual("down", 40)
            norm_apply(2, xT, col("norm_f_w", 0, 8), None, xT)

            if stop < 5:
                return
            modulation("ada2", col("b_ada_2", 0, 48))
            gain(0, col("g_mix_2", 0, 8))
            ts(ONE, ZERO, 1.0, None, ALU.add).then_inc(freed["D"], 1)
            norm_apply(3, xT, GAIN, mod[:, 0:8], hT)
            dve.wait_ge(got_pos, 32)
            ROUND = 12582912.0
            C1 = 6.28125
            C2 = float(np.float32(int((2 * np.pi - C1) * 2 ** 22) / 2 ** 22))
            C3 = float(2 * np.pi - C1 - C2)
            PI_ = float(np.nextafter(np.float32(np.pi), np.float32(0)))
            lk.done(dve.tensor_copy(ANG[:, 2, :], ANG[:, 3, :].bitcast(I32)))
            lk.done(ts(ANG[:, 2, :], ANG[:, 2, :], cst("freq"), None, ALU.mult))
            for i_, quarter in enumerate((0.0, 0.25)):
                o_, tr = ANG[:, i_, :], ANG[:, 3, :]
                lk.done(ts(tr, ANG[:, 2, :], 1.0 / (2 * np.pi), quarter, ALU.mult, ALU.add))
                lk.done(ts(tr, tr, ROUND, -ROUND, ALU.add, ALU.add))
                lk.done(stt(o_, tr, -C1, ANG[:, 2, :], ALU.mult, ALU.add))
                lk.done(stt(o_, tr, -C2, o_, ALU.mult, ALU.add))
                lk.done(stt(o_, tr, -C3, o_, ALU.mult, ALU.add))
                lk.done(ts(o_, o_, quarter * 2 * np.pi, PI_, ALU.add, ALU.min))
                ins = ts(o_, o_, -PI_, None, ALU.max)
                if i_ == 0:
                    lk.done(ins)
                else:
                    ins.then_inc(angled, 1)
            dve.wait_ge(rotated, 1)
            lk.done(ts(SIN, ANG[:, 0, :], cst("rotsign"), None, ALU.mult))
            lk.done(dve.tensor_copy(COS, ANG[:, 1, :]))
            dve.wait_ge(got_bias, 16)
            for h in range(8):
                lk.done(stt(BT[:, h, :], BT[:, h, :], 8.0, CH, ALU.mult, ALU.add))

            in2_value = lambda o: o + 1 if o < 4 else o + 2
            tok2 = lambda v: v.rearrange("p (a b) -> p a b", b=256)

            def psum_out(phase, dst, src, v):
                dve.wait_ge(half_done, 2 * FIRST[phase] + v)
                dve.tensor_copy(dst, src).then_inc(freed["D"], 1)

            IN2 = [QL[:, 0, :], QL[:, 1, :], KV, KR, KRS] + [QB[:, j, :] for j in range(4)] + [KB[:, j, :] for j in range(4)]
            for o in range(1, 13, 2):
                psum_out("in2", IN2[o], ps[:, o % 4, :], in2_value(o))
            for o in (13, 15):
                c, hf = divmod(o - 13, 2)
                psum_out("in2", VB[:, 2 * hf:2 * hf + 2, c * 256:c * 256 + 256], tok2(ps[:, o % 4, :]), in2_value(o))
            dve.wait_ge(lat_root, 2)
            lk.done(dve.reciprocal(LRT, LRT))
            lk.done(stt(QL[:, 0, :], QL[:, 0, :], col("g_q_2", 0), LRT[:, 0, :], ALU.mult, ALU.mult))
            lk.done(stt(QL[:, 1, :], QL[:, 1, :], col("g_q_2", 1), LRT[:, 0, :], ALU.mult, ALU.mult))
            stt(KV, KV, col("g_kv_2"), LRT[:, 1, :], ALU.mult, ALU.mult).then_inc(lat_ready, 1)
            r = slice(64, 96)
            dve.wait_ge(freed["A"], BEFORE["in2"]["A"] + 3)
            dve.wait_ge(freed["D"], BEFORE["in2"]["D"] + 2)
            lk.done(tt(KR[r], KR[r], COS[r], ALU.mult))
            lk.done(tt(KRS[r], KRS[r], SIN[r], ALU.mult))
            lk.done(tt(KR[r], KR[r], KRS[r], ALU.add))
            lk.done(dve.tensor_copy(KA[r], rep(KR[r], 8)))
            for h in range(8):
                dve.wait_ge(half_done, 2 * FIRST["lat2"] + 2 * h + 2)
                tt(ROT[r, h % 2, :], ps[r, (2 * h + 1) % 4, :], SIN[r], ALU.mult).then_inc(freed["D"], 1)
                dve.wait_ge(freed["A"], BEFORE["lat2"]["A"] + h + 1)
                dve.wait_ge(freed["D"], BEFORE["lat2"]["D"] + h + 1)
                lk.done(tt(QA[r, h, :], QA[r, h, :], COS[r], ALU.mult))
                lk.done(tt(QA[r, h, :], QA[r, h, :], ROT[r, h % 2, :], ALU.add))
            for o in range(17, 24, 2):
                psum_out("lat2", KA[0:64, o - 16, :], ps[0:64, o % 4, :], o + 1)
            for o in (25, 27):
                c, hf = divmod(o - 24, 2)
                psum_out("lat2", VA[:, 2 * hf:2 * hf + 2, c * 256:c * 256 + 256], tok2(ps[:, o % 4, :]), o + 1)
            ts(ONE, ZERO, 1.0, None, ALU.add).then_inc(band_ready, 1)
            attend(32, units, parts_mla, PROB2[0], PROB2[2])
            attend(64, units, parts_band, PROB2[0], PROB2[2])
            gated("mla_out", True, gate2, merged2)
            gated("band_out", False, gate2, merged2)
            residual("w_out2", 16)
            gain(1, col("g_ffn_2", 0, 8))
            norm_apply(4, xT, GAIN, mod[:, 24:32], hT)
            if stop < 6:
                return
            dve.wait_ge(routed, 1)
            t4 = lambda v, k: v[:, 0:4 * k].rearrange("p (t k) -> p t k", k=k)
            lk.done(tt(RL, ps[:, 7, 0:144].rearrange("p (t c) -> p t c", c=36), rep(BRT, 4), ALU.add))
            LG, LE = RL[:, :, 0:4], RL[:, :, 4:36]
            red = lambda o_, i_, op: lk.done(dve.tensor_reduce(o_, i_, AX.X, op))
            rank = lambda k: cst("rank")[:, 0:k].unsqueeze(1).broadcast_to([P, 4, k])
            GM, M1, M2, MX, GS = [rt_[0][:, 4 * i:4 * i + 4] for i in range(5)]

            def first_max(dst, scratch, x, mx, k):
                lk.done(tt(scratch, x, bc(mx, k), ALU.is_equal))
                lk.done(tt(scratch, scratch, rank(k), ALU.mult))
                red(MX, scratch, ALU.max)
                lk.done(tt(dst, scratch, bc(MX, k), ALU.is_equal))

            red(GM, LG, ALU.max)
            OG, SCR4, SCR8, O1, O2, E2 = t4(rt_[1], 4), t4(rt_[2], 4), t4(rt_[3], 8), t4(rt_[4], 8), t4(rt_[5], 8), t4(rt_[6], 8)
            first_max(OG, SCR4, LG, GM, 4)
            ES = t4(rt_[7], 8)
            WIDE = rt_[8][:, 0:128].rearrange("p (t g e) -> p t g e", g=4, e=8)
            for tt_ in range(4):
                lk.done(tt(WIDE[:, tt_], LE[:, tt_].rearrange("p (g e) -> p g e", e=8), bc(OG[:, tt_], 8), ALU.mult))
            for tt_ in range(4):
                red(ES[:, tt_], WIDE[:, tt_].rearrange("p g e -> p e g"), ALU.add)
            red(M1, ES, ALU.max)
            first_max(O1, SCR8, ES, M1, 8)
            lk.done(stt(E2, O1, NEG, ES, ALU.mult, ALU.add))
            red(M2, E2, ALU.max)
            first_max(O2, SCR8, E2, M2, 8)
            ex = rt_e.rearrange("p (t k) -> p t k", k=5)
            lk.done(tt(ex[:, :, 0:4], LG, bc(GM, 4), ALU.subtract))
            tt(ex[:, :, 4], M2, M1, ALU.subtract).then_inc(route_exp, 1)
            dve.wait_ge(route_exp, 2)
            red(GS, ex[:, :, 0:4], ALU.add)
            W1, W2 = rt_[9][:, 0:4], rt_[9][:, 4:8]
            lk.done(ts(W1, ex[:, :, 4], 1.0, None, ALU.add))
            lk.done(tt(W1, W1, GS, ALU.mult))
            lk.done(dve.reciprocal(W1, W1))
            lk.done(tt(W2, W1, ex[:, :, 4], ALU.mult))
            lk.done(tt(O1, O1, bc(W1, 8), ALU.mult))
            lk.done(tt(O2, O2, bc(W2, 8), ALU.mult))
            lk.done(tt(O1, O1, O2, ALU.add))
            for tt_ in range(4):
                ins = tt(rt_comb[:, tt_].rearrange("p (g e) -> p g e", e=8), bc(OG[:, tt_], 8), rep(O1[:, tt_], 4), ALU.mult)
                if tt_ < 3:
                    lk.done(ins)
                else:
                    ins.then_inc(combined, 1)
            ts(ONE, ZERO, 1.0, None, ALU.add).then_inc(down_added, 1)

            def hidden(e, par, l_):
                for f in range(2):
                    dve.wait_ge(gu_done, e * 4 + (f + 3))
                    dve.wait_ge(freed["A"], e * 2 + (BEFORE["moe"]["A"] + f + 1))
                    if not (isinstance(e, int) and e < 2):
                        dve.wait_ge(down_made, (e * 8) - 8)
                    tt(MH[:, 2 * par + f, :], ps[:, 2 + f, :], SG[:, f, :], ALU.mult).then_inc(freed["D"], 1)
                for f in range(2):
                    dve.wait_ge(freed["D"], e * 2 + (BEFORE["moe"]["D"] + f + 1))
                    dve.wait_ge(cb_read, e + 2)
                    tt(MH[:, 2 * par + f, :], MH[:, 2 * par + f, :], CB[:, 0, :], ALU.mult).then_inc(mhid, 1)

            def add_down(e):
                for m_ in range(8):
                    dve.wait_ge(down_made, e * 8 + (m_ + 1))
                    stt(xT[:, m_, :], ps[:, 4 + m_ % 3, :], mod[:, 40 + m_:41 + m_], xT[:, m_, :], ALU.mult, ALU.add).then_inc(down_added, 1)

            for e in range(3):
                hidden(e, e % 2, 0)
                if e:
                    add_down(e - 1)
            with dve.Fori(0, 14) as i:
                for e in (3, 4):
                    ee = i * 2 + e
                    hidden(ee, e % 2, 0)
                    add_down(i * 2 + (e - 1))
            hidden(31, 1, 0)
            add_down(30)
            add_down(31)
            norm_apply(5, xT, col("g_final_2", 0, 8), None, hT)


def kernel(**inputs):
    import numpy as _np
    import concourse.bacc as _bacc
    from concourse import mybir as _mybir
    from concourse.bass_utils import run_bass_kernel_spmd as _run

    arrays = layout({k: _np.asarray(v) for k, v in inputs.items()})
    nc = _bacc.Bacc("TRN2", target_bir_lowering=False, num_devices=1)
    aps = {}
    for name, v in arrays.items():
        aps[name] = nc.dram_tensor(f"in_{name}", v.shape, _mybir.dt.from_np(v.dtype), kind="ExternalInput").ap()
    aps["out"] = nc.dram_tensor("out_0", (D, T), F32, kind="ExternalOutput").ap()
    aps["bias_scratch"] = nc.dram_tensor("bias_scratch", (8, P, 640), F32, kind="Internal").ap()
    build(nc, aps)
    r = _run(nc, [{f"in_{k}": v for k, v in arrays.items()}], core_ids=[0])
    return _np.ascontiguousarray(r.results[0]["out_0"].T)[None]


def layout(x):
    def columns(v):
        v = v.reshape(-1)
        pad = -v.size % P
        return np.concatenate([v, np.zeros(pad, v.dtype)]).reshape(-1, P).T if pad else v.reshape(-1, P).T

    parts = []
    for name, n in COLS:
        key = "mu_shift" if name == "mu" else name
        parts.append(columns(x[key]))
        assert parts[-1].shape[1] == n, name
    arrays = {"cols": np.ascontiguousarray(np.concatenate(parts, axis=1)), "consts": CONSTS,
              "x": np.ascontiguousarray(x["x"][0].T),
              "positions": np.ascontiguousarray(x["positions_2"]),
              "rel_reversed": np.ascontiguousarray(x["rel_bias_2"][0][:, ::-1])}
    swap = np.r_[0:64, 80:96, 64:80]
    uq = x["w_uq_2"][0].reshape(256, 8, 96)
    arrays["w_uq"] = np.zeros((256, 8, 2, P), uq.dtype)
    arrays["w_uq"][:, :, 0, :96] = uq
    arrays["w_uq"][:, :, 1, :96] = uq[:, :, swap]
    arrays["w_uq"] = arrays["w_uq"].reshape(256, 2048)
    kvr = np.zeros((D, 3, P), uq.dtype)
    kvr[:, 0] = x["w_in_2"][0][:, 256:384]
    kvr[:, 1, 64:96] = x["w_in_2"][0][:, 384:416]
    kvr[:, 2, 64:96] = x["w_in_2"][0][:, np.r_[400:416, 384:400]]
    arrays["w_kvr"] = kvr.reshape(D, 384)
    for name in ("w_ada", "w_in", "w2", "a2", "g2", "w_att_out", "w_rwkv_out", "w_o", "w_up", "w_down", "w_ada_2",
                 "w_in_2", "w_uk_2", "w_uv_2", "w_oa_2", "w_ob_2", "w_out_2", "w_rg_2", "w_re_2", "w_gate_2",
                 "w_up_2", "w_down_2"):
        arrays[name] = np.ascontiguousarray(x[name][0])
    arrays["b_router"] = np.ascontiguousarray(np.concatenate([x["b_rg_2"], x["b_re_2"]], axis=1))
    return arrays
```

```python
from contextlib import ExitStack

import numpy as np
import concourse.bass as bass
from concourse import mybir

F32 = mybir.dt.float32
I32 = mybir.dt.int32
ACT = mybir.ActivationFunctionType
ALU = mybir.AluOpType
AX = mybir.AxisListType

P = 128
T = 512
D = 1024
KT = D // P
R = 4
SLOT = 2048
EPS = 1e-6
GN_EPS = 64e-5
KAPPA = float(np.exp(-0.5))
C = 64
NCH = T // C
LEVELS = (2, 4, 8, 16, 32)
NEG = -1e30
SLOTS = 64
FF = 2816
FT = FF // P

COLS = [("b_ada", 48), ("norm1_w", 8), ("b_gate", 16), ("mu", 27), ("w0", 8), ("a0", 8), ("k_k", 8), ("k_a", 8),
        ("r_k", 8), ("lnx_w", 8), ("lnx_b", 8), ("norm2_w", 8), ("conv_w", 132), ("conv_b", 44), ("norm_f_w", 8),
        ("c", 8), ("c_2", 8), ("b_ada_2", 48), ("g_mix_2", 8), ("g_q_2", 2), ("g_kv_2", 1), ("g_ffn_2", 8),
        ("g_final_2", 8)]
COL_AT, NCOL = {}, 0
for _name, _n in COLS:
    COL_AT[_name] = NCOL
    NCOL += _n


def shape_constants():
    p = np.arange(P)[:, None]
    parts = []
    at = {}

    def add(name, a):
        at[name] = (sum(x.shape[1] for x in parts), a.shape[1])
        parts.append(np.ascontiguousarray(a, dtype=np.float32))

    add("ident", (p == np.arange(P)[None, :]))
    add("ones", np.ones((P, P)))
    add("headones", (p // 64 == np.arange(P)[None, :] // 64))
    q, s = p % 64, np.arange(64)[None, :]
    add("eye64", q == s)
    add("upper", q < s)
    add("upto", q <= s)
    add("pair1", (q // 2 == s // 2) & (s < q))
    add("pair1T", (q // 2 == s // 2) & (q < s))
    for b in LEVELS:
        add(f"level{b}", (q // (2 * b) == s // (2 * b)) & (q // b % 2 == 0) & (s // b % 2 == 1))
    add("restart", np.broadcast_to((np.arange(T) % C != 0)[None, :], (P, T)))
    inv = (10000.0 ** (-np.arange(16, dtype=np.float32) / np.float32(16))).astype(np.float32)
    add("freq", inv[np.arange(P) % 16][:, None])
    add("rotsign", np.where(p % 32 < 16, -1.0, 1.0))
    add("rank", np.broadcast_to(8.0 - np.arange(8)[None, :], (P, 8)))
    w = np.arange(256)[None, :]
    add("near", np.where((w >= p) & (w <= p + 128), 0.0, NEG))
    w = np.arange(T)[None, :]
    back = p - w + 384
    add("every4", np.where((back >= 0) & (back % 4 == 0), 0.0, NEG))
    add("every16", np.where((back >= 0) & (back % 16 == 0), 0.0, NEG))
    add("chunked", np.where(p // 64 >= w // 64 - 6, 0.0, NEG))
    add("before", p < np.arange(P)[None, :])
    add("slots", np.broadcast_to(np.arange(SLOTS)[None, :], (P, SLOTS)))
    add("rows", np.broadcast_to(SLOTS * np.arange(32)[None, :], (P, 32)))
    return np.concatenate(parts, axis=1), at


CONSTS, CONST_AT = shape_constants()
NCONST = CONSTS.shape[1]


PHASES = [("ada1", 24), ("lora", 2), ("rkv", 12), ("rw_out", 8), ("qk", 12), ("v", 6), ("at_out", 8), ("w_o", 4),
          ("up", 22), ("down", 12), ("ada2", 24), ("in2", 9), ("lat2", 14), ("mla_out", 8), ("band_out", 8),
          ("w_out2", 4), ("moe", 96)]
FIRST, _n = {}, 0
for _name, _k in PHASES:
    FIRST[_name] = _n
    _n += _k

PRODUCTS = [("lora", "A"), ("ssq", "A"), ("bonus", "D"), ("tv", "AD"), ("tat", "AD"), ("tbh", "AD"), ("tkh", "AD"),
            ("ab", "D"), ("abT", "D"), ("akT", "D"), ("rbT", "D"), ("rkT", "D")]
for _b in LEVELS:
    PRODUCTS += [(f"y{_b}", "AD")] + ([(f"x{_b}", "D")] if _b != LEVELS[-1] else []) + [(f"xT{_b}", "D")]
PRODUCTS += [("w1", "AD"), ("sav", "AD"), ("z", "AD"), ("r", "D"), ("y0", "AD"), ("g", "D"), ("h", "AD")]
PNAMES = [n for n, _ in PRODUCTS]
PER_QUAD = {e: 2 * sum(e in who for _, who in PRODUCTS) for e in "AD"}


def emptied(quad, product, sub, engine):
    i = PNAMES.index(product)
    n = 2 * sum(engine in who for _, who in PRODUCTS[:i])
    if engine in PRODUCTS[i][1]:
        n += sub + 1
    else:
        n += 0
    return quad * PER_QUAD[engine] + n


class Link:

    def __init__(self, eng, sem):
        self.eng, self.sem, self.n, self.off = eng, sem, 0, 0

    def __call__(self, ins):
        ins.then_inc(self.sem, 1)
        self.n += 1
        return self.n + self.off

    def done(self, ins):
        self.eng.wait_ge(self.sem, self(ins))


def build(nc, a, stop=99):
    with ExitStack() as ctx:
        def sb(name, shape, dt=F32):
            return ctx.enter_context(nc.sbuf_tensor(name, shape, dt))

        def sem(name):
            return ctx.enter_context(nc.semaphore(name))

        ring = sb("ring", [P, R, SLOT])
        const = sb("const", [P, CONST_AT["near"][0]])
        cols = sb("cols", [P, NCOL])
        mod = sb("mod", [P, 48])[:, :]
        small = sb("small", [P, 160])
        hT = sb("hT", [P, KT, T])[:, :, :]
        arena = sb("arena", [P, 37888])
        ps = ctx.enter_context(nc.psum_tensor("ps", [P, 8, 512], F32))

        def area(at, *dims):
            n = int(np.prod(dims))
            v = arena[:, at:at + n]
            if len(dims) == 1:
                return v
            if len(dims) == 2:
                return v.rearrange("p (a b) -> p a b", b=dims[1])
            return v.rearrange("p (a b c) -> p a b c", b=dims[1], c=dims[2])

        def cst(name):
            o, n = CONST_AT[name]
            return const[:, o:o + n]

        def col(name, i=0, n=1):
            return cols[:, COL_AT[name] + i:COL_AT[name] + i + n]

        ident, ones, headones, eye64 = cst("ident"), cst("ones"), cst("headones"), cst("eye64")

        x_in = area(20480, KT, T)
        RT, Y0 = area(0, 8, T), area(4096, 8, T)
        GT = area(8192, 8, NCH, C)
        ST = area(12288, NCH, 8, C)
        BON = area(16384, 8, T)
        tmp = [[area(20480 + (s * 14 + i) * T, T) for i in range(14)] for s in range(2)]
        LOW = area(34816, T)
        GLO, GLO2 = area(35328, T), area(35840, T)
        W2A2 = area(36352, D)
        G2 = area(20480, 2, D)
        ytmp = [[area(22528 + (s * 3 + i) * T, T) for i in range(3)] for s in range(2)]
        merged = area(30720, KT, T)
        gate = area(28416, 2, T)
        QK = area(0, 24, T)
        VT = area(12288, 4, 1536)
        masks = area(18432, 1792)
        near, every4, every16 = masks[:, 0:256], masks[:, 256:768], masks[:, 768:1280]
        xT = area(0, KT, T)
        hid = area(4096, FT, T)
        cvt = [[area(16384 + (s * 2 + i) * T, T) for i in range(2)] for s in range(2)]
        sil = area(18432, 2, T)

        QL, KV = area(4096, 2, T), area(5120, T)
        KR, KRS = area(5632, T), area(6144, T)
        QA, KA = area(6656, 8, T), area(10752, 8, T)
        VA = area(14848, 4, T)
        QB, KB, VB = area(16896, 4, T), area(18944, 4, T), area(20992, 4, T)
        BT = area(23040, 8, T)
        CH = area(27136, T)
        COS, SIN = area(27648, T), area(28160, T)
        PROB2 = [area(28672 + i * T, T) for i in range(2)], area(29696, T), [area(30208 + i * T, T) for i in range(2)]
        OA, OB = area(31232, 4, T), area(33280, 4, T)
        LSQ, LRT = area(35328, 3, T), area(36864, 2, T)
        ROT = area(35328, 2, T)
        ANG = area(31232, 4, T)
        BROW = area(33280, 640)
        merged2, gate2 = area(6656, KT, T), area(4096, 2, T)
        H2T = area(4096, 4, D)
        XE = area(8192, 2, 8, SLOTS)
        PE_ = area(9216, 2, 4, SLOTS)
        SG, MH = area(9728, 2, 2 * SLOTS), area(9984, 2, 2, SLOTS)
        YO = area(10240, 2, D)
        WR, BRT = area(12288, KT, 36), area(12576, 36)
        RL = area(12672, 4, 36)
        rt_ = [area(12832 + 160 * i, 160) for i in range(12)]
        C2S = small[:, 88:96]
        rt_e = area(14880, 20)
        MCON = area(14912, 224)
        BEF, SLOT_NO, ROWS = MCON[:, 0:128], MCON[:, 128:192], MCON[:, 192:224]
        SEL, F1, F2 = [area(15136 + 128 * i_, 4, 32) for i_ in range(3)]
        RK, RM = area(15520, 4, 32), area(15648, 4, 33)
        NRD, SINK = area(15780, 4), area(15784, 12)
        IDX = area(15796, 8).bitcast(mybir.dt.uint32)
        WGT, ROW0, RANK2, RANK_IN, WGT_IN = [area(15804 + 8 * i_, 8) for i_ in range(5)]
        GY, GX = area(16384, 8, D), area(24576, 4, D)
        EPSC, GNC, ZERO, ONE, ZSINK = [small[:, i:i + 1] for i in range(5)]
        NM, DEN, RD = small[:, 6:8], small[:, 8:10], small[:, 10:12]
        PK = small[:, 12:20].rearrange("p (a b) -> p a b", b=4)
        OMU, OKA, GAIN = small[:, 20:47], small[:, 48:56], small[:, 56:64]
        PLS = [small[:, 64:72], small[:, 72:80]]
        ZERO8 = small[:, 80:88]
        RSTD = sb("rstd", [P, T])[:, :]

        full = [sem(f"full{i}") for i in range(R)]
        half_done = sem("half_done")
        freed = {"A": sem("freed_by_act"), "D": sem("freed_by_dve")}
        act_link, dve_link, pool_link = sem("act_link"), sem("dve_link"), sem("pool_link")
        got_const, got_x, got_lora, got_g2, got_masks, got_x1 = [sem(n) for n in (
            "got_const", "got_x", "got_lora", "got_g2", "got_masks", "got_x1")]
        squared, summed, rooted, normed = sem("squared"), sem("summed"), sem("rooted"), sem("normed")
        mod_ready = sem("mod_ready")
        scaled = sem("scaled")
        lora_ready = sem("lora_ready")
        made = sem("made")
        emptA, emptD = sem("emptied_by_act"), sem("emptied_by_dve")
        chan, cum, decay, maskp = sem("chan_ready"), sem("cum_ready"), sem("decay_ready"), sem("masked_by_pool")
        stepped, state_ready = sem("stepped"), sem("state_ready")
        y_made, mean_made, var_made, g_made = sem("y_made"), sem("mean_made"), sem("var_made"), sem("g_made")
        y_added, centred, y_sq, y_root, y_final = [sem(n) for n in (
            "y_added", "centred", "y_squared", "y_rooted", "y_final")]
        gate_ready = sem("gate_ready")
        scored, masked, peaked, probbed, turned, turnedS, weighed, outed, oturned, oready, recipd = [sem(n) for n in (
            "scored", "masked", "peaked", "probbed", "turned", "turned_copied", "weighed", "outed",
            "out_turned", "out_ready", "reciprocal_ready")]
        convd, silud, hidd = sem("conv_scaled"), sem("silu_ready"), sem("hidden_ready")
        silu_c, got_bias, got_pos, got_router = sem("silu_c"), sem("got_bias"), sem("got_positions"), sem("got_router")
        bias_row, bias_out = sem("bias_row"), sem("bias_out")
        lat_sq, lat_sum, lat_root, lat_ready = [sem("latent_" + n) for n in ("squared", "summed", "rooted", "ready")]
        angled, rotated, band_ready = sem("angled"), sem("sines"), sem("band_ready")
        routed, route_exp, h2_made, h2_ready, selected, ranked, counted, rounds_ready, indexed = [sem(n) for n in (
            "logits_made", "route_exp", "h2_made", "h2_ready", "selected", "ranked", "counted", "rounds_ready", "indexed")]
        gu_done, down_made, placed, gathered, xe_ready, silu_m, mhid = [sem(n) for n in (
            "gate_up_done", "down_made", "placed", "gathered", "tokens_ready", "moe_silu", "moe_hidden")]
        copied = {"A": sem("result_by_act"), "D": sem("result_by_dve")}
        y_stored = [sem("results_stored_even"), sem("results_stored_odd")]
        fetched = [sem(f"fetched{i}") for i in range(4)]
        mixed, mix_turned, round_link, half_mixed, round_held = [sem(n) for n in ("mixed", "mix_turned", "round_link", "half_mixed", "round_held")]
        tail_link, out_scaled = sem("tail_link"), sem("out_scaled")
        stored = sem("stored")

        HALVES = {"ada1": (0, 1), "lora": (0, 3), "rkv": (0, 24), "rw_out": (8, 8), "qk": (12, 12), "v": (6, 6),
                  "at_out": (8, 8), "w_o": (0, 8), "up": (0, 44), "down": (0, 8),
                  "ada2": (0, 1), "in2": (9, 8), "lat2": (14, 14), "mla_out": (8, 8), "band_out": (8, 8),
                  "w_out2": (0, 8), "moe": (0, 8)}
        BEFORE, na, nd = {}, 0, 0
        for ph, _k in PHASES:
            BEFORE[ph] = {"A": na, "D": nd}
            x_, y_ = HALVES.get(ph, (0, 0))
            na, nd = na + x_, nd + y_

        def drain_psum(pe, phase):
            for e in "AD":
                if BEFORE[phase][e]:
                    pe.wait_ge(freed[e], BEFORE[phase][e])

        def bc(v, n):
            return v.unsqueeze(2).broadcast_to([v.shape[0], v.shape[1], n])

        def rep(v, n):
            return v.unsqueeze(1).broadcast_to([v.shape[0], n, v.shape[1]])

        def chunks(v):
            return v.rearrange("p (c k) -> p c k", k=C)

        units = [(qt, h) for qt in range(4) for h in range(8)]
        PROB1 = [area(20224 + i * 1280, 1280) for i in range(2)], area(22784, 1280), [area(25344 + i * T, T) for i in range(2)]
        OT1 = area(26368, 4, T)

        def parts1(unit, i):
            qt, h = unit
            r = slice(h % 2 * 64, h % 2 * 64 + 64)
            k0 = max(0, qt - 1) * P
            scores, vals, maskl = [], [], []
            for g in range(3):
                lo, hi = (k0 if g == 0 else 0), (qt + 1) * P
                qT, kT = QK[r, g * 8 + h // 2, qt * P:qt * P + P], QK[r, g * 8 + 4 + h // 2, lo:hi]
                scores.append((g, [(qT, kT)], g, hi - lo))
                m = near[:, 256 - (hi - lo):256] if g == 0 else (every4, every16)[g - 1][:, 384 - qt * P:T]
                maskl.append(m)
                vals += [VT[:, kt, g * T + h * 64:g * T + h * 64 + 64] for kt in range(lo // P, hi // P)]
            return {"scores": scores, "tiles": len(vals), "values": vals, "masks": maskl,
                    "out": slice(h * 64, h * 64 + 64), "scale": 0.125}

        def parts_mla(unit, i):
            qt, h = unit
            n_ = (qt + 1) * P
            return {"scores": [(0, [(QA[0:96, h, qt * P:n_], KA[0:96, h, 0:n_])], i % 2, n_)], "tiles": qt + 1,
                    "values": [VA[:, kt, h * 64:h * 64 + 64] for kt in range(qt + 1)],
                    "masks": [CH[:, 384 - qt * P:T]], "out": slice(h * 64, h * 64 + 64), "scale": 96 ** -0.5}

        def parts_band(unit, i):
            qt, h = unit
            n_, r = (qt + 1) * P, slice(h % 2 * 64, h % 2 * 64 + 64)
            return {"scores": [(0, [(QB[r, h // 2, qt * P:n_], KB[r, h // 2, 0:n_])], i % 2, n_)], "tiles": qt + 1,
                    "values": [VB[:, kt, h * 64:h * 64 + 64] for kt in range(qt + 1)],
                    "masks": [BT[:, h, 384 - qt * P:T]], "out": slice(h * 64, h * 64 + 64), "scale": 0.125}

        TURNED = []
        for parts_, us_ in ((parts1, units), (parts_mla, units), (parts_band, units)):
            for i_, u_ in enumerate(us_):
                TURNED.append((TURNED[-1] if TURNED else 0) + -(-parts_(u_, i_)["tiles"] // 4))

        block = ctx.enter_context(nc.Block())

        @block.sync
        def _(sp):
            for src, dst in ((a["consts"][:, 0:CONST_AT["near"][0]], const[:]), (a["cols"], cols[:])):
                sp.dma_start(dst, src).then_inc(got_const, 16)
            xv = a["x"].rearrange("(k p) t -> p k t", p=P)
            n = [0]

            def load(src, parts=P):
                m = n[0]
                n[0] += 1
                if m >= R:
                    sp.wait_ge(half_done, 2 * (m - R) + 2)
                size = src.shape[1] * src.shape[2]
                dst = ring[0:parts, m % R, 0:size].rearrange("p (k c) -> p k c", c=src.shape[2])
                sp.dma_start(dst, src).then_inc(full[m % R], 16)

            def wcols(w, c0, nc_=256):
                return w.rearrange("(k p) c -> p k c", p=P)[:, :, c0:c0 + nc_]

            def stream(w, count, at=0, step=256):
                first = n[0]
                wv = w.rearrange("(k p) c -> p k c", p=P)
                with sp.Fori(0, count // R) as i:
                    for j in range(R):
                        m = first + j
                        sp.wait_ge(half_done, i * (2 * R) + (2 * (m - R) + 2))
                        sp.dma_start(ring[:, m % R, :].rearrange("p (k c) -> p k c", c=256),
                                     wv[:, :, bass.ds(i * (R * 256) + (at + j * 256), 256)]).then_inc(full[m % R], 16)
                n[0] += count // R * R

            for j in range(R):
                load(wcols(a["w_ada"], j * 256))
            sp.dma_start(x_in, xv).then_inc(got_x, 16)
            sp.dma_start(W2A2[0:64, :], a["w2"]).then_inc(got_lora, 16)
            sp.dma_start(W2A2[64:128, :], a["a2"]).then_inc(got_lora, 16)
            stream(a["w_ada"], 20, at=4 * 256)
            RW = 4608
            if stop < 1:
                return
            load(wcols(a["w_in"], RW + 3072))
            load(wcols(a["w_in"], RW + 3328, 32))
            for q in range(4):
                for part in range(3):
                    load(wcols(a["w_in"], RW + part * D + q * 256))
            if stop < 2:
                return
            for g in range(4):
                load(wcols(a["w_in"], 7968 + D + g * 256))
                if g == 0:
                    sp.wait_ge(made, 8 * len(PRODUCTS))
                    sp.wait_ge(emptD, 4 * PER_QUAD["D"])
                    sp.wait_ge(emptA, 4 * PER_QUAD["A"])
                    sp.dma_start(G2[:, 0, :], a["g2"][0:128, :]).then_inc(got_g2, 16)
                    sp.dma_start(G2[0:32, 1, :], a["g2"][128:160, :]).then_inc(got_g2, 16)
                load(wcols(a["w_rwkv_out"], g * 256))
            if stop < 3:
                return
            for g in range(3):
                for part in range(2):
                    for c in range(2):
                        load(wcols(a["w_in"], g * 1536 + part * 512 + c * 256))
                if g == 0:
                    sp.wait_ge(half_done, 2 * FIRST["qk"])
                    sp.dma_start(masks, a["consts"][:, CONST_AT["near"][0]:CONST_AT["near"][0] + 1792]).then_inc(got_masks, 16)
            for g in range(3):
                for c in range(2):
                    load(wcols(a["w_in"], g * 1536 + 1024 + c * 256))
            for g in range(4):
                load(wcols(a["w_in"], 7968 + g * 256))
                load(wcols(a["w_att_out"], g * 256))
            if stop < 4:
                return
            for g in range(4):
                load(wcols(a["w_o"], g * 256))
                if g == 0:
                    sp.wait_ge(scored, len(units))
                    sp.dma_start(xT, xv).then_inc(got_x1, 16)
            upv = a["w_up"].rearrange("(k p) (g c) -> p g k c", p=P, g=2)
            first = n[0]
            def up_load(m, j):
                for g in range(2):
                    dst = ring[:, m % R, :].rearrange("p (g k c) -> p g k c", g=2, c=P)[:, g]
                    sp.dma_start(dst, upv[:, g, :, j]).then_inc(full[m % R], 8 * 2)
            with sp.Fori(0, 5) as i:
                for j in range(R):
                    m = first + j
                    sp.wait_ge(half_done, i * (2 * R) + (2 * (m - R) + 2))
                    up_load(m, bass.ds(i * (R * P) + j * P, P))
            for j in range(20, 22):
                m = first + j
                sp.wait_ge(half_done, 2 * (m - R) + 2)
                up_load(m, bass.ds(j * P, P))
            n[0] += 22
            dv = a["w_down"].rearrange("(k p) c -> p k c", p=P)
            for mm in range(4):
                for k0, k1 in ((0, 8), (8, 16), (16, 22)):
                    load(dv[:, k0:k1, mm * 256:mm * 256 + 256])

            if stop < 5:
                return
            stream(a["w_ada_2"], 24)
            load(wcols(a["w_in_2"], 0))
            load(wcols(a["w_kvr"], 0))
            load(wcols(a["w_kvr"], 256, 128))
            for c in range(6):
                load(wcols(a["w_in_2"], 416 + c * 256))
            for h in range(8):
                load(wcols(a["w_uq"], h * 256))
            for c in range(4):
                load(wcols(a["w_uk_2"], c * P, P))
            for c in range(2):
                load(wcols(a["w_uv_2"], c * 256))
            for w, at in ((a["w_oa_2"], 1952), (a["w_ob_2"], 1952 + D)):
                for g in range(4):
                    load(wcols(a["w_in_2"], at + g * 256))
                    load(wcols(w, g * 256))
            for g in range(4):
                load(wcols(a["w_out_2"], g * 256))
            if stop < 6:
                return
            gv = a["w_gate_2"].rearrange("e (k p) f -> p e k f", p=P)
            uv = a["w_up_2"].rearrange("e (k p) f -> p e k f", p=P)
            wd = a["w_down_2"].rearrange("e (k p) d -> p e k d", p=P)
            first = n[0]
            sp.wait_ge(half_done, 2 * first)
            sp.wait_ge(rounds_ready, 1)
            rounds = sp.value_load(NRD[0:1, 0:1].bitcast(I32), min_val=1, max_val=T // SLOTS)
            with sp.Fori(0, rounds) as r:
                with sp.Fori(0, 8) as i:
                    for j in range(4):
                        step = r * 32 + i * 4 + j
                        for part, w, c_ in ((0, gv, 256), (1, uv, 256), (2, wd, D)):
                            m = first + 3 * j + part
                            sp.wait_ge(*((down_made, step + 1), (gu_done, step * 2 + 1), (gu_done, step * 2 + 2))[part])
                            sp.dma_start(ring[:, m % R, :].rearrange("p (k c) -> p k c", c=c_),
                                         w[:, bass.ds(i * 4 + j, 1)].rearrange("p e k c -> p (e k) c")).then_inc(full[m % R], 16)
            sp.wait_ge(out_scaled, KT)
            sp.dma_start(a["out"].rearrange("(k p) t -> p k t", p=P), hT).then_inc(stored, 16)
            sp.wait_ge(stored, 16)

        @block.tensor
        def _(pe):
            n = [0]

            def full_value(m):
                up0, up1 = FIRST["up"], FIRST["up"] + 22
                ups = sum(1 for x in range(up0, min(m, up1 - 1) + 1) if x % R == m % R)
                return 16 * (m // R + 1 + ups)

            def slot():
                m = n[0]
                n[0] += 1
                pe.wait_ge(full[m % R], full_value(m))
                return m

            def half(m, hf, bank, rhs, width=P, kts=KT, out=None, start=True, stop=True, inc=1, cols_=256, slot_=None):
                w = ring[:, m % R, 0:kts * cols_].rearrange("p (k c) -> p k c", c=cols_)
                dst = ps[0:width, bank, :] if out is None else out
                for k in range(kts):
                    mm = pe.matmul(dst, w[:, k, hf * P:hf * P + width], rhs(k),
                                   start=(start and k == 0), stop=(stop and k == kts - 1))
                mm.then_inc(half_done, inc)

            def wait_bank(phase, hh, who):
                cnt = who(hh)
                if cnt:
                    pe.wait_ge(freed[cnt[0]], cnt[1])

            pe.wait_ge(got_const, 32)

            def ada_halves(m, at, cvec):
                for hf in range(2):
                    w = ring[:, m % R, :].rearrange("p (k c) -> p k c", c=256)
                    o = ps[:, 7, bass.ds(at + hf, 1)] if not isinstance(at, int) else ps[:, 7, at + hf:at + hf + 1]
                    for k in range(KT):
                        mm = pe.matmul(o, w[:, k, hf * P:hf * P + P], cvec(k), start=(k == 0), stop=(k == KT - 1))
                    mm.then_inc(half_done, 1)

            def ada(cvec):
                first = n[0]
                with pe.Fori(0, 24 // R) as i:
                    for j in range(R):
                        m = first + j
                        pe.wait_ge(full[m % R], i * 16 + full_value(m))
                        ada_halves(m, i * (2 * R) + 2 * j, cvec)
                n[0] += 24

            ada(lambda k: col("c", k))

            def norm_sum(k_norm):
                pe.wait_ge(squared, k_norm + 1)
                for k in range(KT):
                    mm = pe.matmul(ps[:, 6, :], ones, hT[:, k, :], start=(k == 0), stop=(k == KT - 1))
                mm.then_inc(summed, 1)

            norm_sum(0)

            def h_(k):
                return hT[:, k, :]

            if stop < 1:
                return
            pe.wait_ge(normed, 1)
            drain_psum(pe, "lora")
            m = slot()
            half(m, 0, 0, h_)
            half(m, 1, 1, h_)
            m = slot()
            half(m, 0, 2, h_, width=32, cols_=32, inc=2)

            pe.wait_ge(lora_ready, 1)
            pe.wait_ge(got_lora, 32)
            made_n = [0]

            def product(q, name, s, body, dep=()):
                i = made_n[0]
                made_n[0] += 1
                assert PNAMES[(i // 2) % len(PRODUCTS)] == name and i % 2 == s
                idx = (i // 2) % len(PRODUCTS)
                if i >= 2:
                    pq, pn = (q, PNAMES[idx - 1]) if idx else (q - 1, PNAMES[-1])
                    for e, sm in (("A", emptA), ("D", emptD)):
                        if e in PRODUCTS[PNAMES.index(pn)][1]:
                            pe.wait_ge(sm, emptied(pq, pn, s, e))
                for d in dep:
                    for e, sm in (("A", emptA), ("D", emptD)):
                        if e in PRODUCTS[PNAMES.index(d)][1]:
                            pe.wait_ge(sm, emptied(q, d, s, e))
                last = body(4 + 2 * s, 5 + 2 * s)
                last.then_inc(made, 1)

            def per_chunk(banks, terms):
                for e in range(2):
                    r = slice(e * 64, e * 64 + 64)
                    for c in range(NCH):
                        cc = slice(c * C, c * C + C)
                        for i, (l, x) in enumerate(terms):
                            mm = pe.matmul(ps[r, banks[e], cc], l[r, cc], x[r, 0:64] if x is eye64 else x[r, cc],
                                           start=(i == 0), stop=(i == len(terms) - 1))
                return mm

            for q in range(4):
                drain_psum(pe, "rkv") if q == 0 else None
                for part in range(3):
                    m = slot()
                    for hf in range(2):
                        hh = q * 6 + part * 2 + hf
                        if hh >= 4:
                            pe.wait_ge(freed["D"], BEFORE["rkv"]["D"] + hh - 3)
                        half(m, hf, hh % 4, h_)
                for s in range(2):
                    j = 2 * q + s

                    def lora(A, B, j=j):
                        pe.matmul(ps[:, A, :], W2A2[0:64, j * P:j * P + P], LOW[0:64, :], start=True, stop=True)
                        return pe.matmul(ps[:, B, :], W2A2[64:128, j * P:j * P + P], LOW[64:128, :], start=True, stop=True)
                    product(q, "lora", s, lora)
                for s in range(2):
                    pe.wait_ge(chan, 6 * q + 1 + s)
                    product(q, "ssq", s, lambda A, B: pe.matmul(ps[:, A, :], headones, tmp[s][10], start=True, stop=True))
                for s in range(2):
                    pe.wait_ge(chan, 6 * q + 3 + s)
                    product(q, "bonus", s, lambda A, B: pe.matmul(ps[:, A, :], headones, tmp[s][10], start=True, stop=True))
                for s in range(2):
                    t_ = tmp[s]
                    product(q, "tv", s, lambda A, B: per_chunk((A, B), [(t_[2], eye64)]))
                for name, b in (("tat", 6), ("tbh", 5), ("tkh", 3)):
                    for s in range(2):
                        t_ = tmp[s]
                        pe.wait_ge(chan, 6 * q + 5 + s)
                        product(q, name, s, lambda A, B: per_chunk((A, B), [(t_[b], eye64)]))
                for name, l, x in (("ab", 6, 4), ("abT", 4, 6), ("akT", 8, 6), ("rbT", 4, 0), ("rkT", 8, 0)):
                    for s in range(2):
                        t_ = tmp[s]
                        product(q, name, s, lambda A, B: per_chunk((A, B), [(t_[l], t_[x])]))
                nlev = len(LEVELS)
                for li, b in enumerate(LEVELS):
                    prev = ("ab", "abT") if li == 0 else (f"x{LEVELS[li - 1]}", f"xT{LEVELS[li - 1]}")
                    mb = 6 if li % 2 == 0 else 8
                    for s in range(2):
                        t_ = tmp[s]
                        pe.wait_ge(maskp, q * 2 * nlev + 2 * li + s + 1)
                        product(q, f"y{b}", s, lambda A, B: per_chunk((A, B), [(t_[mb], t_[2])]), dep=prev)
                    if b != LEVELS[-1]:
                        for s in range(2):
                            t_ = tmp[s]
                            product(q, f"x{b}", s, lambda A, B: per_chunk((A, B), [(t_[3], t_[4])]), dep=(f"y{b}",))
                    for s in range(2):
                        t_ = tmp[s]
                        product(q, f"xT{b}", s, lambda A, B: per_chunk((A, B), [(t_[4], t_[3])]), dep=(f"y{b}",))
                fin = f"xT{LEVELS[-1]}"
                for s in range(2):
                    t_ = tmp[s]
                    product(q, "w1", s, lambda A, B: per_chunk((A, B), [(t_[11], t_[1])]), dep=(fin,))
                for s in range(2):
                    t_ = tmp[s]
                    product(q, "sav", s, lambda A, B: per_chunk((A, B), [(t_[3], t_[4])]), dep=("w1",))
                for s in range(2):
                    t_ = tmp[s]
                    product(q, "z", s, lambda A, B: per_chunk((A, B), [(t_[3], t_[7])]), dep=())
                for s in range(2):
                    t_ = tmp[s]
                    product(q, "r", s, lambda A, B: per_chunk((A, B), [(t_[5], t_[12])]), dep=("z",))
                for s in range(2):
                    t_ = tmp[s]
                    product(q, "y0", s, lambda A, B: per_chunk((A, B), [(t_[2], t_[12]), (t_[1], t_[13])]), dep=("sav",))
                for s in range(2):
                    t_ = tmp[s]
                    product(q, "g", s, lambda A, B: per_chunk((A, B), [(t_[5], t_[9])]))
                for s in range(2):
                    t_ = tmp[s]
                    product(q, "h", s, lambda A, B: per_chunk((A, B), [(t_[9], t_[2]), (t_[10], t_[1])]))

            if stop < 2:
                return
            for e, sm in (("A", emptA), ("D", emptD)):
                pe.wait_ge(sm, 4 * PER_QUAD[e])
            for c in range(1, NCH - 1):
                pe.wait_ge(state_ready, c - 1) if c > 1 else None
                A = 4 + 2 * (c % 2)
                for e in range(2):
                    r = slice(e * 64, e * 64 + 64)
                    for j in range(8):
                        mm = pe.matmul(ps[r, A + e, j * C:j * C + C], GT[r, j, c, :], ST[r, c - 1, j, :],
                                       start=True, stop=True)
                mm.then_inc(stepped, 1)
            pe.wait_ge(state_ready, NCH - 2)
            pe.wait_ge(got_g2, 32)

            def y_state(j):
                if j >= 2:
                    pe.wait_ge(y_final, j - 1)
                for e in range(2):
                    r = slice(e * 64, e * 64 + 64)
                    for c in range(1, NCH):
                        mm = pe.matmul(ps[r, 4 + 2 * (j % 2) + e, c * C:c * C + C], ST[r, c - 1, j, :],
                                       RT[r, j, c * C:c * C + C], start=True, stop=True)
                mm.then_inc(y_made, 1)

            def y_mean(j):
                pe.wait_ge(y_added, j + 1)
                if j >= 2:
                    pe.wait_ge(centred, j - 1)
                pe.matmul(ps[:, j % 2, :], headones, Y0[:, j, :], start=True, stop=True).then_inc(mean_made, 1)

            def y_var(j):
                pe.wait_ge(y_sq, j + 1)
                if j >= 2:
                    pe.wait_ge(y_root, j - 1)
                pe.matmul(ps[:, 2 + j % 2, :], headones, ytmp[j % 2][0], start=True, stop=True).then_inc(var_made, 1)

            def y_gate(j):
                b = 4 + 2 * (j % 2)
                pe.matmul(ps[:, b, :], G2[:, 0, j * P:j * P + P], GLO, start=True, stop=False)
                pe.matmul(ps[:, b, :], G2[0:32, 1, j * P:j * P + P], GLO2[0:32], start=False, stop=True).then_inc(g_made, 1)

            for t in range(8 + 2):
                if 0 <= t - 2 < 8:
                    y_var(t - 2)
                if 0 <= t - 1 < 8:
                    y_mean(t - 1)
                    y_gate(t - 1)
                if t < 8:
                    y_state(t)
            pe.wait_ge(y_final, 8)

            def gated_projection(phase, rhs, kts):
                drain_psum(pe, phase)
                for g in range(4):
                    m = slot()
                    for hf in range(2):
                        i = 2 * g + hf
                        if i >= 2:
                            pe.wait_ge(freed["A"], BEFORE[phase]["A"] + i - 1)
                        half(m, hf, i % 2, h_)
                    m = slot()
                    for hf in range(2):
                        i = 2 * g + hf
                        if i >= 2:
                            pe.wait_ge(freed["D"], BEFORE[phase]["D"] + i - 1)
                        half(m, hf, 2 + i % 2, rhs, kts=kts)

            gated_projection("rw_out", lambda k: Y0[:, k, :], KT)

            if stop < 3:
                return
            def alternate(phase, hh):
                if hh >= 4:
                    e = "AD"[hh % 2]
                    pe.wait_ge(freed[e], BEFORE[phase][e] + (hh - 4) // 2 + 1)

            drain_psum(pe, "qk")
            for t in range(12):
                m = slot()
                for hf in range(2):
                    alternate("qk", 2 * t + hf)
                    half(m, hf, (2 * t + hf) % 4, h_)

            def token_major(phase, count):
                drain_psum(pe, phase)
                for t in range(count):
                    m = slot()
                    w = ring[:, m % R, :].rearrange("p (k c) -> p k c", c=256)
                    for hf in range(2):
                        hh = 2 * t + hf
                        alternate(phase, hh)
                        for tt in range(2):
                            tok = (2 * hf + tt) * P
                            for k in range(KT):
                                mm = pe.matmul(ps[:, hh % 4, tt * 256:tt * 256 + 256], hT[:, k, tok:tok + P],
                                               w[:, k, :], start=(k == 0), stop=(k == KT - 1))
                        mm.then_inc(half_done, 1)

            token_major("v", 6)
            drain_psum(pe, "at_out")

            def attend(u0, us, parts_of, s_banks):
                def scores(i):
                    if i >= s_banks:
                        pe.wait_ge(masked, u0 + i - s_banks + 1)
                    bank = 0
                    for q_, ks, bk, n_ in parts_of(us[i], i)["scores"]:
                        for t_, (l, x) in enumerate(ks):
                            mm = pe.matmul(ps[:, bk, 0:n_], l, x, start=(t_ == 0), stop=(t_ == len(ks) - 1))
                    mm.then_inc(scored, 1)

                def turn(i):
                    n_ = parts_of(us[i], i)["tiles"]
                    pe.wait_ge(probbed, u0 + i + 1)
                    for t_ in range(n_):
                        if t_ % 4 == 0:
                            g = turn_n[0]
                            turn_n[0] += 1
                            if g >= 2:
                                pe.wait_ge(turnedS, g - 1)
                        mm = pe.transpose(ps[:, 4 + g % 2, t_ % 4 * P:t_ % 4 * P + P],
                                          prob[(u0 + i) % 2][:, t_ * P:t_ * P + P], ident)
                        if t_ % 4 == 3 or t_ == n_ - 1:
                            mm.then_inc(turned, 1)

                def weigh(i):
                    u = u0 + i
                    pe.wait_ge(turnedS, turn_n[0])
                    if u >= 2:
                        pe.wait_ge(outed, u - 1)
                    vs = parts_of(us[i], i)["values"]
                    for t_, v in enumerate(vs):
                        mm = pe.matmul(ps[:, 6 + u % 2, 0:64], probT[:, t_ * P:t_ * P + P], v,
                                       start=(t_ == 0), stop=(t_ == len(vs) - 1))
                    mm.then_inc(weighed, 1)

                def turn_out(i):
                    w = (u0 + i) // 8
                    pe.wait_ge(outed, u0 + i + 1)
                    if w >= 1:
                        pe.wait_ge(oready, w)
                    for t_ in range(4):
                        mm = pe.transpose(ps[:, 3, t_ * P:t_ * P + P], otok[w % 2][:, t_ * P:t_ * P + P], ident)
                    mm.then_inc(oturned, 1)

                scores(0)
                for i in range(len(us)):
                    if i + 1 < len(us):
                        scores(i + 1)
                    turn(i)
                    weigh(i)
                    if i % 8 == 7:
                        turn_out(i)

            turn_n = [0]
            prob, probT, otok = PROB1
            attend(0, units, parts1, 1)
            pe.wait_ge(oready, 4)
            gated_projection("at_out", lambda k: OT1[:, k, :], 4)

            if stop < 4:
                return
            drain_psum(pe, "w_o")
            for t in range(4):
                m = slot()
                for hf in range(2):
                    hh = 2 * t + hf
                    if hh >= 4:
                        pe.wait_ge(freed["D"], BEFORE["w_o"]["D"] + hh - 3)
                    half(m, hf, hh % 4, lambda k: merged[:, k, :])

            norm_sum(1)
            pe.wait_ge(normed, 2)
            drain_psum(pe, "up")
            first = n[0]

            def up_slot(m, fv, hbase):
                pe.wait_ge(full[m % R], fv)
                for g in range(2):
                    w = ring[:, m % R, :].rearrange("p (g k c) -> p g k c", g=2, c=P)[:, g]
                    if hbase is not None:
                        pe.wait_ge(freed["D"], hbase + g)
                    for k in range(KT):
                        mm = pe.matmul(ps[:, (2 * (m - first) + g) % 4, :], w[:, k, :], h_(k), start=(k == 0), stop=(k == KT - 1))
                    mm.then_inc(half_done, 1)

            D0 = BEFORE["up"]["D"]
            for j in range(2):
                up_slot(first + j, full_value(first + j), None)
            with pe.Fori(0, 5) as i:
                for j in range(2, 2 + R):
                    m = first + j
                    up_slot(m, i * 32 + full_value(m), i * (2 * R) + (D0 + 2 * j - 3))
            n[0] += 22
            pe.wait_ge(hidd, FT)
            drain_psum(pe, "down")
            for mm_ in range(4):
                for part, kts in enumerate((8, 8, 6)):
                    m = slot()
                    for hf in range(2):
                        hh = 2 * mm_ + hf
                        if hh >= 4 and part == 0:
                            pe.wait_ge(freed["D"], BEFORE["down"]["D"] + hh - 3)
                        half(m, hf, hh % 4, lambda k, part=part: hid[:, part * 8 + k, :], kts=kts,
                             start=(part == 0), stop=(part == 2))
            norm_sum(2)

            if stop < 5:
                return
            pe.wait_ge(silu_c, 1)
            drain_psum(pe, "ada2")
            ada(lambda k: C2S[:, k:k + 1])
            norm_sum(3)
            pe.wait_ge(normed, 4)
            drain_psum(pe, "in2")
            o = 0
            for t in range(7):
                m = slot()
                for hf in range(1 if t == 2 else 2):
                    alternate("in2", o)
                    half(m, hf, o % 4, h_, cols_=P if t == 2 else 256, inc=2 if t == 2 else 1)
                    o += 1

            def token_slots(phase, o, count, src, kts):
                for t in range(count):
                    m = slot()
                    w = ring[:, m % R, 0:kts * 256].rearrange("p (k c) -> p k c", c=256)
                    for hf in range(2):
                        alternate(phase, o)
                        for tt in range(2):
                            tok = (2 * hf + tt) * P
                            for k in range(kts):
                                mm = pe.matmul(ps[:, o % 4, tt * 256:tt * 256 + 256], src(k)[:, tok:tok + P],
                                               w[:, k, :], start=(k == 0), stop=(k == kts - 1))
                        mm.then_inc(half_done, 1)
                        o += 1

            token_slots("in2", o, 2, h_, KT)
            pe.wait_ge(lat_sq, 1)
            pe.matmul(ps[:, 6, :], ones, LSQ[:, 0, :], start=True, stop=False)
            pe.matmul(ps[:, 6, :], ones, LSQ[:, 1, :], start=False, stop=True)
            pe.matmul(ps[:, 7, :], ones, LSQ[:, 2, :], start=True, stop=True).then_inc(lat_sum, 1)
            pe.wait_ge(lat_ready, 1)
            drain_psum(pe, "lat2")
            o = 0
            for h in range(8):
                m = slot()
                for hf in range(2):
                    alternate("lat2", o)
                    half(m, hf, o % 4, lambda k: QL[:, k, :], width=96, kts=2)
                    o += 1
            for t in range(4):
                m = slot()
                for hf in range(2):
                    alternate("lat2", o)
                    w = ring[:, m % R, 0:P]
                    pe.matmul(ps[0:64, o % 4, :], w[:, hf * 64:hf * 64 + 64], KV, start=True, stop=True).then_inc(half_done, 1)
                    o += 1
            token_slots("lat2", o, 2, lambda k: KV, 1)
            drain_psum(pe, "mla_out")
            pe.wait_ge(band_ready, 1)
            prob, probT, otok = PROB2
            attend(32, units, parts_mla, 2)
            attend(64, units, parts_band, 2)
            pe.wait_ge(oready, 12)
            gated_projection("mla_out", lambda k: OA[:, k, :], 4)
            gated_projection("band_out", lambda k: OB[:, k, :], 4)
            drain_psum(pe, "w_out2")
            for t in range(4):
                m = slot()
                for hf in range(2):
                    hh = 2 * t + hf
                    if hh >= 4:
                        pe.wait_ge(freed["D"], BEFORE["w_out2"]["D"] + hh - 3)
                    half(m, hf, hh % 4, lambda k: merged2[:, k, :])
            norm_sum(4)
            pe.wait_ge(normed, 5)
            if stop < 6:
                return
            pe.wait_ge(got_router, 64)
            for tt in range(4):
                for k in range(KT):
                    mm = pe.matmul(ps[:, 7, tt * 36:tt * 36 + 36], hT[:, k, tt * P:tt * P + P], WR[:, k, :],
                                   start=(k == 0), stop=(k == KT - 1))
            mm.then_inc(routed, 1)
            for g in range(8):
                if g >= 2:
                    pe.wait_ge(h2_ready, g - 1)
                tt = g // 2
                for k in range(4):
                    mm = pe.transpose(ps[:, 4 + g % 2, k * P:k * P + P], hT[:, g % 2 * 4 + k, tt * P:tt * P + P], ident)
                mm.then_inc(h2_made, 1)
            pe.wait_ge(selected, 1)
            for tt in range(4):
                for t_ in range(tt + 1):
                    mm = pe.matmul(ps[:, 6, tt * 32:tt * 32 + 32], BEF if t_ == tt else ones, SEL[:, t_, :],
                                   start=(t_ == 0), stop=(t_ == tt))
            mm.then_inc(ranked, 1)
            for t_ in range(4):
                mm = pe.matmul(ps[:, 3, 0:32], ones, SEL[:, t_, :], start=(t_ == 0), stop=(t_ == 3))
            mm.then_inc(counted, 1)
            pe.wait_ge(h2_ready, 8)
            pe.wait_ge(rounds_ready, 1)
            rounds = pe.value_load(NRD[0:1, 0:1].bitcast(I32), min_val=1, max_val=T // SLOTS)
            first = n[0]

            def gather(step, par):
                pe.wait_ge(placed, step + 1)
                for k in range(KT):
                    for tt in range(4):
                        mm = pe.matmul(ps[:, par, k * SLOTS:k * SLOTS + SLOTS], H2T[:, tt, k * P:k * P + P],
                                       PE_[:, par, tt, :], start=(tt == 0), stop=(tt == 3))
                mm.then_inc(gathered, 1)

            gather(0, 0)
            with pe.Fori(0, rounds) as r:
                with pe.Fori(0, 8) as i:
                    for j in range(4):
                        par = j % 2
                        step = r * 32 + i * 4 + j
                        pe.wait_ge(xe_ready, step + 1)
                        for part in range(2):
                            m = first + 3 * j + part
                            pe.wait_ge(full[m % R], r * 384 + i * 48 + full_value(m))
                            w = ring[:, m % R, :].rearrange("p (k c) -> p k c", c=256)
                            for f in range(2):
                                for k in range(KT):
                                    mm = pe.matmul(ps[:, 2 + par, (2 * part + f) * SLOTS:(2 * part + f + 1) * SLOTS],
                                                   w[:, k, f * P:f * P + P], XE[:, par, k, :], start=(k == 0), stop=(k == KT - 1))
                            mm.then_inc(gu_done, 1)
                        gather(step + 1, 1 - par)
                        m = first + 3 * j + 2
                        pe.wait_ge(full[m % R], r * 384 + i * 48 + full_value(m))
                        pe.wait_ge(copied["A"], step + 1)
                        pe.wait_ge(copied["D"], step + 1)
                        pe.wait_ge(mhid, step + 1)
                        w = ring[:, m % R, :].rearrange("p (k c) -> p k c", c=D)
                        for c in range(2):
                            for f in range(2):
                                mm = pe.matmul(ps[0:SLOTS, 4 + 2 * par + c, :], MH[:, par, f, :], w[:, f, c * 512:c * 512 + 512],
                                               start=(f == 0), stop=(f == 1))
                        mm.then_inc(down_made, 1)
            pe.wait_ge(mixed, rounds * 4)
            for k in range(KT):
                if k >= 2:
                    pe.wait_ge(freed["D"], BEFORE["moe"]["D"] + k - 1)
                for tt in range(4):
                    mm = pe.transpose(ps[:, 2 + k % 2, tt * P:tt * P + P], GX[:, tt, k * P:k * P + P], ident)
                mm.then_inc(mix_turned, 1)
            norm_sum(5)

        @block.scalar
        def _(act):
            lk = Link(act, act_link)
            act.wait_ge(got_const, 32)

            def norm_squares(k_norm, src):
                act.activation(hT, src, ACT.Square).then_inc(squared, 1)

            def norm_root(k_norm):
                act.wait_ge(summed, k_norm + 1)
                act.activation(RSTD, ps[:, 6, :], ACT.Sqrt, scale=1.0 / D, bias=EPSC).then_inc(rooted, 1)

            act.wait_ge(mod_ready, 1)
            act.wait_ge(got_x, 16)
            norm_squares(0, x_in)
            norm_root(0)
            if stop < 1:
                return

            act.wait_ge(got_lora, 32)
            for i, (dst, rows) in enumerate(((LOW, P), (GLO, P), (GLO2, 32))):
                act.wait_ge(half_done, 2 * FIRST["lora"] + (1, 2, 4)[i])
                act.activation(dst[0:rows], ps[0:rows, i, :], ACT.Copy if False else ACT.Identity,
                               scale=OMU[0:rows, 24 + i:25 + i], bias=ZERO[0:rows]).then_inc(scaled, 1)
            act.wait_ge(freed["D"], BEFORE["lora"]["D"] + 1)
            act.activation(LOW[0:64], LOW[0:64], ACT.Tanh).then_inc(act_link, 1)
            act.wait_ge(freed["D"], BEFORE["lora"]["D"] + 3)
            act.activation(GLO, GLO, ACT.Sigmoid).then_inc(act_link, 1)
            act.activation(GLO2[0:32], GLO2[0:32], ACT.Sigmoid).then_inc(act_link, 1)
            act.wait_ge(act_link, 3)
            act.activation(ZSINK, ZERO, ACT.Copy).then_inc(lora_ready, 1)

            np_ = len(PRODUCTS)

            def made_wait(q, name, s):
                act.wait_ge(made, 2 * np_ * q + 2 * PNAMES.index(name) + s + 1)

            def empty_half(q, name, s, dst):
                made_wait(q, name, s)
                act.activation(dst[0:64], ps[0:64, 4 + 2 * s, :], ACT.Copy).then_inc(emptA, 1)

            for q in range(4):
                for part in range(3):
                    for hf in range(2):
                        j = 2 * q + hf
                        hh = q * 6 + part * 2 + hf
                        act.wait_ge(half_done, 2 * FIRST["rkv"] + hh + 1)
                        if q and part == 0 and hf == 0:
                            act.wait_ge(made, 2 * np_ * q)
                            act.wait_ge(emptD, PER_QUAD["D"] * q)
                        act.activation(tmp[hf][part], ps[:, hh % 4, :], ACT.Identity,
                                       scale=OMU[:, part * 8 + j:part * 8 + j + 1], bias=ZERO).then_inc(scaled, 1)
                for s in range(2):
                    j = 2 * q + s
                    made_wait(q, "lora", s)
                    act.activation(tmp[s][3], ps[:, 4 + 2 * s, :], ACT.Sigmoid, bias=col("w0", j)).then_inc(act_link, 1)
                    act.wait_ge(act_link, 3 + 2 * q + s + 1)
                    act.activation(tmp[s][4], ps[:, 5 + 2 * s, :], ACT.Sigmoid, bias=col("a0", j)).then_inc(emptA, 1)
                for s in range(2):
                    made_wait(q, "ssq", s)
                    act.activation(tmp[s][10], ps[:, 4 + 2 * s, :], ACT.Sqrt, bias=ZERO).then_inc(emptA, 1)
                for s in range(2):
                    act.wait_ge(cum, 2 * q + s + 1)
                    t_ = tmp[s]
                    act.activation(t_[7], t_[5], ACT.Exp, scale=-KAPPA).then_inc(decay, 1)
                    act.activation(t_[8], t_[5], ACT.Exp, scale=KAPPA).then_inc(decay, 1)
                    act.activation(t_[6], t_[6], ACT.Exp, scale=-KAPPA).then_inc(decay, 1)
                for s in range(2):
                    act.wait_ge(chan, 6 * q + 5 + s) if s == 0 else act.wait_ge(chan, 6 * q + 6)
                    empty_half(q, "tv", s, tmp[s][1])
                for name, d in (("tat", 7), ("tbh", 9), ("tkh", 10)):
                    for s in range(2):
                        empty_half(q, name, s, tmp[s][d])
                for b in LEVELS:
                    for s in range(2):
                        empty_half(q, f"y{b}", s, tmp[s][4])
                for name, d in (("w1", 4), ("sav", 2), ("z", 5)):
                    for s in range(2):
                        empty_half(q, name, s, tmp[s][d])
                for s in range(2):
                    j = 2 * q + s
                    made_wait(q, "y0", s)
                    act.activation(Y0[0:64, j, :], ps[0:64, 4 + 2 * s, :], ACT.Copy).then_inc(emptA, 1)
                for s in range(2):
                    j = 2 * q + s
                    made_wait(q, "h", s)
                    act.activation(ST[0:64, :, j, :], chunks(ps[0:64, 4 + 2 * s, :]), ACT.Copy).then_inc(emptA, 1)
            if stop < 2:
                return

            def y_square(j):
                act.wait_ge(centred, j + 1)
                if j >= 2:
                    act.wait_ge(y_root, j - 1)
                act.activation(ytmp[j % 2][0], Y0[:, j, :], ACT.Square).then_inc(y_sq, 1)

            def y_roots(j):
                act.wait_ge(var_made, j + 1)
                if j >= 2:
                    act.wait_ge(y_final, j - 1)
                act.activation(ytmp[j % 2][1], ps[:, 2 + j % 2, :], ACT.Sqrt, scale=1.0 / 64, bias=GNC).then_inc(y_root, 1)

            for t in range(9):
                if t >= 1:
                    y_roots(t - 1)
                if t < 8:
                    y_square(t)

            def gates(phase, at):
                for g in range(4):
                    for hf in range(2):
                        i = 2 * g + hf
                        act.wait_ge(half_done, 2 * FIRST[phase] + 4 * g + hf + 1)
                        if i >= 2:
                            act.wait_ge(freed["D"], BEFORE[phase]["D"] + i - 1)
                        elif i == 0:
                            act.wait_ge(freed["D"], BEFORE[phase]["D"])
                        gb, bias = (gate, col("b_gate", at + i)) if at is not None else (gate2, ZERO)
                        act.activation(gb[:, i % 2, :], ps[:, i % 2, :], ACT.Sigmoid, bias=bias).then_inc(freed["A"], 1)

            if True:
                act.wait_ge(y_final, 8)
            gates("rw_out", 8)
            if stop < 3:
                return

            act.wait_ge(freed["D"], BEFORE["qk"]["D"])
            for i in range(12):
                act.wait_ge(half_done, 2 * FIRST["qk"] + 2 * i + 1)
                act.activation(QK[:, 2 * i, :], ps[:, 2 * i % 4, :], ACT.Copy).then_inc(freed["A"], 1)
            for i in range(6):
                act.wait_ge(half_done, 2 * FIRST["v"] + 2 * i + 1)
                act.activation(VT[:, 0:2, i * 256:i * 256 + 256], ps[:, 2 * i % 4, :].rearrange("p (a b) -> p a b", b=256),
                               ACT.Copy).then_inc(freed["A"], 1)

            turn_n = [0]

            def attend(u0, us, parts_of, prob, probT, OT):
                def exps(i):
                    u = u0 + i
                    act.wait_ge(peaked, u + 1)
                    n_ = parts_of(us[i], i)["tiles"] * P
                    act.activation(prob[u % 2][:, 0:n_], prob[u % 2][:, 0:n_], ACT.Exp, scale=parts_of(us[i], i)["scale"],
                                   bias=NM[:, u % 2:u % 2 + 1], accum_out=DEN[:, u % 2:u % 2 + 1]).then_inc(probbed, 1)

                def copies(i):
                    u = u0 + i
                    n_ = parts_of(us[i], i)["tiles"]
                    if u >= 1:
                        act.wait_ge(weighed, u)
                    for t_ in range(0, n_, 4):
                        g = turn_n[0]
                        turn_n[0] += 1
                        k = min(4, n_ - t_)
                        act.wait_ge(turned, g + 1)
                        act.activation(probT[:, t_ * P:(t_ + k) * P], ps[:, 4 + g % 2, 0:k * P], ACT.Copy).then_inc(turnedS, 1)

                def out_copy(i):
                    w = (u0 + i) // 8
                    act.wait_ge(oturned, w + 1)
                    qt = us[i][0]
                    act.activation(OT[:, :, qt * P:qt * P + P], ps[:, 3, :].rearrange("p (a b) -> p a b", b=P),
                                   ACT.Copy).then_inc(oready, 1)

                exps(0)
                for i in range(len(us)):
                    if i + 1 < len(us):
                        exps(i + 1)
                    copies(i)
                    if i % 8 == 0 and i:
                        out_copy(i - 1)
                out_copy(len(us) - 1)

            attend(0, units, parts1, PROB1[0], PROB1[1], OT1)
            gates("at_out", 0)
            if stop < 4:
                return

            act.wait_ge(freed["D"], BEFORE["up"]["D"])
            act.wait_ge(half_done, 2 * FIRST["up"])
            norm_squares(1, xT)
            norm_root(1)
            act.wait_ge(normed, 2)

            H0 = 2 * FIRST["up"]
            D0 = BEFORE["up"]["D"]

            def up_scale(jj, hb, cb):
                for g in range(2):
                    act.wait_ge(half_done, hb(2 * jj + g + 1))
                    if jj >= 2:
                        act.wait_ge(hidd, cb(jj - 1))
                    act.activation(cvt[jj % 2][g], ps[:, (2 * jj + g) % 4, :], ACT.Identity,
                                   scale=up_col(2, g, jj, cb), bias=up_col(3, g, jj, cb)).then_inc(convd, 1)

            def up_silu(jj, hb, cb, db):
                act.wait_ge(freed["D"], db(2 * jj + 1))
                act.activation(sil[:, jj % 2, :], cvt[jj % 2][0], ACT.Silu).then_inc(silud, 1)

            def up_col(tap, g, jj, cb):
                base = (COL_AT["conv_w"] + tap * 44 if tap < 3 else COL_AT["conv_b"]) + g * FT
                i = cb(jj)
                return cols[:, base + i:base + i + 1] if isinstance(i, int) else cols[:, bass.ds(i + base, 1)]

            ident_ = (lambda v: H0 + v), (lambda v: v), (lambda v: D0 + v)
            for jj in range(2):
                up_scale(jj, ident_[0], ident_[1])
                up_silu(jj, *ident_)
            with act.Fori(0, 5) as i:
                for jj in range(2, 2 + R):
                    f = (lambda v: i * 8 + (H0 + v)), (lambda v: i * 4 + v), (lambda v: i * 8 + (D0 + v))
                    up_scale(jj, f[0], f[1])
                    up_silu(jj, *f)
            act.wait_ge(freed["D"], BEFORE["ada2"]["D"])
            norm_squares(2, xT)
            norm_root(2)

            if stop < 5:
                return
            act.activation(C2S, col("c_2", 0, 8), ACT.Silu).then_inc(silu_c, 1)
            act.wait_ge(normed, 3)
            norm_squares(3, xT)
            norm_root(3)
            act.wait_ge(angled, 1)
            act.activation(ANG[:, 0:2, :], ANG[:, 0:2, :], ACT.Sin, bias=ZERO).then_inc(rotated, 1)

            def psum_out(phase, o, dst, src, v):
                act.wait_ge(half_done, 2 * FIRST[phase] + v)
                act.activation(dst, src, ACT.Copy).then_inc(freed["A"], 1)

            in2_value = lambda o: o + 1 if o < 4 else o + 2
            tok2 = lambda v: v.rearrange("p (a b) -> p a b", b=256)
            IN2 = [QL[:, 0, :], QL[:, 1, :], KV, KR, KRS] + [QB[:, j, :] for j in range(4)] + [KB[:, j, :] for j in range(4)]
            act.wait_ge(rotated, 1)
            for o in range(0, 13, 2):
                psum_out("in2", o, IN2[o], ps[:, o % 4, :], in2_value(o))
            for o in (14, 16):
                c, hf = divmod(o - 13, 2)
                psum_out("in2", o, VB[:, 2 * hf:2 * hf + 2, c * 256:c * 256 + 256], tok2(ps[:, o % 4, :]), in2_value(o))
            act.wait_ge(freed["D"], BEFORE["in2"]["D"] + 1)
            act.activation(LSQ[:, 0:2, :], QL, ACT.Square).then_inc(act_link, 1)
            act.activation(LSQ[:, 2, :], KV, ACT.Square).then_inc(lat_sq, 1)
            act.wait_ge(lat_sum, 1)
            act.activation(LRT[:, 0, :], ps[:, 6, :], ACT.Sqrt, scale=1.0 / 256, bias=EPSC).then_inc(lat_root, 1)
            act.activation(LRT[:, 1, :], ps[:, 7, :], ACT.Sqrt, scale=1.0 / 128, bias=EPSC).then_inc(lat_root, 1)
            for o in range(0, 16, 2):
                psum_out("lat2", o, QA[0:96, o // 2, :], ps[0:96, o % 4, :], o + 1)
            for o in range(16, 24, 2):
                psum_out("lat2", o, KA[0:64, o - 16, :], ps[0:64, o % 4, :], o + 1)
            for o in (24, 26):
                c, hf = divmod(o - 24, 2)
                psum_out("lat2", o, VA[:, 2 * hf:2 * hf + 2, c * 256:c * 256 + 256], tok2(ps[:, o % 4, :]), o + 1)
            attend(32, units, parts_mla, PROB2[0], PROB2[1], OA)
            attend(64, units, parts_band, PROB2[0], PROB2[1], OB)
            gates("mla_out", None)
            gates("band_out", None)
            act.wait_ge(freed["D"], BEFORE["moe"]["D"])
            act.wait_ge(half_done, 2 * FIRST["moe"])
            norm_squares(4, xT)
            norm_root(4)
            if stop < 6:
                return
            act.wait_ge(route_exp, 1)
            act.activation(rt_e, rt_e, ACT.Exp).then_inc(route_exp, 1)
            for g in range(8):
                act.wait_ge(h2_made, g + 1)
                act.activation(H2T[:, g // 2, g % 2 * 512:g % 2 * 512 + 512], ps[:, 4 + g % 2, :], ACT.Copy).then_inc(h2_ready, 1)
            for b in range(2):
                act.activation(SINK[:, b:b + 1], ZERO, ACT.Copy).then_inc(copied["A"], 1)
                act.activation(SINK[:, 2 + b:3 + b], ZERO, ACT.Copy).then_inc(y_stored[b], 16)
            act.wait_ge(rounds_ready, 1)
            rounds = act.value_load(NRD[0:1, 0:1].bitcast(I32), min_val=1, max_val=T // SLOTS)
            ybuf = a["y_scratch"].rearrange("(e t) d -> t e d", t=SLOTS)

            def tokens(step, par):
                act.wait_ge(gathered, step + 1)
                act.activation(XE[:, par].rearrange("p k s -> p (k s)"), ps[:, par, :], ACT.Copy).then_inc(xe_ready, 1)

            tokens(0, 0)
            with act.Fori(0, rounds) as r:
                with act.Fori(0, 8) as i:
                    for j in range(4):
                        par = j % 2
                        step = r * 32 + i * 4 + j
                        act.wait_ge(gu_done, step * 2 + 4)
                        act.activation(SG[:, par, :], ps[:, 2 + par, 0:2 * SLOTS], ACT.Silu).then_inc(silu_m, 1)
                        tokens(step + 1, 1 - par)
                        act.wait_ge(down_made, step + 3)
                        act.wait_ge(y_stored[par], r * 256 + i * 32 + (j // 2 * 16 + 16))
                        act.activation(YO[0:SLOTS, par, 0:512], ps[0:SLOTS, 4 + 2 * par, :], ACT.Copy).then_inc(copied["A"], 1)
                        act.wait_ge(copied["A"], step + 3)
                        act.wait_ge(copied["D"], step + 3)
                        act.dma_start(ybuf[:, bass.ds(i * 4 + j, 1), :].rearrange("t e d -> t (e d)"),
                                      YO[0:SLOTS, par, :]).then_inc(y_stored[par], 16)
                act.wait_ge(mixed, r * 4 + 4)
            act.wait_ge(freed["D"], BEFORE["moe"]["D"] + 8)
            norm_squares(5, xT)
            norm_root(5)

        @block.gpsimd
        def _(pool):
            if stop < 1:
                return
            np_ = len(PRODUCTS)
            for q in range(4):
                for li, b in enumerate(LEVELS):
                    for s in range(2):
                        dst = tmp[s][6 if li % 2 == 0 else 8]
                        if li == 0 and s == 0:
                            pool.wait_ge(made, 2 * np_ * q + 2 * PNAMES.index("rkT") + 2)
                            pool.wait_ge(emptD, emptied(q, "rkT", 1, "D"))
                        if li >= 2:
                            pool.wait_ge(made, 2 * np_ * q + 2 * PNAMES.index(f"y{LEVELS[li - 2]}") + s + 1)
                        pool.tensor_tensor(chunks(dst), chunks(tmp[s][5]), rep(cst(f"level{b}"), NCH), ALU.mult).then_inc(maskp, 1)

            if stop < 5:
                return
            pool.wait_ge(half_done, 2 * FIRST["up"])
            pool.wait_ge(freed["D"], BEFORE["up"]["D"])
            pool.dma_start(BROW[0:8, 255:640], a["rel_reversed"][:, 0:385]).then_inc(bias_row, 16)
            pool.dma_start(CH, a["consts"][:, CONST_AT["chunked"][0]:CONST_AT["chunked"][0] + T]).then_inc(got_pos, 16)
            pool.dma_start(ANG[:, 3, :].bitcast(I32), a["positions"].partition_broadcast(P)).then_inc(got_pos, 16)
            pool.wait_ge(bias_row, 16)
            pool.tensor_copy(BROW[0:8, 0:255], BROW[0:8, 255:256].broadcast_to([8, 255])).then_inc(pool_link, 1)
            pool.wait_ge(pool_link, 1)
            pool.dma_start(a["bias_scratch"], BROW[0:8, :].unsqueeze(1).broadcast_to([8, P, 640])).then_inc(bias_out, 16)
            pool.wait_ge(bias_out, 16)
            pool.dma_start(BT, bass.AP(a["bias_scratch"].tensor, 127, [[639, P], [P * 640, 8], [1, T]])).then_inc(got_bias, 16)
            if stop < 6:
                return
            pool.wait_ge(half_done, 2 * FIRST["w_out2"])
            pool.wait_ge(freed["D"], BEFORE["w_out2"]["D"])
            pool.dma_start(WR[:, :, 0:4], a["w_rg_2"].rearrange("(k p) c -> p k c", p=P)).then_inc(got_router, 16)
            pool.dma_start(WR[:, :, 4:36], a["w_re_2"].rearrange("(k p) c -> p k c", p=P)).then_inc(got_router, 16)
            pool.dma_start(MCON, a["consts"][:, CONST_AT["before"][0]:NCONST]).then_inc(got_router, 16)
            pool.dma_start(BRT, a["b_router"].partition_broadcast(P)).then_inc(got_router, 16)
            pool.wait_ge(rounds_ready, 1)
            rounds = pool.value_load(NRD[0:1, 0:1].bitcast(I32), min_val=1, max_val=T // SLOTS)
            with pool.Fori(0, rounds) as r:
                pool.wait_ge(indexed, r + 1)
                for b in range(2):
                    pool.wait_ge(y_stored[b], r * 256 + 272)
                pool.tensor_tensor(SINK[:, 10:11], ZERO, ZERO, ALU.add).then_inc(round_held, 1)
                for tt in range(4):
                    for w in range(2):
                        pool.indirect_dma_start(GY[:, 2 * tt + w, :], None, a["y_scratch"],
                                                bass.IndirectOffsetOnAxis(ap=IDX[:, 2 * tt + w:2 * tt + w + 1], axis=0)).then_inc(fetched[tt], 16)
                pool.wait_ge(round_held, r + 1)

        @block.vector
        def _(dve):
            lk = Link(dve, dve_link)
            tt, ts, stt = dve.tensor_tensor, dve.tensor_scalar, dve.scalar_tensor_tensor
            lk(dve.memset(EPSC, EPS))
            lk(dve.memset(GNC, GN_EPS))
            dve.memset(ZERO, 0.0).then_inc(dve_link, 1)
            lk.n += 1
            dve.wait_ge(dve_link, lk.n)
            dve.wait_ge(got_const, 32)
            lk.done(ts(OMU, col("mu", 0, 27), -1.0, 1.0, ALU.mult, ALU.add))
            ts(OKA, col("k_a", 0, 8), -1.0, 1.0, ALU.mult, ALU.add).then_inc(mod_ready, 1)

            def modulation(phase, bias):
                dve.wait_ge(half_done, 2 * FIRST[phase] + 48)
                lk.done(tt(mod[:], ps[:, 7, 0:48], bias, ALU.add))

            def gain(which, w):
                lk.done(ts(GAIN, mod[:, which * 24 + 8:which * 24 + 16], 1.0, None, ALU.add))
                lk.done(tt(GAIN, GAIN, w, ALU.mult))

            def norm_apply(k_norm, src, g, shift, dst):
                dve.wait_ge(rooted, k_norm + 1)
                lk.done(dve.reciprocal(RSTD, RSTD))
                lk.done(tt(dst, src, rep(RSTD, KT), ALU.mult))
                for k in range(KT):
                    if shift is None:
                        ins = ts(dst[:, k, :], dst[:, k, :], g[:, k:k + 1], None, ALU.mult)
                    else:
                        ins = ts(dst[:, k, :], dst[:, k, :], g[:, k:k + 1], shift[:, k:k + 1], ALU.mult, ALU.add)
                    if k == KT - 1:
                        ins.then_inc(normed, 1)

            modulation("ada1", col("b_ada", 0, 48))
            gain(0, col("norm1_w", 0, 8))
            ts(ONE, ZERO, 1.0, None, ALU.add).then_inc(freed["D"], 1)
            dve.wait_ge(got_x, 16)
            norm_apply(0, x_in, GAIN, mod[:, 0:8], hT)
            if stop < 1:
                return
            sc_n = 0

            def shift(dst, bank, mu, rows=P):
                nonlocal sc_n
                sc_n += 1
                dve.wait_ge(scaled, sc_n)
                stt(dst[0:rows, 1:T], ps[0:rows, bank, 0:T - 1], mu[0:rows], dst[0:rows, 1:T],
                    ALU.mult, ALU.add).then_inc(freed["D"], 1)

            for i, (dst, rows) in enumerate(((LOW, P), (GLO, P), (GLO2, 32))):
                shift(dst, i, col("mu", 24 + i), rows)

            np_ = len(PRODUCTS)

            def made_wait(q, name, s):
                dve.wait_ge(made, 2 * np_ * q + 2 * PNAMES.index(name) + s + 1)

            def bank_rows(s, e):
                return slice(e * 64, e * 64 + 64), 4 + 2 * s + e

            def empty_half(q, name, s, dst):
                made_wait(q, name, s)
                r, b = bank_rows(s, 1)
                dve.tensor_copy(dst[r], ps[r, b, :]).then_inc(emptD, 1)

            def empty_masked(q, name, s, dst, mask):
                made_wait(q, name, s)
                for e in range(2):
                    r, b = bank_rows(s, e)
                    ins = tt(chunks(dst[r]), chunks(ps[r, b, :]), rep(mask[r], NCH), ALU.mult)
                    if e == 0:
                        lk(ins)
                    else:
                        ins.then_inc(emptD, 1)

            def empty_added(q, name, s, dst, src, out3=None):
                made_wait(q, name, s)
                for e in range(2):
                    r, b = bank_rows(s, e)
                    ins = tt(dst[r], ps[r, b, :], src[r], ALU.add)
                    if e == 0:
                        lk(ins)
                    else:
                        ins.then_inc(emptD, 1)

            for q in range(4):
                for part in range(3):
                    for hf in range(2):
                        hh = q * 6 + part * 2 + hf
                        shift(tmp[hf][part], hh % 4, col("mu", part * 8 + 2 * q + hf))
                dve.wait_ge(freed["D"], BEFORE["rkv"]["D"] + 6 * q + 6)
                for s in range(2):
                    t_ = tmp[s]
                    lk.done(ts(t_[9], t_[1], col("k_k", 2 * q + s), None, ALU.mult))
                    tt(t_[10], t_[9], t_[9], ALU.mult).then_inc(chan, 1)
                for s in range(2):
                    t_ = tmp[s]
                    dve.wait_ge(emptA, emptied(q, "lora", s, "A"))
                    lk.done(dve.tensor_tensor_scan(t_[5], cst("restart"), t_[3], 0.0, ALU.mult, ALU.add))
                    tt(t_[6], t_[5], t_[3], ALU.subtract).then_inc(cum, 1)
                for s in range(2):
                    j = 2 * q + s
                    t_ = tmp[s]
                    dve.wait_ge(emptA, emptied(q, "ssq", s, "A"))
                    lk.done(ts(t_[10], t_[10], 1e-12, None, ALU.max))
                    lk.done(dve.reciprocal(t_[10], t_[10]))
                    lk.done(tt(t_[9], t_[9], t_[10], ALU.mult))
                    lk.done(ts(t_[10], t_[4], col("k_a", j), OKA[:, j:j + 1], ALU.mult, ALU.add))
                    lk.done(tt(t_[1], t_[1], t_[10], ALU.mult))
                    lk.done(stt(t_[10], t_[0], col("r_k", j), t_[1], ALU.mult, ALU.mult))
                    tt(t_[4], t_[4], t_[9], ALU.mult).then_inc(chan, 1)
                for s in range(2):
                    t_ = tmp[s]
                    dve.wait_ge(chan, 6 * q + 3 + s)
                    dve.wait_ge(decay, 6 * q + 3 * s + 3)
                    lk.done(stt(t_[6], t_[9], -1.0, t_[6], ALU.mult, ALU.mult))
                    lk.done(tt(t_[4], t_[4], t_[8], ALU.mult))
                    lk.done(tt(t_[8], t_[1], t_[8], ALU.mult))
                    lk.done(tt(t_[0], t_[0], t_[7], ALU.mult))
                    lk.done(dve.tensor_copy(PLS[s], chunks(t_[7])[:, :, C - 1]))
                    lk.done(tt(chunks(t_[5]), chunks(t_[4]), bc(PLS[s], C), ALU.mult))
                    tt(chunks(t_[3]), chunks(t_[8]), bc(PLS[s], C), ALU.mult).then_inc(chan, 1)
                for s in range(2):
                    made_wait(q, "bonus", s)
                    tt(BON[:, 2 * q + s, :], ps[:, 4 + 2 * s, :], tmp[s][2], ALU.mult).then_inc(emptD, 1)
                for name, d in (("tv", 1), ("tat", 7), ("tbh", 9), ("tkh", 10)):
                    for s in range(2):
                        empty_half(q, name, s, tmp[s][d])
                for name, d, mask in (("ab", 2, "pair1"), ("abT", 11, "upper"), ("akT", 11, "upper"),
                                      ("rbT", 12, "upto"), ("rkT", 13, "upto")):
                    for s in range(2):
                        t_ = tmp[s]
                        if name == "ab":
                            made_wait(q, name, s)
                            for e in range(2):
                                r, b = bank_rows(s, e)
                                lk.done(tt(chunks(t_[2][r]), chunks(ps[r, b, :]), rep(cst("pair1")[r], NCH), ALU.mult))
                            tt(chunks(t_[2]), chunks(t_[2]), rep(eye64, NCH), ALU.add).then_inc(emptD, 1)
                        elif name == "abT":
                            made_wait(q, name, s)
                            for e in range(2):
                                r, b = bank_rows(s, e)
                                lk.done(tt(chunks(t_[5][r]), chunks(ps[r, b, :]), rep(cst("upper")[r], NCH), ALU.mult))
                            lk.done(tt(chunks(t_[3]), chunks(t_[5]), rep(cst("pair1T"), NCH), ALU.mult))
                            tt(chunks(t_[3]), chunks(t_[3]), rep(eye64, NCH), ALU.add).then_inc(emptD, 1)
                        else:
                            empty_masked(q, name, s, t_[d], cst(mask))
                for b in LEVELS:
                    for s in range(2):
                        empty_half(q, f"y{b}", s, tmp[s][4])
                    if b != LEVELS[-1]:
                        for s in range(2):
                            empty_added(q, f"x{b}", s, tmp[s][2], tmp[s][2])
                    for s in range(2):
                        empty_added(q, f"xT{b}", s, tmp[s][3], tmp[s][3])
                for name, d in (("w1", 4), ("sav", 2), ("z", 5)):
                    for s in range(2):
                        empty_half(q, name, s, tmp[s][d])
                for s in range(2):
                    empty_added(q, "r", s, RT[:, 2 * q + s, :], tmp[s][0])
                for s in range(2):
                    empty_half(q, "y0", s, Y0[:, 2 * q + s, :])
                for s in range(2):
                    j = 2 * q + s
                    lk.done(tt(GT[:, j], rep(eye64, NCH), bc(PLS[s], C), ALU.mult))
                    gt = GT[:, j].rearrange("p c k -> p (c k)")
                    empty_added(q, "g", s, gt, gt)
                for s in range(2):
                    made_wait(q, "h", s)
                    r, b = bank_rows(s, 1)
                    dve.tensor_copy(ST[r, :, 2 * q + s, :], chunks(ps[r, b, :])).then_inc(emptD, 1)
            if stop < 2:
                return

            dve.wait_ge(emptA, 4 * PER_QUAD["A"])
            dve.wait_ge(emptD, 4 * PER_QUAD["D"])
            for c in range(1, NCH - 1):
                dve.wait_ge(stepped, c)
                for e in range(2):
                    r = slice(e * 64, e * 64 + 64)
                    v = ST[r, c].rearrange("p j k -> p (j k)")
                    ins = tt(v, ps[r, 4 + 2 * (c % 2) + e, :], v, ALU.add)
                    if e == 0:
                        lk(ins)
                    else:
                        ins.then_inc(state_ready, 1)

            def y_add(j):
                dve.wait_ge(y_made, j + 1)
                for e in range(2):
                    r = slice(e * 64, e * 64 + 64)
                    ins = tt(Y0[r, j, C:T], ps[r, 4 + 2 * (j % 2) + e, C:T], Y0[r, j, C:T], ALU.add)
                    if e == 0:
                        lk.done(ins)
                    else:
                        ins.then_inc(y_added, 1)

            def y_centre(j):
                dve.wait_ge(mean_made, j + 1)
                stt(Y0[:, j, :], ps[:, j % 2, :], -1.0 / 64, Y0[:, j, :], ALU.mult, ALU.add).then_inc(centred, 1)

            def y_finish(j):
                dve.wait_ge(y_root, j + 1)
                rs = ytmp[j % 2][1]
                lk.done(dve.reciprocal(rs, rs))
                y = Y0[:, j, :]
                lk.done(tt(y, y, rs, ALU.mult))
                lk.done(ts(y, y, col("lnx_w", j), col("lnx_b", j), ALU.mult, ALU.add))
                lk.done(tt(y, y, BON[:, j, :], ALU.add))
                dve.wait_ge(g_made, j + 1)
                tt(y, ps[:, 4 + 2 * (j % 2), :], y, ALU.mult).then_inc(y_final, 1)

            for t in range(10):
                if 0 <= t - 2 < 8:
                    y_finish(t - 2)
                if t < 8:
                    y_add(t)
                if 0 <= t - 1 < 8:
                    y_centre(t - 1)

            def gated(phase, first, gate, merged):
                for i in range(8):
                    g, hf = divmod(i, 2)
                    dve.wait_ge(half_done, 2 * FIRST[phase] + 4 * g + 2 + hf + 1)
                    dve.wait_ge(freed["A"], BEFORE[phase]["A"] + i + 1)
                    if first:
                        tt(merged[:, i, :], ps[:, 2 + i % 2, :], gate[:, i % 2, :], ALU.mult).then_inc(freed["D"], 1)
                    else:
                        lk.done(tt(gate[:, i % 2, :], ps[:, 2 + i % 2, :], gate[:, i % 2, :], ALU.mult))
                        tt(merged[:, i, :], merged[:, i, :], gate[:, i % 2, :], ALU.add).then_inc(freed["D"], 1)

            gated("rw_out", True, gate, merged)
            if stop < 3:
                return
            dve.wait_ge(freed["A"], BEFORE["qk"]["A"])
            for i in range(12):
                dve.wait_ge(half_done, 2 * FIRST["qk"] + 2 * i + 2)
                dve.tensor_copy(QK[:, 2 * i + 1, :], ps[:, (2 * i + 1) % 4, :]).then_inc(freed["D"], 1)
            for i in range(6):
                dve.wait_ge(half_done, 2 * FIRST["v"] + 2 * i + 2)
                dve.tensor_copy(VT[:, 2:4, i * 256:i * 256 + 256],
                                ps[:, (2 * i + 1) % 4, :].rearrange("p (a b) -> p a b", b=256)).then_inc(freed["D"], 1)

            def attend(u0, us, parts_of, prob, otok):
                def peaks(i):
                    u = u0 + i
                    pt = parts_of(us[i], i)
                    dve.wait_ge(scored, u + 1)
                    if u >= 2:
                        dve.wait_ge(turned, TURNED[u - 2])
                    o = 0
                    for g, (_, _, bk, n_) in enumerate(pt["scores"]):
                        ins = dve.tensor_tensor_reduce(out=prob[u % 2][:, o:o + n_], in0=ps[:, bk, 0:n_], in1=pt["masks"][g],
                                                       scale=1.0, scalar=NEG, op0=ALU.add, op1=ALU.max,
                                                       accum_out=PK[:, u % 2, g:g + 1])
                        o += n_
                        if g == len(pt["scores"]) - 1:
                            ins.then_inc(masked, 1)
                        else:
                            lk(ins)
                    dve.wait_ge(masked, u + 1)
                    if len(pt["scores"]) > 1:
                        dve.wait_ge(dve_link, lk.n)
                    lk.done(dve.tensor_reduce(PK[:, u % 2, 3:4], PK[:, u % 2, 0:len(pt["scores"])], AX.X, ALU.max))
                    ts(NM[:, u % 2:u % 2 + 1], PK[:, u % 2, 3:4], -pt["scale"], None, ALU.mult).then_inc(peaked, 1)

                def outs(i):
                    u = u0 + i
                    w = u // 8
                    pt = parts_of(us[i], i)
                    dve.wait_ge(probbed, u + 1)
                    lk.done(dve.reciprocal(RD[:, u % 2:u % 2 + 1], DEN[:, u % 2:u % 2 + 1]))
                    dve.wait_ge(weighed, u + 1)
                    if i % 8 == 0 and w >= 2:
                        dve.wait_ge(oturned, w - 1)
                    ts(otok[w % 2][:, pt["out"]], ps[:, 6 + u % 2, 0:64], RD[:, u % 2:u % 2 + 1], None, ALU.mult).then_inc(outed, 1)

                peaks(0)
                for i in range(len(us)):
                    if i + 1 < len(us):
                        peaks(i + 1)
                    outs(i)

            dve.wait_ge(got_masks, 16)
            attend(0, units, parts1, PROB1[0], PROB1[2])
            gated("at_out", False, gate, merged)
            if stop < 4:
                return

            dve.wait_ge(got_x1, 16)

            def residual(phase, gcol, wait_to=None):
                for i in range(8):
                    if phase == "down":
                        dve.wait_ge(half_done, 2 * FIRST[phase] + 6 * (i // 2) + 4 + i % 2 + 1)
                    else:
                        dve.wait_ge(half_done, 2 * FIRST[phase] + i + 1)
                    stt(xT[:, i, :], ps[:, i % 4, :], mod[:, gcol + i:gcol + i + 1], xT[:, i, :],
                        ALU.mult, ALU.add).then_inc(freed["D"], 1)

            residual("w_o", 16)
            gain(1, col("norm2_w", 0, 8))
            norm_apply(1, xT, GAIN, mod[:, 24:32], hT)

            D0, H0 = BEFORE["up"]["D"], 2 * FIRST["up"]

            def up_slot(jj, cb, lbase):
                for g in range(2):
                    dst, bank = cvt[jj % 2][g], (2 * jj + g) % 4
                    dve.wait_ge(convd, 2 * cb(jj) + (g + 1) if isinstance(cb(jj), int) else cb(jj) * 2 + (g + 1))
                    stt(dst[:, 1:T], ps[:, bank, 0:T - 1], up_col(1, g, jj, cb), dst[:, 1:T], ALU.mult, ALU.add).then_inc(dve_link, 1)
                    dve.wait_ge(dve_link, lbase(g + 1))
                    stt(dst[:, 2:T], ps[:, bank, 0:T - 2], up_col(0, g, jj, cb), dst[:, 2:T], ALU.mult, ALU.add).then_inc(freed["D"], 1)
                dve.wait_ge(silud, cb(jj) + 1)
                dve.wait_ge(freed["D"], (cb(jj) * 2) + (D0 + 2))
                i = cb(jj)
                h_out = hid[:, i, :] if isinstance(i, int) else hid[:, bass.ds(i, 1), :].rearrange("p a t -> p (a t)")
                tt(h_out, sil[:, jj % 2, :], cvt[jj % 2][1], ALU.mult).then_inc(hidd, 1)

            def up_col(tap, g, jj, cb):
                base = COL_AT["conv_w"] + tap * 44 + g * FT
                i = cb(jj)
                return cols[:, base + i:base + i + 1] if isinstance(i, int) else cols[:, bass.ds(i + base, 1)]

            l0 = lk.n
            for jj in range(2):
                up_slot(jj, lambda v: v, lambda v: l0 + 2 * jj + v)
            with dve.Fori(0, 5) as i:
                for jj in range(2, 2 + R):
                    up_slot(jj, lambda v: i * 4 + v, lambda v: i * 8 + (l0 + 2 * jj + v))
            lk.n = l0 + 44
            residual("down", 40)
            norm_apply(2, xT, col("norm_f_w", 0, 8), None, xT)

            if stop < 5:
                return
            modulation("ada2", col("b_ada_2", 0, 48))
            gain(0, col("g_mix_2", 0, 8))
            ts(ONE, ZERO, 1.0, None, ALU.add).then_inc(freed["D"], 1)
            norm_apply(3, xT, GAIN, mod[:, 0:8], hT)
            dve.wait_ge(got_pos, 32)
            ROUND = 12582912.0
            C1 = 6.28125
            C2 = float(np.float32(int((2 * np.pi - C1) * 2 ** 22) / 2 ** 22))
            C3 = float(2 * np.pi - C1 - C2)
            PI_ = float(np.nextafter(np.float32(np.pi), np.float32(0)))
            lk.done(dve.tensor_copy(ANG[:, 2, :], ANG[:, 3, :].bitcast(I32)))
            lk.done(ts(ANG[:, 2, :], ANG[:, 2, :], cst("freq"), None, ALU.mult))
            for i_, quarter in enumerate((0.0, 0.25)):
                o_, tr = ANG[:, i_, :], ANG[:, 3, :]
                lk.done(ts(tr, ANG[:, 2, :], 1.0 / (2 * np.pi), quarter, ALU.mult, ALU.add))
                lk.done(ts(tr, tr, ROUND, -ROUND, ALU.add, ALU.add))
                lk.done(stt(o_, tr, -C1, ANG[:, 2, :], ALU.mult, ALU.add))
                lk.done(stt(o_, tr, -C2, o_, ALU.mult, ALU.add))
                lk.done(stt(o_, tr, -C3, o_, ALU.mult, ALU.add))
                lk.done(ts(o_, o_, quarter * 2 * np.pi, PI_, ALU.add, ALU.min))
                ins = ts(o_, o_, -PI_, None, ALU.max)
                if i_ == 0:
                    lk.done(ins)
                else:
                    ins.then_inc(angled, 1)
            dve.wait_ge(rotated, 1)
            lk.done(ts(SIN, ANG[:, 0, :], cst("rotsign"), None, ALU.mult))
            lk.done(dve.tensor_copy(COS, ANG[:, 1, :]))
            dve.wait_ge(got_bias, 16)
            for h in range(8):
                lk.done(stt(BT[:, h, :], BT[:, h, :], 8.0, CH, ALU.mult, ALU.add))

            in2_value = lambda o: o + 1 if o < 4 else o + 2
            tok2 = lambda v: v.rearrange("p (a b) -> p a b", b=256)

            def psum_out(phase, dst, src, v):
                dve.wait_ge(half_done, 2 * FIRST[phase] + v)
                dve.tensor_copy(dst, src).then_inc(freed["D"], 1)

            IN2 = [QL[:, 0, :], QL[:, 1, :], KV, KR, KRS] + [QB[:, j, :] for j in range(4)] + [KB[:, j, :] for j in range(4)]
            for o in range(1, 13, 2):
                psum_out("in2", IN2[o], ps[:, o % 4, :], in2_value(o))
            for o in (13, 15):
                c, hf = divmod(o - 13, 2)
                psum_out("in2", VB[:, 2 * hf:2 * hf + 2, c * 256:c * 256 + 256], tok2(ps[:, o % 4, :]), in2_value(o))
            dve.wait_ge(lat_root, 2)
            lk.done(dve.reciprocal(LRT, LRT))
            lk.done(stt(QL[:, 0, :], QL[:, 0, :], col("g_q_2", 0), LRT[:, 0, :], ALU.mult, ALU.mult))
            lk.done(stt(QL[:, 1, :], QL[:, 1, :], col("g_q_2", 1), LRT[:, 0, :], ALU.mult, ALU.mult))
            stt(KV, KV, col("g_kv_2"), LRT[:, 1, :], ALU.mult, ALU.mult).then_inc(lat_ready, 1)
            r = slice(64, 96)
            dve.wait_ge(freed["A"], BEFORE["in2"]["A"] + 3)
            dve.wait_ge(freed["D"], BEFORE["in2"]["D"] + 2)
            lk.done(tt(KR[r], KR[r], COS[r], ALU.mult))
            lk.done(tt(KRS[r], KRS[r], SIN[r], ALU.mult))
            lk.done(tt(KR[r], KR[r], KRS[r], ALU.add))
            lk.done(dve.tensor_copy(KA[r], rep(KR[r], 8)))
            for h in range(8):
                dve.wait_ge(half_done, 2 * FIRST["lat2"] + 2 * h + 2)
                tt(ROT[r, h % 2, :], ps[r, (2 * h + 1) % 4, :], SIN[r], ALU.mult).then_inc(freed["D"], 1)
                dve.wait_ge(freed["A"], BEFORE["lat2"]["A"] + h + 1)
                dve.wait_ge(freed["D"], BEFORE["lat2"]["D"] + h + 1)
                lk.done(tt(QA[r, h, :], QA[r, h, :], COS[r], ALU.mult))
                lk.done(tt(QA[r, h, :], QA[r, h, :], ROT[r, h % 2, :], ALU.add))
            for o in range(17, 24, 2):
                psum_out("lat2", KA[0:64, o - 16, :], ps[0:64, o % 4, :], o + 1)
            for o in (25, 27):
                c, hf = divmod(o - 24, 2)
                psum_out("lat2", VA[:, 2 * hf:2 * hf + 2, c * 256:c * 256 + 256], tok2(ps[:, o % 4, :]), o + 1)
            ts(ONE, ZERO, 1.0, None, ALU.add).then_inc(band_ready, 1)
            attend(32, units, parts_mla, PROB2[0], PROB2[2])
            attend(64, units, parts_band, PROB2[0], PROB2[2])
            gated("mla_out", True, gate2, merged2)
            gated("band_out", False, gate2, merged2)
            residual("w_out2", 16)
            gain(1, col("g_ffn_2", 0, 8))
            norm_apply(4, xT, GAIN, mod[:, 24:32], hT)
            if stop < 6:
                return
            dve.wait_ge(routed, 1)
            t4 = lambda v, k: v[:, 0:4 * k].rearrange("p (t k) -> p t k", k=k)
            lk.done(tt(RL, ps[:, 7, 0:144].rearrange("p (t c) -> p t c", c=36), rep(BRT, 4), ALU.add))
            LG, LE = RL[:, :, 0:4], RL[:, :, 4:36]
            red = lambda o_, i_, op: lk.done(dve.tensor_reduce(o_, i_, AX.X, op))
            rank = lambda k: cst("rank")[:, 0:k].unsqueeze(1).broadcast_to([P, 4, k])
            GM, M1, M2, MX, GS = [rt_[0][:, 4 * i:4 * i + 4] for i in range(5)]

            def first_max(dst, scratch, x, mx, k):
                lk.done(tt(scratch, x, bc(mx, k), ALU.is_equal))
                lk.done(tt(scratch, scratch, rank(k), ALU.mult))
                red(MX, scratch, ALU.max)
                lk.done(tt(dst, scratch, bc(MX, k), ALU.is_equal))

            red(GM, LG, ALU.max)
            OG, SCR4, SCR8, O1, O2, E2 = t4(rt_[1], 4), t4(rt_[2], 4), t4(rt_[3], 8), t4(rt_[4], 8), t4(rt_[5], 8), t4(rt_[6], 8)
            first_max(OG, SCR4, LG, GM, 4)
            ES = t4(rt_[7], 8)
            WIDE = rt_[8][:, 0:128].rearrange("p (t g e) -> p t g e", g=4, e=8)
            for tt_ in range(4):
                lk.done(tt(WIDE[:, tt_], LE[:, tt_].rearrange("p (g e) -> p g e", e=8), bc(OG[:, tt_], 8), ALU.mult))
            for tt_ in range(4):
                red(ES[:, tt_], WIDE[:, tt_].rearrange("p g e -> p e g"), ALU.add)
            red(M1, ES, ALU.max)
            first_max(O1, SCR8, ES, M1, 8)
            lk.done(stt(E2, O1, NEG, ES, ALU.mult, ALU.add))
            red(M2, E2, ALU.max)
            first_max(O2, SCR8, E2, M2, 8)
            ex = rt_e.rearrange("p (t k) -> p t k", k=5)
            lk.done(tt(ex[:, :, 0:4], LG, bc(GM, 4), ALU.subtract))
            tt(ex[:, :, 4], M2, M1, ALU.subtract).then_inc(route_exp, 1)
            dve.wait_ge(route_exp, 2)
            red(GS, ex[:, :, 0:4], ALU.add)
            W1, W2 = rt_[9][:, 0:4], rt_[9][:, 4:8]
            lk.done(ts(W1, ex[:, :, 4], 1.0, None, ALU.add))
            lk.done(tt(W1, W1, GS, ALU.mult))
            lk.done(dve.reciprocal(W1, W1))
            lk.done(tt(W2, W1, ex[:, :, 4], ALU.mult))
            for tt_ in range(4):
                lk.done(dve.tensor_copy(WGT[:, 2 * tt_:2 * tt_ + 1], W1[:, tt_:tt_ + 1]))
                lk.done(dve.tensor_copy(WGT[:, 2 * tt_ + 1:2 * tt_ + 2], W2[:, tt_:tt_ + 1]))
            for F_, O_ in ((F1, O1), (F2, O2)):
                for tt_ in range(4):
                    lk.done(tt(F_[:, tt_].rearrange("p (g e) -> p g e", e=8), bc(OG[:, tt_], 8), rep(O_[:, tt_], 4), ALU.mult))
            tt(SEL, F1, F2, ALU.add).then_inc(selected, 1)
            dve.wait_ge(ranked, 1)
            dve.wait_ge(counted, 1)
            lk.done(dve.tensor_copy(RK, ps[:, 6, 0:128].rearrange("p (t e) -> p t e", e=32)))
            lk.done(dve.tensor_reduce(NRD[:, 1:2], ps[:, 3, 0:32], AX.X, ALU.max))
            lk.done(ts(NRD[:, 1:2], NRD[:, 1:2], 1.0 / SLOTS, (SLOTS - 1.0) / SLOTS - 0.5 + 0.5 / SLOTS, ALU.mult, ALU.add))
            lk.done(ts(NRD[:, 1:2], NRD[:, 1:2], ROUND, -ROUND, ALU.add, ALU.add))
            dve.tensor_copy(NRD[:, 0:1].bitcast(I32), NRD[:, 1:2]).then_inc(rounds_ready, 1)
            far = 4096.0
            lk.done(stt(RM[:, :, 0:32], SEL, -far, RK, ALU.mult, ALU.add))
            lk.done(ts(RM[:, :, 0:32], RM[:, :, 0:32], far, None, ALU.add))
            lk.done(ts(RM[:, :, 32:33], RM[:, :, 0:1], -float(SLOTS), None, ALU.add))
            for b in range(2):
                ts(SINK[:, 4 + b:5 + b], ZERO, 1.0, None, ALU.add).then_inc(copied["D"], 1)
                ts(SINK[:, 6 + b:7 + b], ZERO, 1.0, None, ALU.add).then_inc(down_made, 1)
                ts(SINK[:, 8 + b:9 + b], ZERO, 1.0, None, ALU.add).then_inc(gu_done, 1)

            def place(col_, par):
                rank_ = RM[:, :, col_:col_ + 1] if isinstance(col_, int) else RM[:, :, bass.ds(col_, 1)]
                tt(PE_[:, par], SLOT_NO.unsqueeze(1).broadcast_to([P, 4, SLOTS]), rank_.broadcast_to([P, 4, SLOTS]),
                   ALU.is_equal).then_inc(placed, 1)

            place(0, 0)
            two = lambda ap: ap.rearrange("p (t w) -> p t w", w=2)
            for w, F_ in enumerate((F1, F2)):
                lk.done(tt(SEL, F_, RK, ALU.mult))
                red(two(RANK2)[:, :, w], SEL, ALU.add)
                lk.done(tt(F_, F_, rep(ROWS, 4), ALU.mult))
                red(two(ROW0)[:, :, w], F_, ALU.add)
            lk.done(dve.memset(GX, 0.0))
            dve.wait_ge(rounds_ready, 1)
            rounds = dve.value_load(NRD[0:1, 0:1].bitcast(I32), min_val=1, max_val=T // SLOTS)

            def mix_second(r, tt_):
                dve.wait_ge(half_mixed, r * 4 + (tt_ + 1))
                stt(GX[:, tt_, :], GY[:, 2 * tt_ + 1, :], WGT_IN[:, 2 * tt_ + 1:2 * tt_ + 2], GX[:, tt_, :],
                    ALU.mult, ALU.add).then_inc(mixed, 1)

            with dve.Fori(0, rounds) as r:
                ts(RANK_IN, RANK2, 0.0, SLOTS - 1.0, ALU.max, ALU.min).then_inc(round_link, 1)
                dve.wait_ge(round_link, r * 5 + 1)
                tt(IDX, RANK_IN, ROW0, ALU.add).then_inc(indexed, 1)
                tt(WGT_IN, RANK_IN, RANK2, ALU.is_equal).then_inc(round_link, 1)
                dve.wait_ge(round_link, r * 5 + 2)
                tt(WGT_IN, WGT_IN, WGT, ALU.mult).then_inc(round_link, 1)
                ts(RANK2, RANK2, -float(SLOTS), None, ALU.add).then_inc(round_link, 1)
                with dve.Fori(0, 8) as i:
                    for j in range(4):
                        par = j % 2
                        step = r * 32 + i * 4 + j
                        dve.wait_ge(gu_done, step * 2 + 2)
                        place(i * 4 + (j + 1), 1 - par)
                        dve.wait_ge(gu_done, step * 2 + 4)
                        dve.wait_ge(silu_m, step + 1)
                        tt(MH[:, par].rearrange("p f s -> p (f s)"), ps[:, 2 + par, 2 * SLOTS:4 * SLOTS], SG[:, par, :],
                           ALU.mult).then_inc(mhid, 1)
                        dve.wait_ge(down_made, step + 3)
                        dve.wait_ge(y_stored[par], r * 256 + i * 32 + (j // 2 * 16 + 16))
                        dve.tensor_copy(YO[0:SLOTS, par, 512:D], ps[0:SLOTS, 5 + 2 * par, :]).then_inc(copied["D"], 1)
                dve.wait_ge(placed, r * 32 + 33)
                ts(RM, RM, -float(SLOTS), None, ALU.add).then_inc(round_link, 1)
                dve.wait_ge(round_link, r * 5 + 5)
                for tt_ in range(4):
                    dve.wait_ge(fetched[tt_], r * 32 + 32)
                    stt(GX[:, tt_, :], GY[:, 2 * tt_, :], WGT_IN[:, 2 * tt_:2 * tt_ + 1], GX[:, tt_, :],
                        ALU.mult, ALU.add).then_inc(half_mixed, 1)
                    if tt_ >= 1:
                        mix_second(r, tt_ - 1)
                mix_second(r, 3)
            for k in range(KT):
                dve.wait_ge(mix_turned, k + 1)
                stt(xT[:, k, :], ps[:, 2 + k % 2, :], mod[:, 40 + k:41 + k], xT[:, k, :], ALU.mult, ALU.add).then_inc(freed["D"], 1)
            dve.wait_ge(rooted, 6)
            dve.wait_ge(rooted, 6)
            dve.reciprocal(RSTD, RSTD).then_inc(tail_link, 1)
            dve.wait_ge(tail_link, 1)
            tt(hT, xT, rep(RSTD, KT), ALU.mult).then_inc(tail_link, 1)
            dve.wait_ge(tail_link, 2)
            for k in range(KT):
                ts(hT[:, k, :], hT[:, k, :], col("g_final_2", k), None, ALU.mult).then_inc(out_scaled, 1)


def kernel(**inputs):
    import numpy as _np
    import concourse.bacc as _bacc
    from concourse import mybir as _mybir
    from concourse.bass_utils import run_bass_kernel_spmd as _run

    arrays = layout({k: _np.asarray(v) for k, v in inputs.items()})
    nc = _bacc.Bacc("TRN2", target_bir_lowering=False, num_devices=1)
    aps = {}
    for name, v in arrays.items():
        aps[name] = nc.dram_tensor(f"in_{name}", v.shape, _mybir.dt.from_np(v.dtype), kind="ExternalInput").ap()
    aps["out"] = nc.dram_tensor("out_0", (D, T), F32, kind="ExternalOutput").ap()
    aps["y_scratch"] = nc.dram_tensor("y_scratch", (32 * SLOTS, D), F32, kind="Internal").ap()
    aps["bias_scratch"] = nc.dram_tensor("bias_scratch", (8, P, 640), F32, kind="Internal").ap()
    build(nc, aps)
    r = _run(nc, [{f"in_{k}": v for k, v in arrays.items()}], core_ids=[0])
    return _np.ascontiguousarray(r.results[0]["out_0"].T)[None]


def layout(x):
    def columns(v):
        v = v.reshape(-1)
        pad = -v.size % P
        return np.concatenate([v, np.zeros(pad, v.dtype)]).reshape(-1, P).T if pad else v.reshape(-1, P).T

    parts = []
    for name, n in COLS:
        key = "mu_shift" if name == "mu" else name
        parts.append(columns(x[key]))
        assert parts[-1].shape[1] == n, name
    arrays = {"cols": np.ascontiguousarray(np.concatenate(parts, axis=1)), "consts": CONSTS,
              "x": np.ascontiguousarray(x["x"][0].T),
              "positions": np.ascontiguousarray(x["positions_2"]),
              "rel_reversed": np.ascontiguousarray(x["rel_bias_2"][0][:, ::-1])}
    swap = np.r_[0:64, 80:96, 64:80]
    uq = x["w_uq_2"][0].reshape(256, 8, 96)
    arrays["w_uq"] = np.zeros((256, 8, 2, P), uq.dtype)
    arrays["w_uq"][:, :, 0, :96] = uq
    arrays["w_uq"][:, :, 1, :96] = uq[:, :, swap]
    arrays["w_uq"] = arrays["w_uq"].reshape(256, 2048)
    kvr = np.zeros((D, 3, P), uq.dtype)
    kvr[:, 0] = x["w_in_2"][0][:, 256:384]
    kvr[:, 1, 64:96] = x["w_in_2"][0][:, 384:416]
    kvr[:, 2, 64:96] = x["w_in_2"][0][:, np.r_[400:416, 384:400]]
    arrays["w_kvr"] = kvr.reshape(D, 384)
    for name in ("w_ada", "w_in", "w2", "a2", "g2", "w_att_out", "w_rwkv_out", "w_o", "w_up", "w_down", "w_ada_2",
                 "w_in_2", "w_uk_2", "w_uv_2", "w_oa_2", "w_ob_2", "w_out_2", "w_rg_2", "w_re_2", "w_gate_2",
                 "w_up_2", "w_down_2"):
        arrays[name] = np.ascontiguousarray(x[name][0])
    arrays["b_router"] = np.ascontiguousarray(np.concatenate([x["b_rg_2"], x["b_re_2"]], axis=1))
    return arrays
```

```python
from contextlib import ExitStack

import numpy as np
import concourse.bass as bass
from concourse import mybir

F32 = mybir.dt.float32
F32R = mybir.dt.float32r
I32 = mybir.dt.int32
ACT = mybir.ActivationFunctionType
ALU = mybir.AluOpType
AX = mybir.AxisListType

P = 128
T = 512
D = 1024
KT = D // P
R = 4
SLOT = 2048
EPS = 1e-6
GN_EPS = 64e-5
KAPPA = float(np.exp(-0.5))
C = 64
NCH = T // C
LEVELS = (2, 4, 8, 16, 32)
NEG = -1e30
SLOTS = 64
FF = 2816
FT = FF // P

COLS = [("b_ada", 48), ("norm1_w", 8), ("b_gate", 16), ("mu", 27), ("w0", 8), ("a0", 8), ("k_k", 8), ("k_a", 8),
        ("r_k", 8), ("lnx_w", 8), ("lnx_b", 8), ("norm2_w", 8), ("conv_w", 132), ("conv_b", 44), ("norm_f_w", 8),
        ("c", 8), ("c_2", 8), ("b_ada_2", 48), ("g_mix_2", 8), ("g_q_2", 2), ("g_kv_2", 1), ("g_ffn_2", 8),
        ("g_final_2", 8)]
COL_AT, NCOL = {}, 0
for _name, _n in COLS:
    COL_AT[_name] = NCOL
    NCOL += _n


def shape_constants():
    p = np.arange(P)[:, None]
    parts = []
    at = {}

    def add(name, a):
        at[name] = (sum(x.shape[1] for x in parts), a.shape[1])
        parts.append(np.ascontiguousarray(a, dtype=np.float32))

    add("ident", (p == np.arange(P)[None, :]))
    add("ones", np.ones((P, P)))
    add("headones", (p // 64 == np.arange(P)[None, :] // 64))
    q, s = p % 64, np.arange(64)[None, :]
    add("eye64", q == s)
    add("upper", q < s)
    add("upto", q <= s)
    add("pair1", (q // 2 == s // 2) & (s < q))
    add("pair1T", (q // 2 == s // 2) & (q < s))
    for b in LEVELS:
        add(f"level{b}", (q // (2 * b) == s // (2 * b)) & (q // b % 2 == 0) & (s // b % 2 == 1))
    add("restart", np.broadcast_to((np.arange(T) % C != 0)[None, :], (P, T)))
    inv = (10000.0 ** (-np.arange(16, dtype=np.float32) / np.float32(16))).astype(np.float32)
    add("freq", inv[np.arange(P) % 16][:, None])
    add("rotsign", np.where(p % 32 < 16, -1.0, 1.0))
    add("rank", np.broadcast_to(8.0 - np.arange(8)[None, :], (P, 8)))
    w = np.arange(256)[None, :]
    add("near", np.where((w >= p) & (w <= p + 128), 0.0, NEG))
    w = np.arange(T)[None, :]
    back = p - w + 384
    add("every4", np.where((back >= 0) & (back % 4 == 0), 0.0, NEG))
    add("every16", np.where((back >= 0) & (back % 16 == 0), 0.0, NEG))
    add("chunked", np.where(p // 64 >= w // 64 - 6, 0.0, NEG))
    add("before", p < np.arange(P)[None, :])
    add("slots", np.broadcast_to(np.arange(SLOTS)[None, :], (P, SLOTS)))
    add("rows", np.broadcast_to(SLOTS * np.arange(32)[None, :], (P, 32)))
    return np.concatenate(parts, axis=1), at


CONSTS, CONST_AT = shape_constants()
NCONST = CONSTS.shape[1]


PHASES = [("ada1", 24), ("lora", 2), ("rkv", 12), ("rw_out", 8), ("qk", 12), ("v", 6), ("at_out", 8), ("w_o", 4),
          ("up", 22), ("down", 12), ("ada2", 24), ("in2", 9), ("lat2", 14), ("mla_out", 8), ("band_out", 8),
          ("w_out2", 4), ("moe", 96)]
FIRST, _n = {}, 0
for _name, _k in PHASES:
    FIRST[_name] = _n
    _n += _k

STREAMED = (1, 0, 2)

PRODUCTS = [("lora", "A"), ("ssq", "A"), ("bonus", "D"), ("tv", "AD"), ("tat", "AD"), ("tbh", "AD"), ("tkh", "AD"),
            ("ab", "D"), ("abT", "D"), ("akT", "D"), ("rbT", "D"), ("rkT", "D")]
for _b in LEVELS:
    PRODUCTS += [(f"y{_b}", "AD")] + ([(f"x{_b}", "D")] if _b != LEVELS[-1] else []) + [(f"xT{_b}", "D")]
PRODUCTS += [("w1", "AD"), ("sav", "AD"), ("z", "AD"), ("r", "D"), ("y0", "AD"), ("g", "D"), ("h", "AD")]
PNAMES = [n for n, _ in PRODUCTS]
PER_QUAD = {e: 2 * sum(e in who for _, who in PRODUCTS) for e in "AD"}


def emptied(quad, product, sub, engine):
    i = PNAMES.index(product)
    n = 2 * sum(engine in who for _, who in PRODUCTS[:i])
    if engine in PRODUCTS[i][1]:
        n += sub + 1
    else:
        n += 0
    return quad * PER_QUAD[engine] + n


class Link:

    def __init__(self, eng, sem):
        self.eng, self.sem, self.n, self.off = eng, sem, 0, 0

    def __call__(self, ins):
        ins.then_inc(self.sem, 1)
        self.n += 1
        return self.n + self.off

    def done(self, ins):
        self.eng.wait_ge(self.sem, self(ins))


def build(nc, a):
    with ExitStack() as ctx:
        offset_of = {}

        def sb(name, shape, dt=F32):
            offset_of[name] = -(-nc.sbuf_base // 32) * 32
            return ctx.enter_context(nc.sbuf_tensor(name, shape, dt))

        def sem(name):
            return ctx.enter_context(nc.semaphore(name))

        ring = sb("ring", [P, R, SLOT])
        const = sb("const", [P, CONST_AT["near"][0]])
        cols = sb("cols", [P, NCOL])
        mod = sb("mod", [P, 48])[:, :]
        small = sb("small", [P, 160])
        hT = sb("hT", [P, KT, T])[:, :, :]
        arena = sb("arena", [P, 37888])
        ps = ctx.enter_context(nc.psum_tensor("ps", [P, 8, 512], F32))

        def area(at, *dims):
            n = int(np.prod(dims))
            v = arena[:, at:at + n]
            if len(dims) == 1:
                return v
            if len(dims) == 2:
                return v.rearrange("p (a b) -> p a b", b=dims[1])
            return v.rearrange("p (a b c) -> p a b c", b=dims[1], c=dims[2])

        def cst(name):
            o, n = CONST_AT[name]
            return const[:, o:o + n]

        def col(name, i=0, n=1):
            return cols[:, COL_AT[name] + i:COL_AT[name] + i + n]

        ident, ones, headones, eye64 = cst("ident"), cst("ones"), cst("headones"), cst("eye64")

        MROW = area(12288, 4, 256)
        x_in = area(20480, KT, T)
        RT, Y0 = area(0, 8, T), area(4096, 8, T)
        GT = area(8192, 8, NCH, C)
        ST = area(12288, NCH, 8, C)
        BON = area(16384, 8, T)
        tmp = [[area(20480 + (s * 14 + i) * T, T) for i in range(14)] for s in range(2)]
        LOW = area(34816, T)
        GLO, GLO2 = area(35328, T), area(35840, T)
        W2A2 = area(36352, D)
        G2 = area(20480, 2, D)
        ytmp = [[area(22528 + (s * 3 + i) * T, T) for i in range(3)] for s in range(2)]
        merged = area(30720, KT, T)
        gate = area(28416, 2, T)
        QK = area(0, 24, T)
        VT = area(12288, 4, 1536)
        masks = area(18432, 1792)
        near, every4, every16 = masks[:, 0:256], masks[:, 256:768], masks[:, 768:1280]
        xT = area(0, KT, T)
        cvt = [[area(16384 + (s * 2 + i) * T, T) for i in range(2)] for s in range(2)]
        sil = area(18432, 2, T)

        def rounded(name, at, *shape):
            return nc.alloc_sbuf_tensor_at(name, [P, *shape], F32R, offset=at)

        H_HIGH = rounded("h_high", offset_of["arena"] + 19456 * 4, KT, T)
        H_LOW = rounded("h_low", offset_of["hT"], KT, T)
        W_HIGH = rounded("w_high", offset_of["arena"] + 23552 * 4, 2, SLOT)
        HID_HIGH = rounded("hid_high", offset_of["arena"] + 4096 * 4, FT, T)
        HID_LOW = (rounded("hid_low_first", offset_of["arena"] + 15360 * 4, 2, T),
                   rounded("hid_low_rest", offset_of["arena"] + 27648 * 4, FT - 2, T))
        W_LOW = rounded("w_low", offset_of["ring"], R, SLOT)

        QL, KV = area(4096, 2, T), area(5120, T)
        KR, KRS = area(5632, T), area(6144, T)
        QA, KA = area(6656, 8, T), area(10752, 8, T)
        VA = area(14848, 4, T)
        QB, KB, VB = area(16896, 4, T), area(18944, 4, T), area(20992, 4, T)
        BT = area(23040, 8, T)
        CH = area(27136, T)
        COS, SIN = area(27648, T), area(28160, T)
        PROB2 = ([area(28672 + i * T, T) for i in range(2)], [area(at, T) for at in (29696, 36352)],
                 [area(30208 + i * T, T) for i in range(2)])
        OA, OB = area(31232, 4, T), area(33280, 4, T)
        LSQ, LRT = area(35328, 3, T), area(36864, 2, T)
        ROT = area(35328, 2, T)
        ANG = area(31232, 4, T)
        BROW = area(33280, 640)
        merged2, gate2 = area(6656, KT, T), area(4096, 2, T)
        H2T = area(4096, 4, D)
        XE = area(8192, 2, 8, 2 * SLOTS)
        PICKED = area(10240, 2, 4, 2 * SLOTS)
        SG, MH = area(11264, 2, 2 * SLOTS), area(11520, 2, 2, SLOTS)
        YO = area(12288, 2, D)
        WR, BRT = area(12288, KT, 36), area(12576, 36)
        RL = area(12672, 4, 36)
        rt_ = [area(12832 + 160 * i, 160) for i in range(12)]
        C2S = small[:, 88:96]
        rt_e = area(14880, 20)
        MCON = area(14912, 224)
        BEF, SLOT_NO, ROWS = MCON[:, 0:128], MCON[:, 128:192], MCON[:, 192:224]
        SEL, F1, F2 = [area(15136 + 128 * i_, 4, 32) for i_ in range(3)]
        RK, RM = area(15520, 4, 32), area(15648, 4, 34)
        NRD, SINK = area(15844, 4), area(15848, 12)
        IDX = area(15796, 8).bitcast(mybir.dt.uint32)
        WGT, ROW0, RANK2, RANK_IN, WGT_IN = [area(15804 + 8 * i_, 8) for i_ in range(5)]
        GY, GX = area(16384, 8, D), area(24576, 4, D)
        EPSC, GNC, ZERO, ONE, ZSINK = [small[:, i:i + 1] for i in range(5)]
        NM, DEN, RD = small[:, 6:8], small[:, 8:10], small[:, 10:12]
        PK = small[:, 12:20].rearrange("p (a b) -> p a b", b=4)
        OMU, OKA, GAIN = small[:, 20:47], small[:, 48:56], small[:, 56:64]
        PLS = [small[:, 64:72], small[:, 72:80]]
        RSTD = sb("rstd", [P, T])[:, :]

        full = [sem(f"full{i}") for i in range(R)]
        half_done = sem("half_done")
        freed = {"A": sem("freed_by_act"), "D": sem("freed_by_dve")}
        act_link, dve_link, pool_link = sem("act_link"), sem("dve_link"), sem("pool_link")
        got_const, got_x, got_lora, got_g2, got_masks, got_x1 = [sem(n) for n in (
            "got_const", "got_x", "got_lora", "got_g2", "got_masks", "got_x1")]
        squared, summed, rooted, normed = sem("squared"), sem("summed"), sem("rooted"), sem("normed")
        mod_ready, row_copied, mod_turned = sem("mod_ready"), sem("row_copied"), sem("mod_turned")
        scaled = sem("scaled")
        lora_ready = sem("lora_ready")
        made = sem("made")
        emptA, emptD = sem("emptied_by_act"), sem("emptied_by_dve")
        chan, cum, decay, maskp = sem("chan_ready"), sem("cum_ready"), sem("decay_ready"), sem("masked_by_pool")
        stepped, state_ready = sem("stepped"), sem("state_ready")
        y_made, mean_made, var_made, g_made = sem("y_made"), sem("mean_made"), sem("var_made"), sem("g_made")
        y_added, centred, y_sq, y_root, y_final = [sem(n) for n in (
            "y_added", "centred", "y_squared", "y_rooted", "y_final")]
        gate_ready = sem("gate_ready")
        scored, masked, peaked, probbed, turned, turnedS, weighed, outed, oturned, oready = [sem(n) for n in (
            "scored", "masked", "peaked", "probbed", "turned", "turned_copied", "weighed", "outed",
            "out_turned", "out_ready")]
        h_piece, h_high, w_high, w_low = [sem(n) for n in ("h_piece", "h_high_made", "weights_high_made", "weights_low_made")]
        convd, silud, hidd = sem("conv_scaled"), sem("silu_ready"), sem("hidden_ready")
        silu_c, got_bias, got_pos, got_router = sem("silu_c"), sem("got_bias"), sem("got_positions"), sem("got_router")
        bias_row, bias_out = sem("bias_row"), sem("bias_out")
        lat_sq, lat_sum, lat_root, lat_ready = [sem("latent_" + n) for n in ("squared", "summed", "rooted", "ready")]
        angled, rotated, band_ready = sem("angled"), sem("sines"), sem("band_ready")
        routed, route_exp, h2_made, h2_ready, selected, ranked, counted, rounds_ready, indexed = [sem(n) for n in (
            "logits_made", "route_exp", "h2_made", "h2_ready", "selected", "ranked", "counted", "rounds_ready", "indexed")]
        gu_done, down_made, placed, gathered, xe_ready, silu_m, mhid = [sem(n) for n in (
            "gate_up_done", "down_made", "placed", "gathered", "tokens_ready", "moe_silu", "moe_hidden")]
        copied = {"A": sem("result_by_act"), "D": sem("result_by_dve")}
        y_stored = [sem("results_stored_even"), sem("results_stored_odd")]
        fetched = [sem(f"fetched{i}") for i in range(4)]
        mixed, mix_turned, round_link, half_mixed, round_held = [sem(n) for n in ("mixed", "mix_turned", "round_link", "half_mixed", "round_held")]
        tail_link, out_scaled = sem("tail_link"), sem("out_scaled")
        stored = sem("stored")

        HALVES = {"ada1": (0, 1), "lora": (0, 3), "rkv": (0, 24), "rw_out": (8, 8), "qk": (12, 12), "v": (6, 6),
                  "at_out": (8, 8), "w_o": (0, 8), "up": (0, 44), "down": (0, 8),
                  "ada2": (0, 1), "in2": (9, 8), "lat2": (14, 14), "mla_out": (8, 8), "band_out": (8, 8),
                  "w_out2": (0, 8), "moe": (0, 8)}
        BEFORE, na, nd = {}, 0, 0
        for ph, _k in PHASES:
            BEFORE[ph] = {"A": na, "D": nd}
            x_, y_ = HALVES.get(ph, (0, 0))
            na, nd = na + x_, nd + y_

        def full_value(m):
            up0, up1 = FIRST["up"], FIRST["up"] + 22
            ups = sum(1 for x in range(up0, min(m, up1 - 1) + 1) if x % R == m % R)
            return 16 * (m // R + 1 + ups)

        def drain_psum(pe, phase):
            for e in "AD":
                if BEFORE[phase][e]:
                    pe.wait_ge(freed[e], BEFORE[phase][e])

        def bc(v, n):
            return v.unsqueeze(2).broadcast_to([v.shape[0], v.shape[1], n])

        def rep(v, n):
            return v.unsqueeze(1).broadcast_to([v.shape[0], n, v.shape[1]])

        def chunks(v):
            return v.rearrange("p (c k) -> p c k", k=C)

        units = [(qt, h) for qt in range(4) for h in range(8)]
        PROB1 = ([area(20224 + i * 1280, 1280) for i in range(2)], [area(22784 + i * 1280, 1280) for i in range(2)],
                 [area(25344 + i * T, T) for i in range(2)])
        OT1 = area(26368, 4, T)

        def parts1(unit, i):
            qt, h = unit
            r = slice(h % 2 * 64, h % 2 * 64 + 64)
            k0 = max(0, qt - 1) * P
            scores, vals, maskl = [], [], []
            for g in range(3):
                lo, hi = (k0 if g == 0 else 0), (qt + 1) * P
                qT, kT = QK[r, g * 8 + h // 2, qt * P:qt * P + P], QK[r, g * 8 + 4 + h // 2, lo:hi]
                scores.append((g, [(qT, kT)], g, hi - lo))
                m = near[:, 256 - (hi - lo):256] if g == 0 else (every4, every16)[g - 1][:, 384 - qt * P:T]
                maskl.append(m)
                vals += [VT[:, kt, g * T + h * 64:g * T + h * 64 + 64] for kt in range(lo // P, hi // P)]
            return {"scores": scores, "tiles": len(vals), "values": vals, "masks": maskl,
                    "out": slice(h * 64, h * 64 + 64), "scale": 0.125}

        def parts_mla(unit, i):
            qt, h = unit
            n_ = (qt + 1) * P
            return {"scores": [(0, [(QA[0:96, h, qt * P:n_], KA[0:96, h, 0:n_])], i % 2, n_)], "tiles": qt + 1,
                    "values": [VA[:, kt, h * 64:h * 64 + 64] for kt in range(qt + 1)],
                    "masks": [CH[:, 384 - qt * P:T]], "out": slice(h * 64, h * 64 + 64), "scale": 96 ** -0.5}

        def parts_band(unit, i):
            qt, h = unit
            n_, r = (qt + 1) * P, slice(h % 2 * 64, h % 2 * 64 + 64)
            return {"scores": [(0, [(QB[r, h // 2, qt * P:n_], KB[r, h // 2, 0:n_])], i % 2, n_)], "tiles": qt + 1,
                    "values": [VB[:, kt, h * 64:h * 64 + 64] for kt in range(qt + 1)],
                    "masks": [BT[:, h, 384 - qt * P:T]], "out": slice(h * 64, h * 64 + 64), "scale": 0.125}

        TURNED = []
        for parts_, us_ in ((parts1, units), (parts_mla, units), (parts_band, units)):
            for i_, u_ in enumerate(us_):
                TURNED.append((TURNED[-1] if TURNED else 0) + -(-parts_(u_, i_)["tiles"] // 4))

        block = ctx.enter_context(nc.Block())

        @block.sync
        def _(sp):
            for src, dst in ((a["consts"][:, 0:CONST_AT["near"][0]], const[:]), (a["cols"], cols[:])):
                sp.dma_start(dst, src).then_inc(got_const, 16)
            xv = a["x"].rearrange("(k p) t -> p k t", p=P)
            n = [0]

            def load(src, parts=P):
                m = n[0]
                n[0] += 1
                if m >= R:
                    sp.wait_ge(half_done, 2 * (m - R) + 2)
                size = src.shape[1] * src.shape[2]
                dst = ring[0:parts, m % R, 0:size].rearrange("p (k c) -> p k c", c=src.shape[2])
                sp.dma_start(dst, src).then_inc(full[m % R], 16)

            def wcols(w, c0, nc_=256):
                return w.rearrange("(k p) c -> p k c", p=P)[:, :, c0:c0 + nc_]

            def stream(w, count, at=0, step=256):
                first = n[0]
                wv = w.rearrange("(k p) c -> p k c", p=P)
                with sp.Fori(0, count // R) as i:
                    for j in range(R):
                        m = first + j
                        sp.wait_ge(half_done, i * (2 * R) + (2 * (m - R) + 2))
                        sp.dma_start(ring[:, m % R, :].rearrange("p (k c) -> p k c", c=256),
                                     wv[:, :, bass.ds(i * (R * 256) + (at + j * 256), 256)]).then_inc(full[m % R], 16)
                n[0] += count // R * R

            for j in range(R):
                load(wcols(a["w_ada"], j * 256))
            sp.dma_start(x_in, xv).then_inc(got_x, 16)
            sp.dma_start(W2A2[0:64, :], a["w2"]).then_inc(got_lora, 16)
            sp.dma_start(W2A2[64:128, :], a["a2"]).then_inc(got_lora, 16)
            stream(a["w_ada"], 20, at=4 * 256)
            RW = 4608
            load(wcols(a["w_in"], RW + 3072))
            load(wcols(a["w_in"], RW + 3328, 32))
            for q in range(4):
                for part in STREAMED:
                    load(wcols(a["w_in"], RW + part * D + q * 256))
            for g in range(4):
                load(wcols(a["w_in"], 7968 + D + g * 256))
                if g == 0:
                    sp.wait_ge(made, 8 * len(PRODUCTS))
                    sp.wait_ge(emptD, 4 * PER_QUAD["D"])
                    sp.wait_ge(emptA, 4 * PER_QUAD["A"])
                    sp.dma_start(G2[:, 0, :], a["g2"][0:128, :]).then_inc(got_g2, 16)
                    sp.dma_start(G2[0:32, 1, :], a["g2"][128:160, :]).then_inc(got_g2, 16)
                load(wcols(a["w_rwkv_out"], g * 256))
            for g in range(3):
                for part in range(2):
                    for c in range(2):
                        load(wcols(a["w_in"], g * 1536 + part * 512 + c * 256))
                if g == 0:
                    sp.wait_ge(half_done, 2 * FIRST["qk"])
                    sp.dma_start(masks, a["consts"][:, CONST_AT["near"][0]:CONST_AT["near"][0] + 1792]).then_inc(got_masks, 16)
            for g in range(3):
                for c in range(2):
                    load(wcols(a["w_in"], g * 1536 + 1024 + c * 256))
            for g in range(4):
                load(wcols(a["w_in"], 7968 + g * 256))
                load(wcols(a["w_att_out"], g * 256))
            for g in range(4):
                load(wcols(a["w_o"], g * 256))
                if g == 0:
                    sp.wait_ge(scored, len(units))
                    sp.dma_start(xT, xv).then_inc(got_x1, 16)
            upv = a["w_up"].rearrange("(k p) (g c) -> p g k c", p=P, g=2)
            first = n[0]
            def up_load(m, j):
                for g in range(2):
                    dst = ring[:, m % R, :].rearrange("p (g k c) -> p g k c", g=2, c=P)[:, g]
                    sp.dma_start(dst, upv[:, g, :, j]).then_inc(full[m % R], 8 * 2)
            with sp.Fori(0, 5) as i:
                for j in range(R):
                    m = first + j
                    sp.wait_ge(half_done, i * (2 * R) + (2 * (m - R) + 2))
                    up_load(m, bass.ds(i * (R * P) + j * P, P))
            for j in range(20, 22):
                m = first + j
                sp.wait_ge(half_done, 2 * (m - R) + 2)
                up_load(m, bass.ds(j * P, P))
            n[0] += 22
            dv = a["w_down"].rearrange("(k p) c -> p k c", p=P)
            for mm in range(4):
                for k0, k1 in ((0, 8), (8, 16), (16, 22)):
                    load(dv[:, k0:k1, mm * 256:mm * 256 + 256])

            stream(a["w_ada_2"], 24)
            load(wcols(a["w_in_2"], 0))
            load(wcols(a["w_kvr"], 0))
            load(wcols(a["w_kvr"], 256, 128))
            for c in range(6):
                load(wcols(a["w_in_2"], 416 + c * 256))
            for h in range(8):
                load(wcols(a["w_uq"], h * 256))
            for c in range(4):
                load(wcols(a["w_uk_2"], c * P, P))
            for c in range(2):
                load(wcols(a["w_uv_2"], c * 256))
            for w, at in ((a["w_oa_2"], 1952), (a["w_ob_2"], 1952 + D)):
                for g in range(4):
                    load(wcols(a["w_in_2"], at + g * 256))
                    load(wcols(w, g * 256))
            for g in range(4):
                load(wcols(a["w_out_2"], g * 256))
            gv = a["w_gate_2"].rearrange("e (k p) f -> p e k f", p=P)
            uv = a["w_up_2"].rearrange("e (k p) f -> p e k f", p=P)
            wd = a["w_down_2"].rearrange("e (k p) d -> p e k d", p=P)
            first = n[0]
            sp.wait_ge(half_done, 2 * first)
            sp.wait_ge(rounds_ready, 1)
            rounds = sp.value_load(NRD[0:1, 0:1].bitcast(I32), min_val=1, max_val=T // SLOTS)
            with sp.Fori(0, rounds) as r:
                with sp.Fori(0, 8) as i:
                    for j in range(4):
                        step = r * 32 + i * 4 + j
                        for part, w, c_ in ((0, gv, 256), (1, uv, 256), (2, wd, D)):
                            m = first + 3 * j + part
                            sp.wait_ge(*((down_made, step + 1), (gu_done, step * 2 + 1), (gu_done, step * 2 + 2))[part])
                            sp.dma_start(ring[:, m % R, :].rearrange("p (k c) -> p k c", c=c_),
                                         w[:, bass.ds(i * 4 + j, 1)].rearrange("p e k c -> p (e k) c")).then_inc(full[m % R], 16)
            sp.wait_ge(out_scaled, KT)
            sp.dma_start(a["out"].rearrange("(k p) t -> p k t", p=P), hT).then_inc(stored, 16)
            sp.wait_ge(stored, 16)

        @block.tensor
        def _(pe):
            n = [0]

            def slot():
                m = n[0]
                n[0] += 1
                pe.wait_ge(full[m % R], full_value(m))
                return m

            def half(m, hf, bank, rhs, width=P, kts=KT, out=None, start=True, stop=True, inc=1, cols_=256, slot_=None):
                w = ring[:, m % R, 0:kts * cols_].rearrange("p (k c) -> p k c", c=cols_)
                dst = ps[0:width, bank, :] if out is None else out
                for k in range(kts):
                    mm = pe.matmul(dst, w[:, k, hf * P:hf * P + width], rhs(k),
                                   start=(start and k == 0), stop=(stop and k == kts - 1))
                mm.then_inc(half_done, inc)

            pe.wait_ge(got_const, 32)

            def norm_sum(k_norm):
                pe.wait_ge(squared, k_norm + 1)
                for k in range(KT):
                    mm = pe.matmul(ps[:, 6, :], ones, hT[:, k, :], start=(k == 0), stop=(k == KT - 1))
                mm.then_inc(summed, 1)

            def ada(block_no, cvec):
                def turn(at, j):
                    for hf in range(2):
                        o = ps[:, 7, at + hf:at + hf + 1] if isinstance(at, int) else ps[:, 7, bass.ds(at + hf, 1)]
                        mm = pe.matmul(o, MROW[0:1, j % 4, hf * P:hf * P + P], ones[0:1, 0:1], start=True, stop=True)
                    return mm

                def one_slot(i, s_):
                    m = first + s_
                    pe.wait_ge(full[m % R], i * 16 + full_value(m))
                    pe.wait_ge(row_copied, i * 4 + (24 * block_no + s_ + 1))
                    w = ring[:, m % R, :].rearrange("p (k c) -> p k c", c=256)
                    for k in range(KT):
                        mm = pe.matmul(ps[0:1, s_ % 4, 0:256], cvec(k), w[:, k, :], start=(k == 0), stop=(k == KT - 1))
                    mm.then_inc(half_done, 2)
                    if s_ >= 2:
                        turn(i * 8 + 2 * (s_ - 2), s_ - 2)

                first = n[0]
                one_slot(0, 0)
                one_slot(0, 1)
                with pe.Fori(0, 3) as i:
                    for j in range(2, 6):
                        one_slot(i, j)
                norm_sum(3 * block_no)
                with pe.Fori(0, 2) as i:
                    for j in range(14, 18):
                        one_slot(i, j)
                one_slot(0, 22)
                one_slot(0, 23)
                pe.wait_ge(row_copied, 24 * block_no + 26)
                turn(44, 22)
                turn(46, 23).then_inc(mod_turned, 1)
                n[0] += 24

            ada(0, lambda k: col("c", k))

            def h_(k):
                return hT[:, k, :]

            pe.wait_ge(normed, 1)
            drain_psum(pe, "lora")
            m = slot()
            half(m, 0, 0, h_)
            half(m, 1, 1, h_)
            m = slot()
            half(m, 0, 2, h_, width=32, cols_=32, inc=2)

            pe.wait_ge(lora_ready, 1)
            pe.wait_ge(got_lora, 32)
            made_n = [0]

            def product(q, name, s, body, dep=()):
                i = made_n[0]
                made_n[0] += 1
                assert PNAMES[(i // 2) % len(PRODUCTS)] == name and i % 2 == s
                idx = (i // 2) % len(PRODUCTS)
                if i >= 2:
                    pq, pn = (q, PNAMES[idx - 1]) if idx else (q - 1, PNAMES[-1])
                    for e, sm in (("A", emptA), ("D", emptD)):
                        if e in PRODUCTS[PNAMES.index(pn)][1]:
                            pe.wait_ge(sm, emptied(pq, pn, s, e))
                for d in dep:
                    for e, sm in (("A", emptA), ("D", emptD)):
                        if e in PRODUCTS[PNAMES.index(d)][1]:
                            pe.wait_ge(sm, emptied(q, d, s, e))
                last = body(4 + 2 * s, 5 + 2 * s)
                last.then_inc(made, 1)

            def per_chunk(banks, terms):
                for e in range(2):
                    r = slice(e * 64, e * 64 + 64)
                    for c in range(NCH):
                        cc = slice(c * C, c * C + C)
                        if e == 0 and terms[0][1] is eye64:
                            mm = pe.transpose(ps[r, banks[e], cc], terms[0][0][r, cc], eye64[r])
                            continue
                        for i, (l, x) in enumerate(terms):
                            mm = pe.matmul(ps[r, banks[e], cc], l[r, cc], x[r, 0:64] if x is eye64 else x[r, cc],
                                           start=(i == 0), stop=(i == len(terms) - 1))
                return mm

            for q in range(4):
                if q == 0:
                    drain_psum(pe, "rkv")
                for s in range(2):
                    j = 2 * q + s

                    def lora(A, B, j=j):
                        pe.matmul(ps[:, A, :], W2A2[0:64, j * P:j * P + P], LOW[0:64, :], start=True, stop=True)
                        return pe.matmul(ps[:, B, :], W2A2[64:128, j * P:j * P + P], LOW[64:128, :], start=True, stop=True)
                    product(q, "lora", s, lora)

                def projected(m, hf, i):
                    hh = q * 6 + i
                    if hh >= 4:
                        pe.wait_ge(freed["D"], BEFORE["rkv"]["D"] + hh - 3)
                    half(m, hf, hh % 4, h_)

                m = slot()
                projected(m, 0, 0)
                projected(m, 1, 1)
                m = slot()
                projected(m, 0, 2)
                for s in range(2):
                    pe.wait_ge(chan, 6 * q + 1 + s)
                    product(q, "ssq", s, lambda A, B: pe.matmul(ps[:, A, :], headones, tmp[s][10], start=True, stop=True))
                projected(m, 1, 3)
                m = slot()
                projected(m, 0, 4)
                projected(m, 1, 5)
                for s in range(2):
                    pe.wait_ge(chan, 6 * q + 3 + s)
                    product(q, "bonus", s, lambda A, B: pe.matmul(ps[:, A, :], headones, tmp[s][10], start=True, stop=True))
                pe.wait_ge(freed["D"], BEFORE["rkv"]["D"] + 6 * q + 6)
                for s in range(2):
                    t_ = tmp[s]
                    product(q, "tv", s, lambda A, B: per_chunk((A, B), [(t_[2], eye64)]))
                for name, b in (("tat", 6), ("tbh", 5), ("tkh", 3)):
                    for s in range(2):
                        t_ = tmp[s]
                        pe.wait_ge(chan, 6 * q + 5 + s)
                        product(q, name, s, lambda A, B: per_chunk((A, B), [(t_[b], eye64)]))
                for name, l, x in (("ab", 6, 4), ("abT", 4, 6), ("akT", 8, 6), ("rbT", 4, 0), ("rkT", 8, 0)):
                    for s in range(2):
                        t_ = tmp[s]
                        product(q, name, s, lambda A, B: per_chunk((A, B), [(t_[l], t_[x])]))
                nlev = len(LEVELS)
                for li, b in enumerate(LEVELS):
                    prev = ("ab", "abT") if li == 0 else (f"x{LEVELS[li - 1]}", f"xT{LEVELS[li - 1]}")
                    mb = 6 if li % 2 == 0 else 8
                    for s in range(2):
                        t_ = tmp[s]
                        pe.wait_ge(maskp, q * 2 * nlev + 2 * li + s + 1)
                        product(q, f"y{b}", s, lambda A, B: per_chunk((A, B), [(t_[mb], t_[2])]), dep=prev)
                    if b != LEVELS[-1]:
                        for s in range(2):
                            t_ = tmp[s]
                            product(q, f"x{b}", s, lambda A, B: per_chunk((A, B), [(t_[3], t_[4])]), dep=(f"y{b}",))
                    for s in range(2):
                        t_ = tmp[s]
                        product(q, f"xT{b}", s, lambda A, B: per_chunk((A, B), [(t_[4], t_[3])]), dep=(f"y{b}",))
                fin = f"xT{LEVELS[-1]}"
                for s in range(2):
                    t_ = tmp[s]
                    product(q, "w1", s, lambda A, B: per_chunk((A, B), [(t_[11], t_[1])]), dep=(fin,))
                for s in range(2):
                    t_ = tmp[s]
                    product(q, "sav", s, lambda A, B: per_chunk((A, B), [(t_[3], t_[4])]), dep=("w1",))
                for s in range(2):
                    t_ = tmp[s]
                    product(q, "z", s, lambda A, B: per_chunk((A, B), [(t_[3], t_[7])]), dep=())
                for s in range(2):
                    t_ = tmp[s]
                    product(q, "r", s, lambda A, B: per_chunk((A, B), [(t_[5], t_[12])]), dep=("z",))
                for s in range(2):
                    t_ = tmp[s]
                    product(q, "y0", s, lambda A, B: per_chunk((A, B), [(t_[2], t_[12]), (t_[1], t_[13])]), dep=("sav",))
                for s in range(2):
                    t_ = tmp[s]
                    product(q, "g", s, lambda A, B: per_chunk((A, B), [(t_[5], t_[9])]))
                for s in range(2):
                    t_ = tmp[s]
                    product(q, "h", s, lambda A, B: per_chunk((A, B), [(t_[9], t_[2]), (t_[10], t_[1])]))

            for e, sm in (("A", emptA), ("D", emptD)):
                pe.wait_ge(sm, 4 * PER_QUAD[e])
            for c in range(1, NCH - 1):
                pe.wait_ge(state_ready, c - 1) if c > 1 else None
                A = 4 + 2 * (c % 2)
                for e in range(2):
                    r = slice(e * 64, e * 64 + 64)
                    for j in range(8):
                        mm = pe.matmul(ps[r, A + e, j * C:j * C + C], GT[r, j, c, :], ST[r, c - 1, j, :],
                                       start=True, stop=True)
                mm.then_inc(stepped, 1)
            pe.wait_ge(state_ready, NCH - 2)
            pe.wait_ge(got_g2, 32)

            def y_state(j):
                if j >= 2:
                    pe.wait_ge(y_final, j - 1)
                for e in range(2):
                    r = slice(e * 64, e * 64 + 64)
                    for c in range(1, NCH):
                        mm = pe.matmul(ps[r, 4 + 2 * (j % 2) + e, c * C:c * C + C], ST[r, c - 1, j, :],
                                       RT[r, j, c * C:c * C + C], start=True, stop=True)
                mm.then_inc(y_made, 1)

            def y_mean(j):
                pe.wait_ge(y_added, j + 1)
                if j >= 2:
                    pe.wait_ge(centred, j - 1)
                pe.matmul(ps[:, j % 2, :], headones, Y0[:, j, :], start=True, stop=True).then_inc(mean_made, 1)

            def y_var(j):
                pe.wait_ge(y_sq, j + 1)
                if j >= 2:
                    pe.wait_ge(y_root, j - 1)
                pe.matmul(ps[:, 2 + j % 2, :], headones, ytmp[j % 2][0], start=True, stop=True).then_inc(var_made, 1)

            def y_gate(j):
                b = 4 + 2 * (j % 2)
                pe.matmul(ps[:, b, :], G2[:, 0, j * P:j * P + P], GLO, start=True, stop=False)
                pe.matmul(ps[:, b, :], G2[0:32, 1, j * P:j * P + P], GLO2[0:32], start=False, stop=True).then_inc(g_made, 1)

            for t in range(8 + 2):
                if 0 <= t - 2 < 8:
                    y_var(t - 2)
                if 0 <= t - 1 < 8:
                    y_mean(t - 1)
                    y_gate(t - 1)
                if t < 8:
                    y_state(t)
            pe.wait_ge(y_final, 8)

            def gated_projection(phase, rhs, kts):
                drain_psum(pe, phase)
                for g in range(4):
                    m = slot()
                    for hf in range(2):
                        i = 2 * g + hf
                        if i >= 2:
                            pe.wait_ge(freed["A"], BEFORE[phase]["A"] + i - 1)
                        half(m, hf, i % 2, h_)
                    m = slot()
                    for hf in range(2):
                        i = 2 * g + hf
                        if i >= 2:
                            pe.wait_ge(freed["D"], BEFORE[phase]["D"] + i - 1)
                        half(m, hf, 2 + i % 2, rhs, kts=kts)

            gated_projection("rw_out", lambda k: Y0[:, k, :], KT)

            def alternate(phase, hh):
                if hh >= 4:
                    e = "AD"[hh % 2]
                    pe.wait_ge(freed[e], BEFORE[phase][e] + (hh - 4) // 2 + 1)

            drain_psum(pe, "qk")
            for t in range(12):
                m = slot()
                for hf in range(2):
                    alternate("qk", 2 * t + hf)
                    half(m, hf, (2 * t + hf) % 4, h_)

            def token_major(phase, count):
                drain_psum(pe, phase)
                for t in range(count):
                    m = slot()
                    w = ring[:, m % R, :].rearrange("p (k c) -> p k c", c=256)
                    for hf in range(2):
                        hh = 2 * t + hf
                        alternate(phase, hh)
                        for tt in range(2):
                            tok = (2 * hf + tt) * P
                            for k in range(KT):
                                mm = pe.matmul(ps[:, hh % 4, tt * 256:tt * 256 + 256], hT[:, k, tok:tok + P],
                                               w[:, k, :], start=(k == 0), stop=(k == KT - 1))
                        mm.then_inc(half_done, 1)

            token_major("v", 6)
            drain_psum(pe, "at_out")

            def attend(u0, us, parts_of, s_banks):
                def scores(i):
                    if i >= s_banks:
                        pe.wait_ge(masked, u0 + i - s_banks + 1)
                    for q_, ks, bk, n_ in parts_of(us[i], i)["scores"]:
                        for t_, (l, x) in enumerate(ks):
                            mm = pe.matmul(ps[:, bk, 0:n_], l, x, start=(t_ == 0), stop=(t_ == len(ks) - 1))
                    mm.then_inc(scored, 1)

                def turn(i):
                    n_ = parts_of(us[i], i)["tiles"]
                    pe.wait_ge(probbed, u0 + i + 1)
                    for t_ in range(n_):
                        if t_ % 4 == 0:
                            g = turn_n[0]
                            turn_n[0] += 1
                            if g >= 2:
                                pe.wait_ge(turnedS, g - 1)
                        mm = pe.transpose(ps[:, 4 + g % 2, t_ % 4 * P:t_ % 4 * P + P],
                                          prob[(u0 + i) % 2][:, t_ * P:t_ * P + P], ident)
                        if t_ % 4 == 3 or t_ == n_ - 1:
                            mm.then_inc(turned, 1)

                def weigh(i):
                    u = u0 + i
                    pe.wait_ge(turnedS, TURNED[u])
                    if u >= 2:
                        pe.wait_ge(outed, u - 1)
                    vs = parts_of(us[i], i)["values"]
                    for t_, v in enumerate(vs):
                        mm = pe.matmul(ps[:, 6 + u % 2, 0:64], probT[u % 2][:, t_ * P:t_ * P + P], v,
                                       start=(t_ == 0), stop=(t_ == len(vs) - 1))
                    mm.then_inc(weighed, 1)

                def turn_out(i):
                    w = (u0 + i) // 8
                    pe.wait_ge(outed, u0 + i + 1)
                    if w >= 1:
                        pe.wait_ge(oready, w)
                    for t_ in range(4):
                        mm = pe.transpose(ps[:, 3, t_ * P:t_ * P + P], otok[w % 2][:, t_ * P:t_ * P + P], ident)
                    mm.then_inc(oturned, 1)

                scores(0)
                for i in range(len(us)):
                    if i + 1 < len(us):
                        scores(i + 1)
                    if i >= 1:
                        weigh(i - 1)
                    turn(i)
                    if i >= 1 and (i - 1) % 8 == 7:
                        turn_out(i - 1)
                weigh(len(us) - 1)
                turn_out(len(us) - 1)

            turn_n = [0]
            prob, probT, otok = PROB1
            attend(0, units, parts1, 1)
            pe.wait_ge(oready, 4)
            gated_projection("at_out", lambda k: OT1[:, k, :], 4)

            drain_psum(pe, "w_o")
            for t in range(4):
                m = slot()
                for hf in range(2):
                    hh = 2 * t + hf
                    if hh >= 4:
                        pe.wait_ge(freed["D"], BEFORE["w_o"]["D"] + hh - 3)
                    half(m, hf, hh % 4, lambda k: merged[:, k, :])

            norm_sum(1)
            pe.wait_ge(normed, 2)
            drain_psum(pe, "up")
            first = n[0]

            def up_slot(m, fv, hbase):
                pe.wait_ge(w_low, fv)
                for g in range(2):
                    wl, wh = [v.rearrange("p (g k c) -> p g k c", g=2, c=P)[:, g]
                              for v in (W_LOW[:, m % R, :], W_HIGH[:, (m - first) % 2, :])]
                    if hbase is not None:
                        pe.wait_ge(freed["D"], hbase + g)
                    for k in range(KT):
                        for i_, (w_, x_) in enumerate(((wl, H_HIGH), (wh, H_LOW), (wh, H_HIGH))):
                            mm = pe.matmul(ps[:, (2 * (m - first) + g) % 4, :], w_[:, k, :], x_[:, k, :],
                                           start=(k == 0 and i_ == 0), stop=(k == KT - 1 and i_ == 2))
                    mm.then_inc(half_done, 1)

            D0 = BEFORE["up"]["D"]
            for j in range(2):
                up_slot(first + j, j + 1, None)
            with pe.Fori(0, 5) as i:
                for j in range(2, 2 + R):
                    m = first + j
                    up_slot(m, i * R + (j + 1), i * (2 * R) + (D0 + 2 * j - 3))
            n[0] += 22
            pe.wait_ge(hidd, FT)
            drain_psum(pe, "down")
            for mm_ in range(4):
                for part, kts in enumerate((8, 8, 6)):
                    m = n[0]
                    n[0] += 1
                    d = m - FIRST["down"]
                    pe.wait_ge(w_low, 22 + d + 1)
                    wl, wh = [v[:, 0:kts * 256].rearrange("p (k c) -> p k c", c=256) for v in (W_LOW[:, m % R, :], W_HIGH[:, d % 2, :])]
                    for hf in range(2):
                        hh = 2 * mm_ + hf
                        if hh >= 4 and part == 0:
                            pe.wait_ge(freed["D"], BEFORE["down"]["D"] + hh - 3)
                        for k in range(kts):
                            kt = part * 8 + k
                            x_low = HID_LOW[0][:, kt, :] if kt < 2 else HID_LOW[1][:, kt - 2, :]
                            for i_, (w_, x_) in enumerate(((wl, HID_HIGH[:, kt, :]), (wh, x_low), (wh, HID_HIGH[:, kt, :]))):
                                mm = pe.matmul(ps[:, hh % 4, :], w_[:, k, hf * P:hf * P + P], x_,
                                               start=(kt == 0 and i_ == 0), stop=(kt == FT - 1 and i_ == 2))
                        mm.then_inc(half_done, 1)
            norm_sum(2)

            pe.wait_ge(silu_c, 1)
            drain_psum(pe, "ada2")
            ada(1, lambda k: C2S[:, k:k + 1])
            pe.wait_ge(normed, 4)
            drain_psum(pe, "in2")
            o = 0
            for t in range(7):
                m = slot()
                for hf in range(1 if t == 2 else 2):
                    alternate("in2", o)
                    half(m, hf, o % 4, h_, cols_=P if t == 2 else 256, inc=2 if t == 2 else 1)
                    o += 1

            def token_slots(phase, o, count, src, kts):
                for t in range(count):
                    m = slot()
                    w = ring[:, m % R, 0:kts * 256].rearrange("p (k c) -> p k c", c=256)
                    for hf in range(2):
                        alternate(phase, o)
                        for tt in range(2):
                            tok = (2 * hf + tt) * P
                            for k in range(kts):
                                mm = pe.matmul(ps[:, o % 4, tt * 256:tt * 256 + 256], src(k)[:, tok:tok + P],
                                               w[:, k, :], start=(k == 0), stop=(k == kts - 1))
                        mm.then_inc(half_done, 1)
                        o += 1

            token_slots("in2", o, 2, h_, KT)
            pe.wait_ge(lat_sq, 1)
            pe.matmul(ps[:, 6, :], ones, LSQ[:, 0, :], start=True, stop=False)
            pe.matmul(ps[:, 6, :], ones, LSQ[:, 1, :], start=False, stop=True)
            pe.matmul(ps[:, 7, :], ones, LSQ[:, 2, :], start=True, stop=True).then_inc(lat_sum, 1)
            pe.wait_ge(lat_ready, 1)
            drain_psum(pe, "lat2")
            o = 0
            for h in range(8):
                m = slot()
                for hf in range(2):
                    alternate("lat2", o)
                    half(m, hf, o % 4, lambda k: QL[:, k, :], width=96, kts=2)
                    o += 1
            for t in range(4):
                m = slot()
                for hf in range(2):
                    alternate("lat2", o)
                    w = ring[:, m % R, 0:P]
                    pe.matmul(ps[0:64, o % 4, :], w[:, hf * 64:hf * 64 + 64], KV, start=True, stop=True).then_inc(half_done, 1)
                    o += 1
            token_slots("lat2", o, 2, lambda k: KV, 1)
            drain_psum(pe, "mla_out")
            pe.wait_ge(band_ready, 1)
            prob, probT, otok = PROB2
            attend(32, units, parts_mla, 2)
            attend(64, units, parts_band, 2)
            pe.wait_ge(oready, 12)
            gated_projection("mla_out", lambda k: OA[:, k, :], 4)
            gated_projection("band_out", lambda k: OB[:, k, :], 4)
            drain_psum(pe, "w_out2")
            for t in range(4):
                m = slot()
                for hf in range(2):
                    hh = 2 * t + hf
                    if hh >= 4:
                        pe.wait_ge(freed["D"], BEFORE["w_out2"]["D"] + hh - 3)
                    half(m, hf, hh % 4, lambda k: merged2[:, k, :])
            norm_sum(4)
            pe.wait_ge(normed, 5)
            pe.wait_ge(got_router, 64)
            for tt in range(4):
                for k in range(KT):
                    mm = pe.matmul(ps[:, 7, tt * 36:tt * 36 + 36], hT[:, k, tt * P:tt * P + P], WR[:, k, :],
                                   start=(k == 0), stop=(k == KT - 1))
            mm.then_inc(routed, 1)
            for g in range(8):
                if g >= 2:
                    pe.wait_ge(h2_ready, g - 1)
                tt = g // 2
                for k in range(4):
                    mm = pe.transpose(ps[:, 4 + g % 2, k * P:k * P + P], hT[:, g % 2 * 4 + k, tt * P:tt * P + P], ident)
                mm.then_inc(h2_made, 1)
            pe.wait_ge(selected, 1)
            for tt in range(4):
                for t_ in range(tt + 1):
                    mm = pe.matmul(ps[:, 6, tt * 32:tt * 32 + 32], BEF if t_ == tt else ones, SEL[:, t_, :],
                                   start=(t_ == 0), stop=(t_ == tt))
            mm.then_inc(ranked, 1)
            for t_ in range(4):
                mm = pe.matmul(ps[:, 3, 0:32], ones, SEL[:, t_, :], start=(t_ == 0), stop=(t_ == 3))
            mm.then_inc(counted, 1)
            pe.wait_ge(h2_ready, 8)
            pe.wait_ge(rounds_ready, 1)
            rounds = pe.value_load(NRD[0:1, 0:1].bitcast(I32), min_val=1, max_val=T // SLOTS)
            first = n[0]

            def gather(value, par, hf):
                pe.wait_ge(placed, value)
                for k in range(4):
                    for tt in range(4):
                        mm = pe.matmul(ps[:, hf, k * P:k * P + P], H2T[:, tt, (4 * hf + k) * P:(4 * hf + k + 1) * P],
                                       PICKED[:, par, tt, :], start=(tt == 0), stop=(tt == 3))
                mm.then_inc(gathered, 1)

            gather(2, 0, 0)
            gather(2, 0, 1)
            with pe.Fori(0, rounds) as r:
                with pe.Fori(0, 8) as i:
                    for j in range(4):
                        par = j % 2
                        step = r * 32 + i * 4 + j
                        if j % 2 == 0:
                            pe.wait_ge(xe_ready, step + 2)
                        for part in range(2):
                            m = first + 3 * j + part
                            pe.wait_ge(full[m % R], r * 384 + i * 48 + full_value(m))
                            w = ring[:, m % R, :].rearrange("p (k c) -> p k c", c=256)
                            for f in range(2):
                                for k in range(KT):
                                    mm = pe.matmul(ps[:, 2 + par, (2 * part + f) * SLOTS:(2 * part + f + 1) * SLOTS],
                                                   w[:, k, f * P:f * P + P], XE[:, j // 2, k, par * SLOTS:(par + 1) * SLOTS],
                                                   start=(k == 0), stop=(k == KT - 1))
                            mm.then_inc(gu_done, 1)
                        gather(r * 32 + i * 4 + (j // 2 * 2 + 4), 1 - j // 2, j % 2)
                        m = first + 3 * j + 2
                        pe.wait_ge(full[m % R], r * 384 + i * 48 + full_value(m))
                        pe.wait_ge(copied["A"], step + 1)
                        pe.wait_ge(copied["D"], step + 1)
                        pe.wait_ge(mhid, step + 1)
                        w = ring[:, m % R, :].rearrange("p (k c) -> p k c", c=D)
                        for c in range(2):
                            for f in range(2):
                                mm = pe.matmul(ps[0:SLOTS, 4 + 2 * par + c, :], MH[:, par, f, :], w[:, f, c * 512:c * 512 + 512],
                                               start=(f == 0), stop=(f == 1))
                        mm.then_inc(down_made, 1)
            pe.wait_ge(mixed, rounds * 4)
            for k in range(KT):
                if k >= 2:
                    pe.wait_ge(freed["D"], BEFORE["moe"]["D"] + k - 1)
                for tt in range(4):
                    mm = pe.transpose(ps[:, 2 + k % 2, tt * P:tt * P + P], GX[:, tt, k * P:k * P + P], ident)
                mm.then_inc(mix_turned, 1)
            norm_sum(5)

        @block.scalar
        def _(act):
            lk = Link(act, act_link)
            act.wait_ge(got_const, 32)

            def norm_squares(k_norm, src):
                act.activation(hT, src, ACT.Square).then_inc(squared, 1)

            def norm_root(k_norm):
                act.wait_ge(summed, k_norm + 1)
                act.activation(RSTD, ps[:, 6, :], ACT.Sqrt, scale=1.0 / D, bias=EPSC).then_inc(rooted, 1)

            def copy_rows(phase, i, slots_):
                for s_ in slots_:
                    act.wait_ge(half_done, i * 8 + (2 * FIRST[phase] + 2 * s_ + 2))
                    act.activation(MROW[0:1, s_ % 4, :], ps[0:1, s_ % 4, 0:256], ACT.Copy).then_inc(row_copied, 1)

            def modulation_rows(phase, squares, root):
                copy_rows(phase, 0, range(2))
                with act.Fori(0, 2) as i:
                    copy_rows(phase, i, range(2, 6))
                squares()
                copy_rows(phase, 0, range(10, 14))
                root()
                with act.Fori(0, 2) as i:
                    copy_rows(phase, i, range(14, 18))
                copy_rows(phase, 0, range(22, 24))

            act.wait_ge(mod_ready, 1)
            act.activation(small[:, 5:6], ZERO, ACT.Copy).then_inc(row_copied, 2)

            def squares0():
                act.wait_ge(got_x, 16)
                norm_squares(0, x_in)

            modulation_rows("ada1", squares0, lambda: norm_root(0))

            act.wait_ge(got_lora, 32)
            for i, (dst, rows) in enumerate(((LOW, P), (GLO, P), (GLO2, 32))):
                act.wait_ge(half_done, 2 * FIRST["lora"] + (1, 2, 4)[i])
                act.activation(dst[0:rows], ps[0:rows, i, :], ACT.Identity,
                               scale=OMU[0:rows, 24 + i:25 + i], bias=ZERO[0:rows]).then_inc(scaled, 1)
            act.wait_ge(freed["D"], BEFORE["lora"]["D"] + 1)
            act.activation(LOW[0:64], LOW[0:64], ACT.Tanh).then_inc(act_link, 1)
            act.wait_ge(freed["D"], BEFORE["lora"]["D"] + 3)
            act.activation(GLO, GLO, ACT.Sigmoid).then_inc(act_link, 1)
            act.activation(GLO2[0:32], GLO2[0:32], ACT.Sigmoid).then_inc(act_link, 1)
            act.wait_ge(act_link, 3)
            act.activation(ZSINK, ZERO, ACT.Copy).then_inc(lora_ready, 1)

            np_ = len(PRODUCTS)

            def made_wait(q, name, s):
                act.wait_ge(made, 2 * np_ * q + 2 * PNAMES.index(name) + s + 1)

            def empty_half(q, name, s, dst):
                made_wait(q, name, s)
                act.activation(dst[0:64], ps[0:64, 4 + 2 * s, :], ACT.Copy).then_inc(emptA, 1)

            for q in range(4):
                if q:
                    act.wait_ge(made, 2 * np_ * q)
                    act.wait_ge(emptD, PER_QUAD["D"] * q)
                for s in range(2):
                    j = 2 * q + s
                    made_wait(q, "lora", s)
                    act.activation(tmp[s][3], ps[:, 4 + 2 * s, :], ACT.Sigmoid, bias=col("w0", j)).then_inc(act_link, 1)
                    act.wait_ge(act_link, 3 + 2 * q + s + 1)
                    act.activation(tmp[s][4], ps[:, 5 + 2 * s, :], ACT.Sigmoid, bias=col("a0", j)).then_inc(emptA, 1)

                def scale_own(i):
                    part, hf = STREAMED[i // 2], i % 2
                    act.wait_ge(half_done, 2 * FIRST["rkv"] + q * 6 + i + 1)
                    o = part * 8 + 2 * q + hf
                    act.activation(tmp[hf][part], ps[:, (q * 6 + i) % 4, :], ACT.Identity,
                                   scale=OMU[:, o:o + 1], bias=ZERO).then_inc(scaled, 1)

                scale_own(0)
                scale_own(1)
                for s in range(2):
                    act.wait_ge(cum, 2 * q + s + 1)
                    t_ = tmp[s]
                    act.activation(t_[7], t_[5], ACT.Exp, scale=-KAPPA).then_inc(decay, 1)
                    act.activation(t_[8], t_[5], ACT.Exp, scale=KAPPA).then_inc(decay, 1)
                    act.activation(t_[6], t_[6], ACT.Exp, scale=-KAPPA).then_inc(decay, 1)
                scale_own(2)
                for s in range(2):
                    made_wait(q, "ssq", s)
                    act.activation(tmp[s][10], ps[:, 4 + 2 * s, :], ACT.Sqrt, bias=ZERO).then_inc(emptA, 1)
                for i in range(3, 6):
                    scale_own(i)
                for s in range(2):
                    act.wait_ge(chan, 6 * q + 5 + s) if s == 0 else act.wait_ge(chan, 6 * q + 6)
                    empty_half(q, "tv", s, tmp[s][1])
                for name, d in (("tat", 7), ("tbh", 9), ("tkh", 10)):
                    for s in range(2):
                        empty_half(q, name, s, tmp[s][d])
                for b in LEVELS:
                    for s in range(2):
                        empty_half(q, f"y{b}", s, tmp[s][4])
                for name, d in (("w1", 4), ("sav", 2), ("z", 5)):
                    for s in range(2):
                        empty_half(q, name, s, tmp[s][d])
                for s in range(2):
                    j = 2 * q + s
                    made_wait(q, "y0", s)
                    act.activation(Y0[0:64, j, :], ps[0:64, 4 + 2 * s, :], ACT.Copy).then_inc(emptA, 1)
                for s in range(2):
                    j = 2 * q + s
                    made_wait(q, "h", s)
                    act.activation(ST[0:64, :, j, :], chunks(ps[0:64, 4 + 2 * s, :]), ACT.Copy).then_inc(emptA, 1)

            def y_square(j):
                act.wait_ge(centred, j + 1)
                if j >= 2:
                    act.wait_ge(y_root, j - 1)
                act.activation(ytmp[j % 2][0], Y0[:, j, :], ACT.Square).then_inc(y_sq, 1)

            def y_roots(j):
                act.wait_ge(var_made, j + 1)
                if j >= 2:
                    act.wait_ge(y_final, j - 1)
                act.activation(ytmp[j % 2][1], ps[:, 2 + j % 2, :], ACT.Sqrt, scale=1.0 / 64, bias=GNC).then_inc(y_root, 1)

            for t in range(9):
                if t >= 1:
                    y_roots(t - 1)
                if t < 8:
                    y_square(t)

            def gates(phase, at):
                for g in range(4):
                    for hf in range(2):
                        i = 2 * g + hf
                        act.wait_ge(half_done, 2 * FIRST[phase] + 4 * g + hf + 1)
                        if i >= 2:
                            act.wait_ge(freed["D"], BEFORE[phase]["D"] + i - 1)
                        elif i == 0:
                            act.wait_ge(freed["D"], BEFORE[phase]["D"])
                        gb, bias = (gate, col("b_gate", at + i)) if at is not None else (gate2, ZERO)
                        act.activation(gb[:, i % 2, :], ps[:, i % 2, :], ACT.Sigmoid, bias=bias).then_inc(freed["A"], 1)

            act.wait_ge(y_final, 8)
            gates("rw_out", 8)

            act.wait_ge(freed["D"], BEFORE["qk"]["D"])
            for i in range(12):
                act.wait_ge(half_done, 2 * FIRST["qk"] + 2 * i + 1)
                act.activation(QK[:, 2 * i, :], ps[:, 2 * i % 4, :], ACT.Copy).then_inc(freed["A"], 1)
            for i in range(6):
                act.wait_ge(half_done, 2 * FIRST["v"] + 2 * i + 1)
                act.activation(VT[:, 0:2, i * 256:i * 256 + 256], ps[:, 2 * i % 4, :].rearrange("p (a b) -> p a b", b=256),
                               ACT.Copy).then_inc(freed["A"], 1)

            turn_n = [0]

            def attend(u0, us, parts_of, prob, probT, OT):
                def exps(i):
                    u = u0 + i
                    act.wait_ge(peaked, u + 1)
                    n_ = parts_of(us[i], i)["tiles"] * P
                    act.activation(prob[u % 2][:, 0:n_], prob[u % 2][:, 0:n_], ACT.Exp, scale=parts_of(us[i], i)["scale"],
                                   bias=NM[:, u % 2:u % 2 + 1], accum_out=DEN[:, u % 2:u % 2 + 1]).then_inc(probbed, 1)

                def copies(i):
                    u = u0 + i
                    n_ = parts_of(us[i], i)["tiles"]
                    if u >= 2:
                        act.wait_ge(weighed, u - 1)
                    for t_ in range(0, n_, 4):
                        g = turn_n[0]
                        turn_n[0] += 1
                        k = min(4, n_ - t_)
                        act.wait_ge(turned, g + 1)
                        act.activation(probT[u % 2][:, t_ * P:(t_ + k) * P], ps[:, 4 + g % 2, 0:k * P], ACT.Copy).then_inc(turnedS, 1)

                def out_copy(i):
                    w = (u0 + i) // 8
                    act.wait_ge(oturned, w + 1)
                    qt = us[i][0]
                    act.activation(OT[:, :, qt * P:qt * P + P], ps[:, 3, :].rearrange("p (a b) -> p a b", b=P),
                                   ACT.Copy).then_inc(oready, 1)

                exps(0)
                for i in range(len(us)):
                    if i + 1 < len(us):
                        exps(i + 1)
                    copies(i)
                    if i % 8 == 0 and i:
                        out_copy(i - 1)
                out_copy(len(us) - 1)

            attend(0, units, parts1, PROB1[0], PROB1[1], OT1)
            gates("at_out", 0)

            act.wait_ge(freed["D"], BEFORE["up"]["D"])
            act.wait_ge(half_done, 2 * FIRST["up"])
            norm_squares(1, xT)
            norm_root(1)
            up_first = FIRST["up"]

            def weights_high(j, i=0):
                m = up_first + j
                act.wait_ge(full[m % R], full_value(m) + 32 * i)
                act.activation(W_HIGH[:, j % 2, :], ring[:, m % R, :], ACT.Copy).then_inc(w_high, 1)

            def down_weights_high(d):
                m = FIRST["down"] + d
                size = (2048, 2048, 1536)[d % 3]
                act.wait_ge(full[m % R], full_value(m))
                act.wait_ge(half_done, 2 * (m - 2) + 2)
                act.activation(W_HIGH[:, d % 2, 0:size], ring[:, m % R, 0:size], ACT.Copy).then_inc(w_high, 1)

            weights_high(0)
            weights_high(1)
            for k in range(KT):
                act.wait_ge(h_piece, k + 1)
                act.activation(H_HIGH[:, k, :], hT[:, k, :], ACT.Copy).then_inc(h_high, 1)
            act.wait_ge(normed, 2)

            H0 = 2 * FIRST["up"]
            D0 = BEFORE["up"]["D"]

            def up_scale(jj, hb, cb):
                for g in range(2):
                    act.wait_ge(half_done, hb(2 * jj + g + 1))
                    if jj >= 2:
                        act.wait_ge(hidd, cb(jj - 1))
                    act.activation(cvt[jj % 2][g], ps[:, (2 * jj + g) % 4, :], ACT.Identity,
                                   scale=up_col(2, g, jj, cb), bias=up_col(3, g, jj, cb)).then_inc(convd, 1)

            def up_silu(jj, hb, cb, db):
                act.wait_ge(freed["D"], db(2 * jj + 1))
                act.activation(sil[:, jj % 2, :], cvt[jj % 2][0], ACT.Silu).then_inc(silud, 1)

            def up_col(tap, g, jj, cb):
                base = (COL_AT["conv_w"] + tap * 44 if tap < 3 else COL_AT["conv_b"]) + g * FT
                i = cb(jj)
                return cols[:, base + i:base + i + 1] if isinstance(i, int) else cols[:, bass.ds(i + base, 1)]

            ident_ = (lambda v: H0 + v), (lambda v: v), (lambda v: D0 + v)
            for jj in range(2):
                up_scale(jj, ident_[0], ident_[1])
                weights_high(jj + 2)
                up_silu(jj, *ident_)
            with act.Fori(0, 4) as i:
                for jj in range(2, 2 + R):
                    f = (lambda v: i * 8 + (H0 + v)), (lambda v: i * 4 + v), (lambda v: i * 8 + (D0 + v))
                    up_scale(jj, f[0], f[1])
                    weights_high(jj + 2, i)
                    up_silu(jj, *f)
            for jj in range(18, 22):
                up_scale(jj, ident_[0], ident_[1])
                weights_high(jj + 2) if jj < 20 else down_weights_high(jj - 20)
                up_silu(jj, *ident_)
            for d in range(2, 12):
                down_weights_high(d)
            act.wait_ge(freed["D"], BEFORE["ada2"]["D"])
            norm_squares(2, xT)
            norm_root(2)

            act.activation(C2S, col("c_2", 0, 8), ACT.Silu).then_inc(silu_c, 1)

            def squares3():
                act.wait_ge(normed, 3)
                norm_squares(3, xT)

            modulation_rows("ada2", squares3, lambda: norm_root(3))
            act.wait_ge(angled, 1)
            act.activation(ANG[:, 0:2, :], ANG[:, 0:2, :], ACT.Sin, bias=ZERO).then_inc(rotated, 1)

            def psum_out(phase, o, dst, src, v):
                act.wait_ge(half_done, 2 * FIRST[phase] + v)
                act.activation(dst, src, ACT.Copy).then_inc(freed["A"], 1)

            in2_value = lambda o: o + 1 if o < 4 else o + 2
            tok2 = lambda v: v.rearrange("p (a b) -> p a b", b=256)
            IN2 = [QL[:, 0, :], QL[:, 1, :], KV, KR, KRS] + [QB[:, j, :] for j in range(4)] + [KB[:, j, :] for j in range(4)]
            act.wait_ge(rotated, 1)
            for o in range(0, 13, 2):
                psum_out("in2", o, IN2[o], ps[:, o % 4, :], in2_value(o))
            for o in (14, 16):
                c, hf = divmod(o - 13, 2)
                psum_out("in2", o, VB[:, 2 * hf:2 * hf + 2, c * 256:c * 256 + 256], tok2(ps[:, o % 4, :]), in2_value(o))
            act.wait_ge(freed["D"], BEFORE["in2"]["D"] + 1)
            act.activation(LSQ[:, 0:2, :], QL, ACT.Square).then_inc(act_link, 1)
            act.activation(LSQ[:, 2, :], KV, ACT.Square).then_inc(lat_sq, 1)
            act.wait_ge(lat_sum, 1)
            act.activation(LRT[:, 0, :], ps[:, 6, :], ACT.Sqrt, scale=1.0 / 256, bias=EPSC).then_inc(lat_root, 1)
            act.activation(LRT[:, 1, :], ps[:, 7, :], ACT.Sqrt, scale=1.0 / 128, bias=EPSC).then_inc(lat_root, 1)
            for o in range(0, 16, 2):
                psum_out("lat2", o, QA[0:96, o // 2, :], ps[0:96, o % 4, :], o + 1)
            for o in range(16, 24, 2):
                psum_out("lat2", o, KA[0:64, o - 16, :], ps[0:64, o % 4, :], o + 1)
            for o in (24, 26):
                c, hf = divmod(o - 24, 2)
                psum_out("lat2", o, VA[:, 2 * hf:2 * hf + 2, c * 256:c * 256 + 256], tok2(ps[:, o % 4, :]), o + 1)
            attend(32, units, parts_mla, PROB2[0], PROB2[1], OA)
            attend(64, units, parts_band, PROB2[0], PROB2[1], OB)
            gates("mla_out", None)
            gates("band_out", None)
            act.wait_ge(freed["D"], BEFORE["moe"]["D"])
            act.wait_ge(half_done, 2 * FIRST["moe"])
            norm_squares(4, xT)
            norm_root(4)
            act.wait_ge(route_exp, 1)
            act.activation(rt_e, rt_e, ACT.Exp).then_inc(route_exp, 1)
            for g in range(8):
                act.wait_ge(h2_made, g + 1)
                act.activation(H2T[:, g // 2, g % 2 * 512:g % 2 * 512 + 512], ps[:, 4 + g % 2, :], ACT.Copy).then_inc(h2_ready, 1)
            for b in range(2):
                act.activation(SINK[:, b:b + 1], ZERO, ACT.Copy).then_inc(copied["A"], 1)
                act.activation(SINK[:, 2 + b:3 + b], ZERO, ACT.Copy).then_inc(y_stored[b], 16)
            act.wait_ge(rounds_ready, 1)
            rounds = act.value_load(NRD[0:1, 0:1].bitcast(I32), min_val=1, max_val=T // SLOTS)
            ybuf = a["y_scratch"].rearrange("(e t) d -> t e d", t=SLOTS)

            def tokens(value, par, hf):
                act.wait_ge(gathered, value)
                act.activation(XE[:, par, 4 * hf:4 * hf + 4].rearrange("p k s -> p (k s)"), ps[:, hf, :], ACT.Copy).then_inc(xe_ready, 1)

            tokens(1, 0, 0)
            tokens(2, 0, 1)
            with act.Fori(0, rounds) as r:
                with act.Fori(0, 8) as i:
                    for j in range(4):
                        par = j % 2
                        step = r * 32 + i * 4 + j
                        act.wait_ge(gu_done, step * 2 + 4)
                        act.activation(SG[:, par, :], ps[:, 2 + par, 0:2 * SLOTS], ACT.Silu).then_inc(silu_m, 1)
                        tokens(step + 3, 1 - j // 2, j % 2)
                        act.wait_ge(down_made, step + 3)
                        act.wait_ge(y_stored[par], r * 256 + i * 32 + (j // 2 * 16 + 16))
                        act.activation(YO[0:SLOTS, par, 0:512], ps[0:SLOTS, 4 + 2 * par, :], ACT.Copy).then_inc(copied["A"], 1)
                        act.wait_ge(copied["A"], step + 3)
                        act.wait_ge(copied["D"], step + 3)
                        act.dma_start(ybuf[:, bass.ds(i * 4 + j, 1), :].rearrange("t e d -> t (e d)"),
                                      YO[0:SLOTS, par, :]).then_inc(y_stored[par], 16)
                act.wait_ge(mixed, r * 4 + 4)
            act.wait_ge(freed["D"], BEFORE["moe"]["D"] + 8)
            norm_squares(5, xT)
            norm_root(5)

        @block.gpsimd
        def _(pool):
            np_ = len(PRODUCTS)
            for q in range(4):
                for li, b in enumerate(LEVELS):
                    for s in range(2):
                        dst = tmp[s][6 if li % 2 == 0 else 8]
                        if li == 0 and s == 0:
                            pool.wait_ge(made, 2 * np_ * q + 2 * PNAMES.index("rkT") + 2)
                            pool.wait_ge(emptD, emptied(q, "rkT", 1, "D"))
                        if li >= 2:
                            pool.wait_ge(made, 2 * np_ * q + 2 * PNAMES.index(f"y{LEVELS[li - 2]}") + s + 1)
                        pool.tensor_tensor(chunks(dst), chunks(tmp[s][5]), rep(cst(f"level{b}"), NCH), ALU.mult).then_inc(maskp, 1)

            def weights_low(j, value):
                pool.wait_ge(w_high, value)
                slot_ = (FIRST["up"] + j) % R
                pool.tensor_tensor(W_LOW[:, slot_, :], ring[:, slot_, :], W_HIGH[:, j % 2, :].bitcast(F32), ALU.subtract).then_inc(w_low, 1)

            for j in range(2):
                weights_low(j, j + 1)
            with pool.Fori(0, 5) as i:
                for j in range(2, 2 + R):
                    weights_low(j, i * R + (j + 1))
            for d in range(12):
                slot_, size = (FIRST["down"] + d) % R, (2048, 2048, 1536)[d % 3]
                pool.wait_ge(w_high, 22 + d + 1)
                pool.tensor_tensor(W_LOW[:, slot_, 0:size], ring[:, slot_, 0:size], W_HIGH[:, d % 2, 0:size].bitcast(F32),
                                   ALU.subtract).then_inc(w_low, 1)
            pool.wait_ge(half_done, 2 * FIRST["ada2"])
            pool.wait_ge(freed["D"], BEFORE["ada2"]["D"])
            pool.dma_start(BROW[0:8, 255:640], a["rel_reversed"][:, 0:385]).then_inc(bias_row, 16)
            pool.dma_start(CH, a["consts"][:, CONST_AT["chunked"][0]:CONST_AT["chunked"][0] + T]).then_inc(got_pos, 16)
            pool.dma_start(ANG[:, 3, :].bitcast(I32), a["positions"].partition_broadcast(P)).then_inc(got_pos, 16)
            pool.wait_ge(bias_row, 16)
            pool.tensor_copy(BROW[0:8, 0:255], BROW[0:8, 255:256].broadcast_to([8, 255])).then_inc(pool_link, 1)
            pool.wait_ge(pool_link, 1)
            pool.dma_start(a["bias_scratch"], BROW[0:8, :].unsqueeze(1).broadcast_to([8, P, 640])).then_inc(bias_out, 16)
            pool.wait_ge(bias_out, 16)
            pool.dma_start(BT, bass.AP(a["bias_scratch"].tensor, 127, [[639, P], [P * 640, 8], [1, T]])).then_inc(got_bias, 16)
            pool.wait_ge(half_done, 2 * FIRST["w_out2"])
            pool.wait_ge(freed["D"], BEFORE["w_out2"]["D"])
            pool.dma_start(WR[:, :, 0:4], a["w_rg_2"].rearrange("(k p) c -> p k c", p=P)).then_inc(got_router, 16)
            pool.dma_start(WR[:, :, 4:36], a["w_re_2"].rearrange("(k p) c -> p k c", p=P)).then_inc(got_router, 16)
            pool.dma_start(MCON, a["consts"][:, CONST_AT["before"][0]:NCONST]).then_inc(got_router, 16)
            pool.dma_start(BRT, a["b_router"].partition_broadcast(P)).then_inc(got_router, 16)
            pool.wait_ge(rounds_ready, 1)
            rounds = pool.value_load(NRD[0:1, 0:1].bitcast(I32), min_val=1, max_val=T // SLOTS)
            with pool.Fori(0, rounds) as r:
                pool.wait_ge(indexed, r + 1)
                for b in range(2):
                    pool.wait_ge(y_stored[b], r * 256 + 272)
                pool.tensor_tensor(SINK[:, 10:11], ZERO, ZERO, ALU.add).then_inc(round_held, 1)
                for tt in range(4):
                    for w in range(2):
                        pool.indirect_dma_start(GY[:, 2 * tt + w, :], None, a["y_scratch"],
                                                bass.IndirectOffsetOnAxis(ap=IDX[:, 2 * tt + w:2 * tt + w + 1], axis=0)).then_inc(fetched[tt], 16)
                pool.wait_ge(round_held, r + 1)

        @block.vector
        def _(dve):
            lk = Link(dve, dve_link)
            tt, ts, stt = dve.tensor_tensor, dve.tensor_scalar, dve.scalar_tensor_tensor
            lk(dve.memset(EPSC, EPS))
            lk(dve.memset(GNC, GN_EPS))
            dve.memset(ZERO, 0.0).then_inc(dve_link, 1)
            lk.n += 1
            dve.wait_ge(dve_link, lk.n)
            dve.wait_ge(got_const, 32)
            lk.done(ts(OMU, col("mu", 0, 27), -1.0, 1.0, ALU.mult, ALU.add))
            ts(OKA, col("k_a", 0, 8), -1.0, 1.0, ALU.mult, ALU.add).then_inc(mod_ready, 1)

            def modulation(phase, bias):
                dve.wait_ge(mod_turned, 1 if phase == "ada1" else 2)
                lk.done(tt(mod[:], ps[:, 7, 0:48], bias, ALU.add))

            def gain(which, w):
                lk.done(ts(GAIN, mod[:, which * 24 + 8:which * 24 + 16], 1.0, None, ALU.add))
                lk.done(tt(GAIN, GAIN, w, ALU.mult))

            def norm_scale(k_norm, src, dst):
                dve.wait_ge(rooted, k_norm + 1)
                lk.done(dve.reciprocal(RSTD, RSTD))
                lk.done(tt(dst, src, rep(RSTD, KT), ALU.mult))

            def norm_apply(k_norm, src, g, shift, dst, scaled_=False):
                if not scaled_:
                    norm_scale(k_norm, src, dst)
                for k in range(KT):
                    if shift is None:
                        ins = ts(dst[:, k, :], dst[:, k, :], g[:, k:k + 1], None, ALU.mult)
                    else:
                        ins = ts(dst[:, k, :], dst[:, k, :], g[:, k:k + 1], shift[:, k:k + 1], ALU.mult, ALU.add)
                    if k == KT - 1:
                        ins.then_inc(normed, 1)

            dve.wait_ge(got_x, 16)
            norm_scale(0, x_in, hT)
            modulation("ada1", col("b_ada", 0, 48))
            gain(0, col("norm1_w", 0, 8))
            ts(ONE, ZERO, 1.0, None, ALU.add).then_inc(freed["D"], 1)
            norm_apply(0, x_in, GAIN, mod[:, 0:8], hT, scaled_=True)
            sc_n = 0

            def shift(dst, bank, mu, rows=P):
                nonlocal sc_n
                sc_n += 1
                dve.wait_ge(scaled, sc_n)
                stt(dst[0:rows, 1:T], ps[0:rows, bank, 0:T - 1], mu[0:rows], dst[0:rows, 1:T],
                    ALU.mult, ALU.add).then_inc(freed["D"], 1)

            for i, (dst, rows) in enumerate(((LOW, P), (GLO, P), (GLO2, 32))):
                shift(dst, i, col("mu", 24 + i), rows)

            np_ = len(PRODUCTS)

            def made_wait(q, name, s):
                dve.wait_ge(made, 2 * np_ * q + 2 * PNAMES.index(name) + s + 1)

            def bank_rows(s, e):
                return slice(e * 64, e * 64 + 64), 4 + 2 * s + e

            def empty_half(q, name, s, dst):
                made_wait(q, name, s)
                r, b = bank_rows(s, 1)
                dve.tensor_copy(dst[r], ps[r, b, :]).then_inc(emptD, 1)

            def empty_masked(q, name, s, dst, mask):
                made_wait(q, name, s)
                for e in range(2):
                    r, b = bank_rows(s, e)
                    ins = tt(chunks(dst[r]), chunks(ps[r, b, :]), rep(mask[r], NCH), ALU.mult)
                    if e == 0:
                        lk(ins)
                    else:
                        ins.then_inc(emptD, 1)

            def empty_added(q, name, s, dst, src):
                made_wait(q, name, s)
                for e in range(2):
                    r, b = bank_rows(s, e)
                    ins = tt(dst[r], ps[r, b, :], src[r], ALU.add)
                    if e == 0:
                        lk(ins)
                    else:
                        ins.then_inc(emptD, 1)

            for q in range(4):
                def add_previous(i):
                    part, hf = STREAMED[i // 2], i % 2
                    shift(tmp[hf][part], (q * 6 + i) % 4, col("mu", part * 8 + 2 * q + hf))

                def complete(i):
                    dve.wait_ge(freed["D"], BEFORE["rkv"]["D"] + 6 * q + i)

                for s in range(2):
                    t_ = tmp[s]
                    dve.wait_ge(emptA, emptied(q, "lora", s, "A"))
                    lk.done(dve.tensor_tensor_scan(t_[5], cst("restart"), t_[3], 0.0, ALU.mult, ALU.add))
                    tt(t_[6], t_[5], t_[3], ALU.subtract).then_inc(cum, 1)
                for s in range(2):
                    t_ = tmp[s]
                    add_previous(s)
                    complete(1 + s)
                    lk.done(ts(t_[9], t_[1], col("k_k", 2 * q + s), None, ALU.mult))
                    tt(t_[10], t_[9], t_[9], ALU.mult).then_inc(chan, 1)
                for s in range(2):
                    j = 2 * q + s
                    t_ = tmp[s]
                    add_previous(2 + s)
                    dve.wait_ge(emptA, emptied(q, "ssq", s, "A"))
                    lk.done(ts(t_[10], t_[10], 1e-12, None, ALU.max))
                    lk.done(dve.reciprocal(t_[10], t_[10]))
                    lk.done(tt(t_[9], t_[9], t_[10], ALU.mult))
                    lk.done(ts(t_[10], t_[4], col("k_a", j), OKA[:, j:j + 1], ALU.mult, ALU.add))
                    lk.done(tt(t_[1], t_[1], t_[10], ALU.mult))
                    complete(3 + s)
                    lk.done(stt(t_[10], t_[0], col("r_k", j), t_[1], ALU.mult, ALU.mult))
                    tt(t_[4], t_[4], t_[9], ALU.mult).then_inc(chan, 1)
                for s in range(2):
                    t_ = tmp[s]
                    add_previous(4 + s)
                    dve.wait_ge(chan, 6 * q + 3 + s)
                    dve.wait_ge(decay, 6 * q + 3 * s + 3)
                    lk.done(stt(t_[6], t_[9], -1.0, t_[6], ALU.mult, ALU.mult))
                    lk.done(tt(t_[4], t_[4], t_[8], ALU.mult))
                    lk.done(tt(t_[8], t_[1], t_[8], ALU.mult))
                    lk.done(tt(t_[0], t_[0], t_[7], ALU.mult))
                    lk.done(dve.tensor_copy(PLS[s], chunks(t_[7])[:, :, C - 1]))
                    lk.done(tt(chunks(t_[5]), chunks(t_[4]), bc(PLS[s], C), ALU.mult))
                    tt(chunks(t_[3]), chunks(t_[8]), bc(PLS[s], C), ALU.mult).then_inc(chan, 1)
                complete(6)
                for s in range(2):
                    made_wait(q, "bonus", s)
                    tt(BON[:, 2 * q + s, :], ps[:, 4 + 2 * s, :], tmp[s][2], ALU.mult).then_inc(emptD, 1)
                for name, d in (("tv", 1), ("tat", 7), ("tbh", 9), ("tkh", 10)):
                    for s in range(2):
                        empty_half(q, name, s, tmp[s][d])
                for name, d, mask in (("ab", 2, "pair1"), ("abT", 11, "upper"), ("akT", 11, "upper"),
                                      ("rbT", 12, "upto"), ("rkT", 13, "upto")):
                    for s in range(2):
                        t_ = tmp[s]
                        if name == "ab":
                            made_wait(q, name, s)
                            for e in range(2):
                                r, b = bank_rows(s, e)
                                lk.done(tt(chunks(t_[2][r]), chunks(ps[r, b, :]), rep(cst("pair1")[r], NCH), ALU.mult))
                            tt(chunks(t_[2]), chunks(t_[2]), rep(eye64, NCH), ALU.add).then_inc(emptD, 1)
                        elif name == "abT":
                            made_wait(q, name, s)
                            for e in range(2):
                                r, b = bank_rows(s, e)
                                lk.done(tt(chunks(t_[5][r]), chunks(ps[r, b, :]), rep(cst("upper")[r], NCH), ALU.mult))
                            lk.done(tt(chunks(t_[3]), chunks(t_[5]), rep(cst("pair1T"), NCH), ALU.mult))
                            tt(chunks(t_[3]), chunks(t_[3]), rep(eye64, NCH), ALU.add).then_inc(emptD, 1)
                        else:
                            empty_masked(q, name, s, t_[d], cst(mask))
                for b in LEVELS:
                    for s in range(2):
                        empty_half(q, f"y{b}", s, tmp[s][4])
                    if b != LEVELS[-1]:
                        for s in range(2):
                            empty_added(q, f"x{b}", s, tmp[s][2], tmp[s][2])
                    for s in range(2):
                        empty_added(q, f"xT{b}", s, tmp[s][3], tmp[s][3])
                for name, d in (("w1", 4), ("sav", 2), ("z", 5)):
                    for s in range(2):
                        empty_half(q, name, s, tmp[s][d])
                for s in range(2):
                    empty_added(q, "r", s, RT[:, 2 * q + s, :], tmp[s][0])
                for s in range(2):
                    empty_half(q, "y0", s, Y0[:, 2 * q + s, :])
                for s in range(2):
                    j = 2 * q + s
                    lk.done(tt(GT[:, j], rep(eye64, NCH), bc(PLS[s], C), ALU.mult))
                    gt = GT[:, j].rearrange("p c k -> p (c k)")
                    empty_added(q, "g", s, gt, gt)
                for s in range(2):
                    made_wait(q, "h", s)
                    r, b = bank_rows(s, 1)
                    dve.tensor_copy(ST[r, :, 2 * q + s, :], chunks(ps[r, b, :])).then_inc(emptD, 1)

            dve.wait_ge(emptA, 4 * PER_QUAD["A"])
            dve.wait_ge(emptD, 4 * PER_QUAD["D"])
            for c in range(1, NCH - 1):
                dve.wait_ge(stepped, c)
                for e in range(2):
                    r = slice(e * 64, e * 64 + 64)
                    v = ST[r, c].rearrange("p j k -> p (j k)")
                    ins = tt(v, ps[r, 4 + 2 * (c % 2) + e, :], v, ALU.add)
                    if e == 0:
                        lk(ins)
                    else:
                        ins.then_inc(state_ready, 1)

            def y_add(j):
                dve.wait_ge(y_made, j + 1)
                for e in range(2):
                    r = slice(e * 64, e * 64 + 64)
                    ins = tt(Y0[r, j, C:T], ps[r, 4 + 2 * (j % 2) + e, C:T], Y0[r, j, C:T], ALU.add)
                    if e == 0:
                        lk.done(ins)
                    else:
                        ins.then_inc(y_added, 1)

            def y_centre(j):
                dve.wait_ge(mean_made, j + 1)
                stt(Y0[:, j, :], ps[:, j % 2, :], -1.0 / 64, Y0[:, j, :], ALU.mult, ALU.add).then_inc(centred, 1)

            def y_finish(j):
                dve.wait_ge(y_root, j + 1)
                rs = ytmp[j % 2][1]
                lk.done(dve.reciprocal(rs, rs))
                y = Y0[:, j, :]
                lk.done(tt(y, y, rs, ALU.mult))
                lk.done(ts(y, y, col("lnx_w", j), col("lnx_b", j), ALU.mult, ALU.add))
                lk.done(tt(y, y, BON[:, j, :], ALU.add))
                dve.wait_ge(g_made, j + 1)
                tt(y, ps[:, 4 + 2 * (j % 2), :], y, ALU.mult).then_inc(y_final, 1)

            for t in range(10):
                if 0 <= t - 2 < 8:
                    y_finish(t - 2)
                if t < 8:
                    y_add(t)
                if 0 <= t - 1 < 8:
                    y_centre(t - 1)

            def gated(phase, first, gate, merged):
                for i in range(8):
                    g, hf = divmod(i, 2)
                    dve.wait_ge(half_done, 2 * FIRST[phase] + 4 * g + 2 + hf + 1)
                    dve.wait_ge(freed["A"], BEFORE[phase]["A"] + i + 1)
                    if first:
                        tt(merged[:, i, :], ps[:, 2 + i % 2, :], gate[:, i % 2, :], ALU.mult).then_inc(freed["D"], 1)
                    else:
                        lk.done(tt(gate[:, i % 2, :], ps[:, 2 + i % 2, :], gate[:, i % 2, :], ALU.mult))
                        tt(merged[:, i, :], merged[:, i, :], gate[:, i % 2, :], ALU.add).then_inc(freed["D"], 1)

            gated("rw_out", True, gate, merged)
            dve.wait_ge(freed["A"], BEFORE["qk"]["A"])
            for i in range(12):
                dve.wait_ge(half_done, 2 * FIRST["qk"] + 2 * i + 2)
                dve.tensor_copy(QK[:, 2 * i + 1, :], ps[:, (2 * i + 1) % 4, :]).then_inc(freed["D"], 1)
            for i in range(6):
                dve.wait_ge(half_done, 2 * FIRST["v"] + 2 * i + 2)
                dve.tensor_copy(VT[:, 2:4, i * 256:i * 256 + 256],
                                ps[:, (2 * i + 1) % 4, :].rearrange("p (a b) -> p a b", b=256)).then_inc(freed["D"], 1)

            def attend(u0, us, parts_of, prob, otok):
                def peaks(i):
                    u = u0 + i
                    pt = parts_of(us[i], i)
                    dve.wait_ge(scored, u + 1)
                    if u >= 2:
                        dve.wait_ge(turned, TURNED[u - 2])
                    o = 0
                    for g, (_, _, bk, n_) in enumerate(pt["scores"]):
                        ins = dve.tensor_tensor_reduce(out=prob[u % 2][:, o:o + n_], in0=ps[:, bk, 0:n_], in1=pt["masks"][g],
                                                       scale=1.0, scalar=NEG, op0=ALU.add, op1=ALU.max,
                                                       accum_out=PK[:, u % 2, g:g + 1])
                        o += n_
                        if g == len(pt["scores"]) - 1:
                            ins.then_inc(masked, 1)
                        else:
                            lk(ins)
                    dve.wait_ge(masked, u + 1)
                    if len(pt["scores"]) > 1:
                        dve.wait_ge(dve_link, lk.n)
                    lk.done(dve.tensor_reduce(PK[:, u % 2, 3:4], PK[:, u % 2, 0:len(pt["scores"])], AX.X, ALU.max))
                    ts(NM[:, u % 2:u % 2 + 1], PK[:, u % 2, 3:4], -pt["scale"], None, ALU.mult).then_inc(peaked, 1)

                def denominators(i):
                    u = u0 + i
                    dve.wait_ge(probbed, u + 1)
                    lk.done(dve.reciprocal(RD[:, u % 2:u % 2 + 1], DEN[:, u % 2:u % 2 + 1]))

                def outs(i):
                    u = u0 + i
                    w = u // 8
                    pt = parts_of(us[i], i)
                    dve.wait_ge(weighed, u + 1)
                    if i % 8 == 0 and w >= 2:
                        dve.wait_ge(oturned, w - 1)
                    ts(otok[w % 2][:, pt["out"]], ps[:, 6 + u % 2, 0:64], RD[:, u % 2:u % 2 + 1], None, ALU.mult).then_inc(outed, 1)

                peaks(0)
                for i in range(len(us)):
                    if i + 1 < len(us):
                        peaks(i + 1)
                    if i >= 1:
                        outs(i - 1)
                    denominators(i)
                outs(len(us) - 1)

            dve.wait_ge(got_masks, 16)
            attend(0, units, parts1, PROB1[0], PROB1[2])
            gated("at_out", False, gate, merged)

            dve.wait_ge(got_x1, 16)

            def residual(phase, gcol):
                for i in range(8):
                    if phase == "down":
                        dve.wait_ge(half_done, 2 * FIRST[phase] + 6 * (i // 2) + 4 + i % 2 + 1)
                    else:
                        dve.wait_ge(half_done, 2 * FIRST[phase] + i + 1)
                    stt(xT[:, i, :], ps[:, i % 4, :], mod[:, gcol + i:gcol + i + 1], xT[:, i, :],
                        ALU.mult, ALU.add).then_inc(freed["D"], 1)

            residual("w_o", 16)
            gain(1, col("norm2_w", 0, 8))
            norm_scale(1, xT, hT)
            for k in range(KT):
                ts(hT[:, k, :], hT[:, k, :], GAIN[:, k:k + 1], mod[:, 24 + k:25 + k], ALU.mult, ALU.add).then_inc(h_piece, 1)
            for k in range(KT):
                dve.wait_ge(h_high, k + 1)
                ins = tt(H_LOW[:, k, :], hT[:, k, :], H_HIGH[:, k, :].bitcast(F32), ALU.subtract)
            ins.then_inc(normed, 1)

            D0, H0 = BEFORE["up"]["D"], 2 * FIRST["up"]

            def up_slot(jj, cb, lbase):
                for g in range(2):
                    dst, bank = cvt[jj % 2][g], (2 * jj + g) % 4
                    dve.wait_ge(convd, 2 * cb(jj) + (g + 1) if isinstance(cb(jj), int) else cb(jj) * 2 + (g + 1))
                    stt(dst[:, 1:T], ps[:, bank, 0:T - 1], up_col(1, g, jj, cb), dst[:, 1:T], ALU.mult, ALU.add).then_inc(dve_link, 1)
                    dve.wait_ge(dve_link, lbase(g + 1))
                    stt(dst[:, 2:T], ps[:, bank, 0:T - 2], up_col(0, g, jj, cb), dst[:, 2:T], ALU.mult, ALU.add).then_inc(freed["D"], 1)
                dve.wait_ge(silud, cb(jj) + 1)
                dve.wait_ge(freed["D"], (cb(jj) * 2) + (D0 + 2))
                i = cb(jj)
                val = RSTD
                if jj:
                    dve.wait_ge(hidd, cb(jj))
                high, low = ((HID_HIGH[:, i, :], HID_LOW[0][:, i, :]) if isinstance(i, int) else
                             [v.rearrange("p a t -> p (a t)") for v in (HID_HIGH[:, bass.ds(i, 1), :], HID_LOW[1][:, bass.ds(i - 2, 1), :])])
                tt(val, sil[:, jj % 2, :], cvt[jj % 2][1], ALU.mult).then_inc(dve_link, 1)
                dve.wait_ge(dve_link, lbase(3))
                dve.tensor_copy(high, val).then_inc(dve_link, 1)
                dve.wait_ge(dve_link, lbase(4))
                tt(low, val, high.bitcast(F32), ALU.subtract).then_inc(hidd, 1)

            def up_col(tap, g, jj, cb):
                base = COL_AT["conv_w"] + tap * 44 + g * FT
                i = cb(jj)
                return cols[:, base + i:base + i + 1] if isinstance(i, int) else cols[:, bass.ds(i + base, 1)]

            l0 = lk.n
            for jj in range(2):
                up_slot(jj, lambda v: v, lambda v: l0 + 4 * jj + v)
            with dve.Fori(0, 5) as i:
                for jj in range(2, 2 + R):
                    up_slot(jj, lambda v: i * 4 + v, lambda v: i * 16 + (l0 + 4 * jj + v))
            lk.n = l0 + 88
            residual("down", 40)
            norm_apply(2, xT, col("norm_f_w", 0, 8), None, xT)

            norm_scale(3, xT, hT)
            modulation("ada2", col("b_ada_2", 0, 48))
            gain(0, col("g_mix_2", 0, 8))
            ts(ONE, ZERO, 1.0, None, ALU.add).then_inc(freed["D"], 1)
            norm_apply(3, xT, GAIN, mod[:, 0:8], hT, scaled_=True)
            dve.wait_ge(got_pos, 32)
            ROUND = 12582912.0
            C1 = 6.28125
            C2 = float(np.float32(int((2 * np.pi - C1) * 2 ** 22) / 2 ** 22))
            C3 = float(2 * np.pi - C1 - C2)
            PI_ = float(np.nextafter(np.float32(np.pi), np.float32(0)))
            lk.done(dve.tensor_copy(ANG[:, 2, :], ANG[:, 3, :].bitcast(I32)))
            lk.done(ts(ANG[:, 2, :], ANG[:, 2, :], cst("freq"), None, ALU.mult))
            for i_, quarter in enumerate((0.0, 0.25)):
                o_, tr = ANG[:, i_, :], ANG[:, 3, :]
                lk.done(ts(tr, ANG[:, 2, :], 1.0 / (2 * np.pi), quarter, ALU.mult, ALU.add))
                lk.done(ts(tr, tr, ROUND, -ROUND, ALU.add, ALU.add))
                lk.done(stt(o_, tr, -C1, ANG[:, 2, :], ALU.mult, ALU.add))
                lk.done(stt(o_, tr, -C2, o_, ALU.mult, ALU.add))
                lk.done(stt(o_, tr, -C3, o_, ALU.mult, ALU.add))
                lk.done(ts(o_, o_, quarter * 2 * np.pi, PI_, ALU.add, ALU.min))
                ins = ts(o_, o_, -PI_, None, ALU.max)
                if i_ == 0:
                    lk.done(ins)
                else:
                    ins.then_inc(angled, 1)
            dve.wait_ge(rotated, 1)
            lk.done(ts(SIN, ANG[:, 0, :], cst("rotsign"), None, ALU.mult))
            lk.done(dve.tensor_copy(COS, ANG[:, 1, :]))
            dve.wait_ge(got_bias, 16)
            for h in range(8):
                lk.done(stt(BT[:, h, :], BT[:, h, :], 8.0, CH, ALU.mult, ALU.add))

            in2_value = lambda o: o + 1 if o < 4 else o + 2
            tok2 = lambda v: v.rearrange("p (a b) -> p a b", b=256)

            def psum_out(phase, dst, src, v):
                dve.wait_ge(half_done, 2 * FIRST[phase] + v)
                dve.tensor_copy(dst, src).then_inc(freed["D"], 1)

            IN2 = [QL[:, 0, :], QL[:, 1, :], KV, KR, KRS] + [QB[:, j, :] for j in range(4)] + [KB[:, j, :] for j in range(4)]
            for o in range(1, 13, 2):
                psum_out("in2", IN2[o], ps[:, o % 4, :], in2_value(o))
            for o in (13, 15):
                c, hf = divmod(o - 13, 2)
                psum_out("in2", VB[:, 2 * hf:2 * hf + 2, c * 256:c * 256 + 256], tok2(ps[:, o % 4, :]), in2_value(o))
            dve.wait_ge(lat_root, 2)
            lk.done(dve.reciprocal(LRT, LRT))
            lk.done(stt(QL[:, 0, :], QL[:, 0, :], col("g_q_2", 0), LRT[:, 0, :], ALU.mult, ALU.mult))
            lk.done(stt(QL[:, 1, :], QL[:, 1, :], col("g_q_2", 1), LRT[:, 0, :], ALU.mult, ALU.mult))
            stt(KV, KV, col("g_kv_2"), LRT[:, 1, :], ALU.mult, ALU.mult).then_inc(lat_ready, 1)
            r = slice(64, 96)
            dve.wait_ge(freed["A"], BEFORE["in2"]["A"] + 3)
            dve.wait_ge(freed["D"], BEFORE["in2"]["D"] + 2)
            lk.done(tt(KR[r], KR[r], COS[r], ALU.mult))
            lk.done(tt(KRS[r], KRS[r], SIN[r], ALU.mult))
            lk.done(tt(KR[r], KR[r], KRS[r], ALU.add))
            lk.done(dve.tensor_copy(KA[r], rep(KR[r], 8)))
            for h in range(8):
                dve.wait_ge(half_done, 2 * FIRST["lat2"] + 2 * h + 2)
                tt(ROT[r, h % 2, :], ps[r, (2 * h + 1) % 4, :], SIN[r], ALU.mult).then_inc(freed["D"], 1)
                dve.wait_ge(freed["A"], BEFORE["lat2"]["A"] + h + 1)
                dve.wait_ge(freed["D"], BEFORE["lat2"]["D"] + h + 1)
                lk.done(tt(QA[r, h, :], QA[r, h, :], COS[r], ALU.mult))
                lk.done(tt(QA[r, h, :], QA[r, h, :], ROT[r, h % 2, :], ALU.add))
            for o in range(17, 24, 2):
                psum_out("lat2", KA[0:64, o - 16, :], ps[0:64, o % 4, :], o + 1)
            for o in (25, 27):
                c, hf = divmod(o - 24, 2)
                psum_out("lat2", VA[:, 2 * hf:2 * hf + 2, c * 256:c * 256 + 256], tok2(ps[:, o % 4, :]), o + 1)
            ts(ONE, ZERO, 1.0, None, ALU.add).then_inc(band_ready, 1)
            attend(32, units, parts_mla, PROB2[0], PROB2[2])
            attend(64, units, parts_band, PROB2[0], PROB2[2])
            gated("mla_out", True, gate2, merged2)
            gated("band_out", False, gate2, merged2)
            residual("w_out2", 16)
            gain(1, col("g_ffn_2", 0, 8))
            norm_apply(4, xT, GAIN, mod[:, 24:32], hT)
            dve.wait_ge(routed, 1)
            t4 = lambda v, k: v[:, 0:4 * k].rearrange("p (t k) -> p t k", k=k)
            lk.done(tt(RL, ps[:, 7, 0:144].rearrange("p (t c) -> p t c", c=36), rep(BRT, 4), ALU.add))
            LG, LE = RL[:, :, 0:4], RL[:, :, 4:36]
            red = lambda o_, i_, op: lk.done(dve.tensor_reduce(o_, i_, AX.X, op))
            rank = lambda k: cst("rank")[:, 0:k].unsqueeze(1).broadcast_to([P, 4, k])
            GM, M1, M2, MX, GS = [rt_[0][:, 4 * i:4 * i + 4] for i in range(5)]

            def first_max(dst, scratch, x, mx, k):
                lk.done(tt(scratch, x, bc(mx, k), ALU.is_equal))
                lk.done(tt(scratch, scratch, rank(k), ALU.mult))
                red(MX, scratch, ALU.max)
                lk.done(tt(dst, scratch, bc(MX, k), ALU.is_equal))

            red(GM, LG, ALU.max)
            OG, SCR4, SCR8, O1, O2, E2 = t4(rt_[1], 4), t4(rt_[2], 4), t4(rt_[3], 8), t4(rt_[4], 8), t4(rt_[5], 8), t4(rt_[6], 8)
            first_max(OG, SCR4, LG, GM, 4)
            ES = t4(rt_[7], 8)
            WIDE = rt_[8][:, 0:128].rearrange("p (t g e) -> p t g e", g=4, e=8)
            for tt_ in range(4):
                lk.done(tt(WIDE[:, tt_], LE[:, tt_].rearrange("p (g e) -> p g e", e=8), bc(OG[:, tt_], 8), ALU.mult))
            for tt_ in range(4):
                red(ES[:, tt_], WIDE[:, tt_].rearrange("p g e -> p e g"), ALU.add)
            red(M1, ES, ALU.max)
            first_max(O1, SCR8, ES, M1, 8)
            lk.done(stt(E2, O1, NEG, ES, ALU.mult, ALU.add))
            red(M2, E2, ALU.max)
            first_max(O2, SCR8, E2, M2, 8)
            ex = rt_e.rearrange("p (t k) -> p t k", k=5)
            lk.done(tt(ex[:, :, 0:4], LG, bc(GM, 4), ALU.subtract))
            tt(ex[:, :, 4], M2, M1, ALU.subtract).then_inc(route_exp, 1)
            dve.wait_ge(route_exp, 2)
            red(GS, ex[:, :, 0:4], ALU.add)
            W1, W2 = rt_[9][:, 0:4], rt_[9][:, 4:8]
            lk.done(ts(W1, ex[:, :, 4], 1.0, None, ALU.add))
            lk.done(tt(W1, W1, GS, ALU.mult))
            lk.done(dve.reciprocal(W1, W1))
            lk.done(tt(W2, W1, ex[:, :, 4], ALU.mult))
            for tt_ in range(4):
                lk.done(dve.tensor_copy(WGT[:, 2 * tt_:2 * tt_ + 1], W1[:, tt_:tt_ + 1]))
                lk.done(dve.tensor_copy(WGT[:, 2 * tt_ + 1:2 * tt_ + 2], W2[:, tt_:tt_ + 1]))
            for F_, O_ in ((F1, O1), (F2, O2)):
                for tt_ in range(4):
                    lk.done(tt(F_[:, tt_].rearrange("p (g e) -> p g e", e=8), bc(OG[:, tt_], 8), rep(O_[:, tt_], 4), ALU.mult))
            tt(SEL, F1, F2, ALU.add).then_inc(selected, 1)
            dve.wait_ge(ranked, 1)
            dve.wait_ge(counted, 1)
            lk.done(dve.tensor_copy(RK, ps[:, 6, 0:128].rearrange("p (t e) -> p t e", e=32)))
            lk.done(dve.tensor_reduce(NRD[:, 1:2], ps[:, 3, 0:32], AX.X, ALU.max))
            lk.done(ts(NRD[:, 1:2], NRD[:, 1:2], 1.0 / SLOTS, (SLOTS - 1.0) / SLOTS - 0.5 + 0.5 / SLOTS, ALU.mult, ALU.add))
            lk.done(ts(NRD[:, 1:2], NRD[:, 1:2], ROUND, -ROUND, ALU.add, ALU.add))
            dve.tensor_copy(NRD[:, 0:1].bitcast(I32), NRD[:, 1:2]).then_inc(rounds_ready, 1)
            far = 4096.0
            lk.done(stt(RM[:, :, 0:32], SEL, -far, RK, ALU.mult, ALU.add))
            lk.done(ts(RM[:, :, 0:32], RM[:, :, 0:32], far, None, ALU.add))
            lk.done(ts(RM[:, :, 32:34], RM[:, :, 0:2], -float(SLOTS), None, ALU.add))
            for b in range(2):
                ts(SINK[:, 4 + b:5 + b], ZERO, 1.0, None, ALU.add).then_inc(copied["D"], 1)
                ts(SINK[:, 6 + b:7 + b], ZERO, 1.0, None, ALU.add).then_inc(down_made, 1)
                ts(SINK[:, 8 + b:9 + b], ZERO, 1.0, None, ALU.add).then_inc(gu_done, 1)

            def place(col_, par, second):
                rank_ = RM[:, :, col_:col_ + 1] if isinstance(col_, int) else RM[:, :, bass.ds(col_, 1)]
                tt(PICKED[:, par, :, second * SLOTS:(second + 1) * SLOTS], SLOT_NO.unsqueeze(1).broadcast_to([P, 4, SLOTS]),
                   rank_.broadcast_to([P, 4, SLOTS]), ALU.is_equal).then_inc(placed, 1)

            place(0, 0, 0)
            place(1, 0, 1)
            two = lambda ap: ap.rearrange("p (t w) -> p t w", w=2)
            for w, F_ in enumerate((F1, F2)):
                lk.done(tt(SEL, F_, RK, ALU.mult))
                red(two(RANK2)[:, :, w], SEL, ALU.add)
                lk.done(tt(F_, F_, rep(ROWS, 4), ALU.mult))
                red(two(ROW0)[:, :, w], F_, ALU.add)
            lk.done(dve.memset(GX, 0.0))
            dve.wait_ge(rounds_ready, 1)
            rounds = dve.value_load(NRD[0:1, 0:1].bitcast(I32), min_val=1, max_val=T // SLOTS)

            def mix_second(r, tt_):
                dve.wait_ge(half_mixed, r * 4 + (tt_ + 1))
                stt(GX[:, tt_, :], GY[:, 2 * tt_ + 1, :], WGT_IN[:, 2 * tt_ + 1:2 * tt_ + 2], GX[:, tt_, :],
                    ALU.mult, ALU.add).then_inc(mixed, 1)

            with dve.Fori(0, rounds) as r:
                ts(RANK_IN, RANK2, 0.0, SLOTS - 1.0, ALU.max, ALU.min).then_inc(round_link, 1)
                dve.wait_ge(round_link, r * 5 + 1)
                tt(IDX, RANK_IN, ROW0, ALU.add).then_inc(indexed, 1)
                tt(WGT_IN, RANK_IN, RANK2, ALU.is_equal).then_inc(round_link, 1)
                dve.wait_ge(round_link, r * 5 + 2)
                tt(WGT_IN, WGT_IN, WGT, ALU.mult).then_inc(round_link, 1)
                ts(RANK2, RANK2, -float(SLOTS), None, ALU.add).then_inc(round_link, 1)
                with dve.Fori(0, 8) as i:
                    for j in range(4):
                        par = j % 2
                        step = r * 32 + i * 4 + j
                        if j % 2 == 0:
                            dve.wait_ge(gu_done, step * 2 + 2)
                            for second in range(2):
                                place(i * 4 + (j + 2 + second), 1 - j // 2, second)
                        dve.wait_ge(gu_done, step * 2 + 4)
                        dve.wait_ge(silu_m, step + 1)
                        tt(MH[:, par].rearrange("p f s -> p (f s)"), ps[:, 2 + par, 2 * SLOTS:4 * SLOTS], SG[:, par, :],
                           ALU.mult).then_inc(mhid, 1)
                        dve.wait_ge(down_made, step + 3)
                        dve.wait_ge(y_stored[par], r * 256 + i * 32 + (j // 2 * 16 + 16))
                        dve.tensor_copy(YO[0:SLOTS, par, 512:D], ps[0:SLOTS, 5 + 2 * par, :]).then_inc(copied["D"], 1)
                dve.wait_ge(placed, r * 32 + 34)
                ts(RM, RM, -float(SLOTS), None, ALU.add).then_inc(round_link, 1)
                dve.wait_ge(round_link, r * 5 + 5)
                for tt_ in range(4):
                    dve.wait_ge(fetched[tt_], r * 32 + 32)
                    stt(GX[:, tt_, :], GY[:, 2 * tt_, :], WGT_IN[:, 2 * tt_:2 * tt_ + 1], GX[:, tt_, :],
                        ALU.mult, ALU.add).then_inc(half_mixed, 1)
                    if tt_ >= 1:
                        mix_second(r, tt_ - 1)
                mix_second(r, 3)
            for k in range(KT):
                dve.wait_ge(mix_turned, k + 1)
                stt(xT[:, k, :], ps[:, 2 + k % 2, :], mod[:, 40 + k:41 + k], xT[:, k, :], ALU.mult, ALU.add).then_inc(freed["D"], 1)
            dve.wait_ge(rooted, 6)
            dve.wait_ge(rooted, 6)
            dve.reciprocal(RSTD, RSTD).then_inc(tail_link, 1)
            dve.wait_ge(tail_link, 1)
            tt(hT, xT, rep(RSTD, KT), ALU.mult).then_inc(tail_link, 1)
            dve.wait_ge(tail_link, 2)
            for k in range(KT):
                ts(hT[:, k, :], hT[:, k, :], col("g_final_2", k), None, ALU.mult).then_inc(out_scaled, 1)


def kernel(**inputs):
    import numpy as _np
    import concourse.bacc as _bacc
    from concourse import mybir as _mybir
    from concourse.bass_utils import run_bass_kernel_spmd as _run

    arrays = layout({k: _np.asarray(v) for k, v in inputs.items()})
    nc = _bacc.Bacc("TRN2", target_bir_lowering=False, num_devices=1)
    aps = {}
    for name, v in arrays.items():
        aps[name] = nc.dram_tensor(f"in_{name}", v.shape, _mybir.dt.from_np(v.dtype), kind="ExternalInput").ap()
    aps["out"] = nc.dram_tensor("out_0", (D, T), F32, kind="ExternalOutput").ap()
    aps["y_scratch"] = nc.dram_tensor("y_scratch", (32 * SLOTS, D), F32, kind="Internal").ap()
    aps["bias_scratch"] = nc.dram_tensor("bias_scratch", (8, P, 640), F32, kind="Internal").ap()
    build(nc, aps)
    r = _run(nc, [{f"in_{k}": v for k, v in arrays.items()}], core_ids=[0])
    return _np.ascontiguousarray(r.results[0]["out_0"].T)[None]


def layout(x):
    def columns(v):
        v = v.reshape(-1)
        pad = -v.size % P
        return np.concatenate([v, np.zeros(pad, v.dtype)]).reshape(-1, P).T if pad else v.reshape(-1, P).T

    parts = []
    for name, n in COLS:
        key = "mu_shift" if name == "mu" else name
        parts.append(columns(x[key]))
        assert parts[-1].shape[1] == n, name
    arrays = {"cols": np.ascontiguousarray(np.concatenate(parts, axis=1)), "consts": CONSTS,
              "x": np.ascontiguousarray(x["x"][0].T),
              "positions": np.ascontiguousarray(x["positions_2"]),
              "rel_reversed": np.ascontiguousarray(x["rel_bias_2"][0][:, ::-1])}
    swap = np.r_[0:64, 80:96, 64:80]
    uq = x["w_uq_2"][0].reshape(256, 8, 96)
    arrays["w_uq"] = np.zeros((256, 8, 2, P), uq.dtype)
    arrays["w_uq"][:, :, 0, :96] = uq
    arrays["w_uq"][:, :, 1, :96] = uq[:, :, swap]
    arrays["w_uq"] = arrays["w_uq"].reshape(256, 2048)
    kvr = np.zeros((D, 3, P), uq.dtype)
    kvr[:, 0] = x["w_in_2"][0][:, 256:384]
    kvr[:, 1, 64:96] = x["w_in_2"][0][:, 384:416]
    kvr[:, 2, 64:96] = x["w_in_2"][0][:, np.r_[400:416, 384:400]]
    arrays["w_kvr"] = kvr.reshape(D, 384)
    for name in ("w_ada", "w_in", "w2", "a2", "g2", "w_att_out", "w_rwkv_out", "w_o", "w_up", "w_down", "w_ada_2",
                 "w_in_2", "w_uk_2", "w_uv_2", "w_oa_2", "w_ob_2", "w_out_2", "w_rg_2", "w_re_2", "w_gate_2",
                 "w_up_2", "w_down_2"):
        arrays[name] = np.ascontiguousarray(x[name][0])
    arrays["b_router"] = np.ascontiguousarray(np.concatenate([x["b_rg_2"], x["b_re_2"]], axis=1))
    return arrays
```
